# Optimizing a Trainium2 kernel written in Bass

```python
import jax, jax.numpy as jnp
from jax import lax
import numpy as np

D_MODEL = 1024
BATCH = 1
SEQ = 512
DEPTH = 2

CHUNK = 64
D_PLE = 256
N_GROUPS = 4
GROUP_W = D_MODEL // N_GROUPS
HEAD_DIM = 64
N_HEADS_GROUP = GROUP_W // HEAD_DIM
D_FF = 2816
NORM_EPS = 1e-6
CONV_W = 4
LRU_C = 8.0
FOX_BLOCK = 128
RW_DECAY_RANK = 64
RW_A_RANK = 64
RW_GATE_RANK = 128
RW_IN_W = 3 * GROUP_W + RW_DECAY_RANK + RW_A_RANK + RW_GATE_RANK
RW_OFFSETS = (GROUP_W, 2 * GROUP_W, 3 * GROUP_W, 3 * GROUP_W + RW_DECAY_RANK,
              3 * GROUP_W + RW_DECAY_RANK + RW_A_RANK)
RW_GN_EPS = 64e-5
SW_WINDOW = 128
SW_WINDOW_CHUNKS = SW_WINDOW // CHUNK
SW_KV_HEADS = 2
KV_W = SW_KV_HEADS * HEAD_DIM

IN_WIDTHS = (GROUP_W, GROUP_W,
             GROUP_W, GROUP_W, GROUP_W, N_HEADS_GROUP,
             GROUP_W, GROUP_W, GROUP_W,
             RW_DECAY_RANK, RW_A_RANK, RW_GATE_RANK,
             GROUP_W, KV_W, KV_W)
D_IN = sum(IN_WIDTHS)
IN_OFFSETS = tuple(int(o) for o in np.cumsum(IN_WIDTHS)[:-1])

kernel_name = 'hybrid_chunk_causal_encoder'

def rmsnorm(x, g):
    xf = x.astype(jnp.float32)
    y = xf * lax.rsqrt(jnp.mean(xf * xf, axis=-1, keepdims=True) + NORM_EPS)
    return (y * g.astype(jnp.float32)).astype(x.dtype)

def swiglu(x, wg, wu, wd):
    return (jax.nn.silu(x @ wg) * (x @ wu)) @ wd

def causal_depthwise_conv(x, w, b):
    C = x.shape[-1]
    K = w.shape[0]
    y = lax.conv_general_dilated(x, w[:, None, :].astype(x.dtype), window_strides=(1,),
                                 padding=((K - 1, 0),), dimension_numbers=('NWC', 'WIO', 'NWC'),
                                 feature_group_count=C)
    return y + b

def rg_lru(x, w_a, b_a, w_x, b_x, lam):
    B, S, C = x.shape
    xh = x.reshape(B, S, N_HEADS_GROUP, HEAD_DIM)
    gate_r = jax.nn.sigmoid((jnp.einsum('bshd,hde->bshe', xh, w_a).reshape(B, S, C) + b_a).astype(jnp.float32))
    gate_i = jax.nn.sigmoid((jnp.einsum('bshd,hde->bshe', xh, w_x).reshape(B, S, C) + b_x).astype(jnp.float32))
    log_a = -LRU_C * gate_r * jax.nn.softplus(-lam.astype(jnp.float32))
    a = jnp.exp(log_a)
    u = jnp.sqrt(-jnp.expm1(2.0 * log_a)) * gate_i * x.astype(jnp.float32)

    def combine(left, right):
        a_l, h_l = left
        a_r, h_r = right
        return a_l * a_r, a_r * h_l + h_r

    _, h = lax.associative_scan(combine, (a, u), axis=1)
    return h.astype(x.dtype)

def forgetting_attention(q, k, v, log_f):
    B, S, H, Dh = q.shape
    nb = S // FOX_BLOCK
    c = jnp.cumsum(log_f, axis=1).transpose(0, 2, 1)
    q_blocks = q.reshape(B, nb, FOX_BLOCK, H, Dh).transpose(1, 0, 2, 3, 4)
    c_blocks = c.reshape(B, H, nb, FOX_BLOCK).transpose(2, 0, 1, 3)
    k_pos = jnp.arange(S)

    def block(args):
        q_i, c_i, idx = args
        s = jnp.einsum('bqhd,bkhd->bhqk', q_i, k).astype(jnp.float32) * (Dh ** -0.5)
        s = s + c_i[..., :, None] - c[:, :, None, :]
        q_pos = idx * FOX_BLOCK + jnp.arange(FOX_BLOCK)
        s = jnp.where(k_pos[None, :] <= q_pos[:, None], s, -jnp.inf)
        pr = jax.nn.softmax(s, axis=-1)
        return jnp.einsum('bhqk,bkhd->bqhd', pr.astype(v.dtype), v)

    out = lax.map(block, (q_blocks, c_blocks, jnp.arange(nb)))
    return out.transpose(1, 0, 2, 3, 4).reshape(B, S, H * Dh)

def rwkv7_time_mix(z, mu, w0, w2, a0, a2, g2, k_k, k_a, r_k, ln_g, ln_b):
    B, S, _ = z.shape
    H, N = N_HEADS_GROUP, HEAD_DIM
    f32 = jnp.float32
    z_prev = jnp.pad(z, ((0, 0), (1, 0), (0, 0)))[:, :-1]
    z = z + (z_prev - z) * mu
    r, k, v, w_lo, a_lo, g_lo = jnp.split(z, RW_OFFSETS, axis=-1)
    w_log = -jax.nn.softplus(-(w0 + jnp.tanh(w_lo) @ w2).astype(f32)) - 0.5
    decay = jnp.exp(-jnp.exp(w_log))
    a = jax.nn.sigmoid((a0 + a_lo @ a2).astype(f32))
    g = jax.nn.sigmoid(g_lo) @ g2

    def heads(t):
        return t.astype(f32).reshape(B, S, H, N)

    k_f = k.astype(f32)
    kk = heads(k_f * k_k)
    kk = kk / jnp.maximum(jnp.linalg.norm(kk, axis=-1, keepdims=True), 1e-12)
    r_h, v_h = heads(r), heads(v)
    k_h = heads(k_f * (1.0 + (a - 1.0) * k_a))
    w_h, a_h = heads(decay), heads(a)

    def step(state, inp):
        r_t, w_t, k_t, v_t, kk_t, b_t = inp
        sa = jnp.einsum('bhij,bhj->bhi', state, -kk_t)
        state = state * w_t[:, :, None, :] + sa[..., None] * b_t[:, :, None, :] + v_t[..., None] * k_t[:, :, None, :]
        return state, jnp.einsum('bhij,bhj->bhi', state, r_t)

    xs = tuple(jnp.moveaxis(t, 1, 0) for t in (r_h, w_h, k_h, v_h, kk, kk * a_h))
    _, y = lax.scan(step, jnp.zeros((B, H, N, N), f32), xs)
    y = jnp.moveaxis(y, 0, 1)
    mean = jnp.mean(y, axis=-1, keepdims=True)
    var = jnp.mean(jnp.square(y - mean), axis=-1, keepdims=True)
    y = ((y - mean) * lax.rsqrt(var + RW_GN_EPS)).reshape(B, S, GROUP_W) * ln_g + ln_b
    bonus = jnp.sum(r_h * k_h * r_k, axis=-1, keepdims=True) * v_h
    y = (y + bonus.reshape(B, S, GROUP_W)) * g.astype(f32)
    return y.astype(z.dtype)

def swa_with_sinks(q, k, v, sinks):
    B, S, H, Dh = q.shape
    G = k.shape[2]
    R = H // G
    nc = S // CHUNK
    nw = SW_WINDOW_CHUNKS
    qc = q.reshape(B, nc, CHUNK, G, R, Dh)

    def band(t):
        tc = t.reshape(B, nc, CHUNK, G, Dh)
        tp = jnp.pad(tc, ((0, 0), (nw - 1, 0), (0, 0), (0, 0), (0, 0)))
        return jnp.concatenate([tp[:, j:j + nc] for j in range(nw)], axis=2)

    kb, vb = band(k), band(v)
    key_chunk = jnp.arange(nc)[:, None] - (nw - 1) + jnp.arange(nw * CHUNK)[None, :] // CHUNK
    valid = key_chunk >= 0
    s = jnp.einsum('bcqgrd,bckgd->bcgrqk', qc, kb).astype(jnp.float32) * (Dh ** -0.5)
    s = jnp.where(valid[None, :, None, None, None, :], s, -jnp.inf)
    sink = jnp.broadcast_to(sinks.astype(jnp.float32).reshape(G, R)[None, None, :, :, None, None],
                            s.shape[:-1] + (1,))
    pr = jax.nn.softmax(jnp.concatenate([s, sink], axis=-1), axis=-1)[..., :-1]
    o = jnp.einsum('bcgrqk,bckgd->bcqgrd', pr.astype(v.dtype), vb)
    return o.reshape(B, S, H * Dh)

def hybrid_mixer(h, w_in, lru_conv_w, lru_conv_b, lru_wa, lru_ba, lru_wx, lru_bx, lru_lambda,
                 fox_fb, rw_mu, rw_w0, rw_w2, rw_a0, rw_a2, rw_g2, rw_kk, rw_ka, rw_rk,
                 rw_ln_g, rw_ln_b, sw_sinks, grp_gain, w_out):
    B, S, _ = h.shape
    H, N = N_HEADS_GROUP, HEAD_DIM
    (lru_x, lru_gate, fox_q, fox_k, fox_v, fox_f, rw_r, rw_k, rw_v, rw_wlo, rw_alo, rw_glo,
     sw_q, sw_k, sw_v) = jnp.split(h @ w_in, IN_OFFSETS, axis=-1)
    xc = causal_depthwise_conv(lru_x, lru_conv_w, lru_conv_b)
    y_a = rg_lru(xc, lru_wa, lru_ba, lru_wx, lru_bx, lru_lambda) * jax.nn.gelu(lru_gate)
    log_f = jax.nn.log_sigmoid((fox_f + fox_fb).astype(jnp.float32))
    y_b = forgetting_attention(fox_q.reshape(B, S, H, N), fox_k.reshape(B, S, H, N),
                               fox_v.reshape(B, S, H, N), log_f)
    z = jnp.concatenate([rw_r, rw_k, rw_v, rw_wlo, rw_alo, rw_glo], axis=-1)
    y_c = rwkv7_time_mix(z, rw_mu, rw_w0, rw_w2, rw_a0, rw_a2, rw_g2, rw_kk, rw_ka, rw_rk, rw_ln_g, rw_ln_b)
    y_d = swa_with_sinks(sw_q.reshape(B, S, H, N), sw_k.reshape(B, S, SW_KV_HEADS, N),
                         sw_v.reshape(B, S, SW_KV_HEADS, N), sw_sinks)
    y = jnp.stack([y_a, y_b, y_c, y_d], axis=2).astype(jnp.float32)
    y = y * lax.rsqrt(jnp.mean(y * y, axis=-1, keepdims=True) + NORM_EPS)
    y = (y.reshape(B, S, D_MODEL) * grp_gain).astype(h.dtype)
    return y @ w_out

def setup_inputs(seed: int = 0) -> dict:
    key = jax.random.key(seed)
    keys = iter(jax.random.split(key, 64))
    L, H, N = DEPTH, N_HEADS_GROUP, HEAD_DIM

    def nrm(shape, scale=1.0):
        return scale * jax.random.normal(next(keys), shape, jnp.float32)

    def unif(shape, lo, hi):
        return jax.random.uniform(next(keys), shape, jnp.float32, lo, hi)

    def gain(shape):
        return 1.0 + nrm(shape, 0.05)

    a_root = unif((L, GROUP_W), 0.9, 0.999) ** (1.0 / LRU_C)
    return {
        'x': nrm((BATCH, SEQ, D_MODEL)),
        'p': nrm((DEPTH, BATCH, SEQ, D_PLE)),
        'ffn1_pre': gain((L, D_MODEL)),
        'ffn1_post': gain((L, D_MODEL)),
        'ffn1_wg': nrm((L, D_MODEL, D_FF), D_MODEL ** -0.5),
        'ffn1_wu': nrm((L, D_MODEL, D_FF), D_MODEL ** -0.5),
        'ffn1_wd': nrm((L, D_FF, D_MODEL), D_FF ** -0.5),
        'mix_pre': gain((L, D_MODEL)),
        'mix_post': gain((L, D_MODEL)),
        'w_in': nrm((L, D_MODEL, D_IN), D_MODEL ** -0.5),
        'lru_conv_w': nrm((L, CONV_W, GROUP_W), CONV_W ** -0.5),
        'lru_conv_b': nrm((L, GROUP_W), 0.02),
        'lru_wa': nrm((L, H, N, N), N ** -0.5),
        'lru_ba': nrm((L, GROUP_W), 0.02),
        'lru_wx': nrm((L, H, N, N), N ** -0.5),
        'lru_bx': nrm((L, GROUP_W), 0.02),
        'lru_lambda': jnp.log(a_root) - jnp.log1p(-a_root),
        'fox_fb': 3.0 + nrm((L, H), 0.5),
        'rw_mu': unif((L, RW_IN_W), 0.0, 1.0),
        'rw_w0': unif((L, GROUP_W), -6.0, 1.0),
        'rw_w2': nrm((L, RW_DECAY_RANK, GROUP_W), RW_DECAY_RANK ** -0.5),
        'rw_a0': nrm((L, GROUP_W), 0.1),
        'rw_a2': nrm((L, RW_A_RANK, GROUP_W), RW_A_RANK ** -0.5),
        'rw_g2': nrm((L, RW_GATE_RANK, GROUP_W), RW_GATE_RANK ** -0.5),
        'rw_kk': 0.85 + nrm((L, GROUP_W), 0.05),
        'rw_ka': 1.0 + nrm((L, GROUP_W), 0.05),
        'rw_rk': nrm((L, H, N), 0.1),
        'rw_ln_g': gain((L, GROUP_W)),
        'rw_ln_b': nrm((L, GROUP_W), 0.02),
        'sw_sinks': nrm((L, H), 0.5),
        'grp_gain': gain((L, D_MODEL)),
        'w_out': nrm((L, D_MODEL, D_MODEL), D_MODEL ** -0.5),
        'ffn2_pre': gain((L, D_MODEL)),
        'ffn2_post': gain((L, D_MODEL)),
        'ffn2_wg': nrm((L, D_MODEL, D_FF), D_MODEL ** -0.5),
        'ffn2_wu': nrm((L, D_MODEL, D_FF), D_MODEL ** -0.5),
        'ffn2_wd': nrm((L, D_FF, D_MODEL), D_FF ** -0.5),
        'pe_pre': gain((L, D_MODEL)),
        'pe_wg': nrm((L, D_MODEL, D_MODEL), D_MODEL ** -0.5),
        'pe_wp': nrm((L, D_PLE, D_MODEL), D_PLE ** -0.5),
        'pe_post': gain((L, D_MODEL)),
    }

def reference(x, p, ffn1_pre, ffn1_post, ffn1_wg, ffn1_wu, ffn1_wd, mix_pre, mix_post, w_in,
              lru_conv_w, lru_conv_b, lru_wa, lru_ba, lru_wx, lru_bx, lru_lambda, fox_fb,
              rw_mu, rw_w0, rw_w2, rw_a0, rw_a2, rw_g2, rw_kk, rw_ka, rw_rk, rw_ln_g, rw_ln_b,
              sw_sinks, grp_gain, w_out, ffn2_pre, ffn2_post, ffn2_wg, ffn2_wu, ffn2_wd,
              pe_pre, pe_wg, pe_wp, pe_post):
    for i in range(DEPTH):
        x = x + 0.5 * rmsnorm(swiglu(rmsnorm(x, ffn1_pre[i]), ffn1_wg[i], ffn1_wu[i], ffn1_wd[i]), ffn1_post[i])
        m = hybrid_mixer(rmsnorm(x, mix_pre[i]), w_in[i], lru_conv_w[i], lru_conv_b[i], lru_wa[i], lru_ba[i],
                         lru_wx[i], lru_bx[i], lru_lambda[i], fox_fb[i], rw_mu[i], rw_w0[i], rw_w2[i],
                         rw_a0[i], rw_a2[i], rw_g2[i], rw_kk[i], rw_ka[i], rw_rk[i], rw_ln_g[i], rw_ln_b[i],
                         sw_sinks[i], grp_gain[i], w_out[i])
        x = x + rmsnorm(m, mix_post[i])
        x = x + 0.5 * rmsnorm(swiglu(rmsnorm(x, ffn2_pre[i]), ffn2_wg[i], ffn2_wu[i], ffn2_wd[i]), ffn2_post[i])
        gate = jax.nn.sigmoid(rmsnorm(x, pe_pre[i]) @ pe_wg[i])
        x = x + gate * rmsnorm(p[i] @ pe_wp[i], pe_post[i])
    return x


_drawn_inputs = setup_inputs


def setup_inputs(seed=0):
    import zlib

    import numpy as np

    out = dict(_drawn_inputs(seed))
    spreads = {}
    factors = {'lru_ba': 8.0,
     'lru_bx': 8.0,
     'rw_a0': 3.412,
     'rw_kk': 2.734,
     'rw_ln_b': 4.393,
     'sw_sinks': 8.0,
     'ffn2_post': 2.711,
     'pe_pre': 6.546}
    for name, (base, spread) in spreads.items():
        noise = np.random.default_rng([zlib.crc32(name.encode()), seed]).standard_normal(out[name].shape)
        drawn = base * np.exp(spread * noise) if base else spread * noise
        out[name] = __import__('jax').numpy.asarray(drawn.astype(out[name].dtype))
    for name, factor in factors.items():
        out[name] = (out[name] * factor).astype(out[name].dtype)
    return out
```

```python
from contextlib import ExitStack

import numpy as np
import concourse.bass as bass
from concourse import mybir

F32 = mybir.dt.float32
F32R = mybir.dt.float32r
ALU = mybir.AluOpType
ACT = mybir.ActivationFunctionType
AX = mybir.AxisListType

P = 128
SEQ = 512
TB = SEQ // P
D = 1024
KD = D // P
DFF = 2816
KF = DFF // P
DEPTH = 2
GW = 256
NH = 4
HD = 64
DPLE = 256
UNIT = 2048
UP_STEPS = KF // 2
DOWN = KF // 2
FFN_UNITS = 2 * UP_STEPS + DOWN
MIX_UNITS = ["wag", "k", "r", "v", "lx", "lg", "fq", "fk", "fv", "sq", "skv"]
U_FFN1 = 0
U_MIX = FFN_UNITS
U_OUT = U_MIX + len(MIX_UNITS)
U_FFN2 = U_OUT + 4
U_PE = U_FFN2 + FFN_UNITS
NUNITS = U_PE + 5
EPS = 1e-6
GN_EPS = 64e-5
DECAY = float(np.exp(-0.5))
NEG = -1.0e30
CH = 64
NCH = SEQ // CH

VEC = {}
_at = 0
for _n, _w in (("ffn1_pre", 8), ("ffn1_post", 8), ("mix_pre", 8), ("mix_post", 8), ("grp_gain", 8),
               ("ffn2_pre", 8), ("ffn2_post", 8), ("pe_pre", 8), ("pe_post", 8), ("conv_w", 8),
               ("conv_b", 2), ("ba", 2), ("bx", 2), ("lam", 2), ("mu", 8), ("w0", 2), ("a0", 2),
               ("kk", 2), ("ka", 2), ("rk", 2), ("ln_g", 2), ("ln_b", 2), ("fb", 16), ("sink", 4)):
    VEC[_n] = _at
    _at += _w
NVEC = _at
SM = {}
for _n, _w in (("bda", 256), ("bdx", 256), ("wa2", 256), ("g2", 256), ("wf", 32)):
    SM[_n] = _at
    _at += _w
NSMALL = _at
CST = {}
_at = 0
for _n, _w in (("ident", 128), ("ones", 128), ("bones", 128), ("causal", 128), ("band", 256), ("tri", 128),
               ("cols", 4), ("mask4", 512), ("level", 6 * 128), ("reset", 512)):
    CST[_n] = _at
    _at += _w
NCST = _at
NCST_F32 = CST["mask4"]
NORM_TILES = [8, 8, 8, 2, 2, 2, 2, 8, 8, 8, 8, 8]
N_FFN1, N_FFN1P, N_MIX, N_GRP, N_MIXP, N_FFN2, N_FFN2P, N_PE, N_PEP = 0, 1, 2, 3, 7, 8, 9, 10, 11
SQ_BASE = [sum(NORM_TILES[:n]) for n in range(len(NORM_TILES))]
Y_BASE = {N_FFN1P: 0, N_MIXP: 8, N_FFN2P: 16, N_PEP: 24}

LAYER_SEMS = ["small_in", "raw0", "raw1", "hi_done", "lo_done", "unit_done", "sq_ready", "stat_mm", "norm_sd",
        "norm_r", "norm_diag", "norm_rstd", "rstd_used", "h_f", "h_hi_rdy", "h_rdy", "x_upd", "silu_done",
        "act_f", "act_hi_rdy", "act_rdy", "down_d", "y_evac", "dve_step", "act_step", "tile_evac",
        "wf_rdy", "f_mm", "f_abs", "f_y", "f_ln", "f_lf", "c_mm", "c_rdy", "cb_diag", "cb_mm", "cb_rdy",
        "lam_e", "lam_sp", "lru_xc", "lru_mm", "lru_gt", "lru_a", "lru_t", "lru_s", "lru_poly", "lru_th",
        "lru_sqg", "lru_y", "at_s", "at_sc", "at_max", "at_es", "at_exp", "at_p", "at_tr", "at_pt", "at_pv",
        "at_y", "z_mixed", "rw_tanh", "rw_lora", "rw_gates", "rw_cum", "rw_E", "rw_kkr", "rw_sqk", "rw_ss",
        "rw_nrm", "rw_ops", "rw_bonus", "rw_tr", "rw_tok", "rw_bon", "rw_A", "rw_am", "rw_xl", "rw_P",
        "rw_Pe", "rw_TP", "rw_updw", "rw_updt", "rw_av", "rw_avE", "rw_m1", "rw_m1E", "rw_vp", "rw_vpE", "rw_u",
        "rw_usb", "rw_x", "rw_s", "rw_y", "rw_yE", "rw_mean", "rw_ym", "rw_ysq", "rw_var", "rw_sd",
        "rw_done", "p_in", "p_tr", "p_f", "p_hi", "p_rdy", "pt_mm", "gate_rdy", "pg_rdy"]


class Buffers:
    pass


class Semaphores:
    pass


def make_semaphores(make):
    s = Semaphores()
    s.in_cst, s.in_masks, s.in_tr = make("in_cst"), make("in_masks"), make("in_tr")
    s.out_tr, s.out_f, s.out_dma = make("out_tr"), make("out_f"), make("out_dma")
    s.in_x = [make(f"in_x{t}") for t in range(TB)]
    s.of_layer = [make(name) for name in LAYER_SEMS]
    (s.small_in, s.raw0, s.raw1, s.hi_done, s.lo_done, s.unit_done, s.sq_ready,
     s.stat_mm, s.norm_sd, s.norm_r, s.norm_diag, s.norm_rstd, s.rstd_used, s.h_f,
     s.h_hi_rdy, s.h_rdy, s.x_upd, s.silu_done, s.act_f, s.act_hi_rdy, s.act_rdy,
     s.down_d, s.y_evac, s.dve_step, s.act_step, s.tile_evac, s.wf_rdy, s.f_mm,
     s.f_abs, s.f_y, s.f_ln, s.f_lf, s.c_mm, s.c_rdy, s.cb_diag, s.cb_mm,
     s.cb_rdy, s.lam_e, s.lam_sp, s.lru_xc, s.lru_mm, s.lru_gt, s.lru_a,
     s.lru_t, s.lru_s, s.lru_poly, s.lru_th, s.lru_sqg, s.lru_y, s.at_s,
     s.at_sc, s.at_max, s.at_es, s.at_exp, s.at_p, s.at_tr, s.at_pt, s.at_pv,
     s.at_y, s.z_mixed, s.rw_tanh, s.rw_lora, s.rw_gates, s.rw_cum, s.rw_E,
     s.rw_kkr, s.rw_sqk, s.rw_ss, s.rw_nrm, s.rw_ops, s.rw_bonus, s.rw_tr,
     s.rw_tok, s.rw_bon, s.rw_A, s.rw_am, s.rw_xl, s.rw_P, s.rw_Pe, s.rw_TP,
     s.rw_updw, s.rw_updt, s.rw_av, s.rw_avE, s.rw_m1, s.rw_m1E, s.rw_vp,
     s.rw_vpE, s.rw_u, s.rw_usb, s.rw_x, s.rw_s, s.rw_y, s.rw_yE, s.rw_mean,
     s.rw_ym, s.rw_ysq, s.rw_var, s.rw_sd, s.rw_done, s.p_in, s.p_tr, s.p_f,
     s.p_hi, s.p_rdy, s.pt_mm, s.gate_rdy, s.pg_rdy) = s.of_layer
    return s


def host_constants():
    c = np.zeros((P, NCST), np.float32)
    i = np.arange(P)
    c[:, CST["ident"]:CST["ident"] + P] = np.eye(P)
    c[:, CST["ones"]:CST["ones"] + P] = 1
    same = (i[:, None] // CH) == (i[None, :] // CH)
    c[:, CST["bones"]:CST["bones"] + P] = same
    strict = same & (i[:, None] < i[None, :])
    incl = same & (i[:, None] <= i[None, :])
    for n, m in enumerate((strict, incl, strict, incl)):
        c[:, CST["mask4"] + n * P:CST["mask4"] + (n + 1) * P] = m
    for l in range(6):
        b = (i >> l) & 1
        m = ((i[:, None] >> (l + 1)) == (i[None, :] >> (l + 1))) & (b[:, None] == 0) & (b[None, :] == 1)
        c[:, CST["level"] + l * P:CST["level"] + (l + 1) * P] = m
    c[:, CST["causal"]:CST["causal"] + P] = np.where(i[None, :] <= i[:, None], 0, NEG)
    w = np.arange(2 * P)
    first = (i[:, None] // CH) * CH + CH
    c[:, CST["band"]:CST["band"] + 2 * P] = np.where((w[None] >= first) & (w[None] < first + P), 0, NEG)
    c[:, CST["tri"]:CST["tri"] + P] = i[:, None] <= i[None, :]
    c[:, CST["reset"]:CST["reset"] + SEQ] = (np.arange(SEQ) % CH != 0)[None]
    c[:, CST["cols"]:CST["cols"] + 4] = np.array([EPS, GN_EPS, 1.0, 0.0], np.float32)[None]
    return c


def build(nc, x_in, p_in, units, small, consts, out):
    ctx = ExitStack()
    with ctx:
        def sb(name, shape, dt=F32):
            return ctx.enter_context(nc.sbuf_tensor(name, shape, dt))

        x = sb("x", [P, KD, SEQ])
        raw = sb("raw", [P, 2, UNIT])
        whi = sb("whi", [P, 2, UNIT], F32R)
        wlo = sb("wlo", [P, 2, UNIT], F32R)
        scr = sb("scr", [P, 4, SEQ])
        diag = sb("diag", [P, TB, P])
        sm = sb("sm", [P, NSMALL])
        cst = sb("cst", [P, NCST_F32])
        masks = sb("masks", [P, NCST - NCST_F32], mybir.dt.bfloat16)
        sd = sb("sd", [P, TB])
        rinv = sb("rinv", [P, TB])
        wf_hi = sb("wf_hi", [P, KD * NH], F32R)
        wf_lo = sb("wf_lo", [P, KD * NH], F32R)
        tiny = sb("tiny", [P, 160])
        base = nc.sbuf_base
        sb("arena", [P, 60 * SEQ])

        def at(name, tile_offset, shape, dt=F32):
            return nc.alloc_sbuf_tensor_at(name, [P] + shape, dt, offset=base + 4 * tile_offset)
        HALF, TOP = 16 * SEQ, 38 * SEQ + 16
        h_hi, h_lo = at("h_hi", 0, [KD, SEQ], F32R), at("h_lo", 8 * SEQ, [KD, SEQ], F32R)
        y_ffn = at("y_ffn", 0, [KD, SEQ])
        act_hi = at("act_hi_t", HALF, [KF, SEQ], F32R)
        act_lo = at("act_lo_t", HALF + KF * SEQ, [KF, SEQ], F32R)
        y_mix, gate = at("y_mix", HALF, [KD, SEQ]), at("gate", HALF + 8 * SEQ, [KD, SEQ])
        p_raw = at("p_raw", TOP, [TB, DPLE])
        p_hi, p_lo = at("p_hi", TOP + 1024, [2, SEQ], F32R), at("p_lo", TOP + 2048, [2, SEQ], F32R)
        o = HALF
        z = at("z", o, [8, SEQ + 1]); o += 8 * (SEQ + 1)
        lg = at("lg", o, [2, SEQ]); o += 1024
        fq = at("fq", o, [2, SEQ]); o += 1024
        fk = at("fk", o, [2, SEQ]); o += 1024
        fv = at("fv", o, [TB, GW]); o += 1024
        sq = at("sq", o, [2, SEQ]); o += 1024
        sk = at("sk", o, [SEQ]); o += 512
        sv = at("sv", o, [TB, 2 * HD]); o += 512
        lx = at("lx", o, [2, SEQ + 3]); o += 2 * (SEQ + 3)
        assert o <= TOP
        xc, gr, gi, la, lth, la2, gsq, gth = (at(n, TOP + 1024 * i, [2, SEQ]) for i, n in enumerate(
            ("xc", "gr", "gi", "la", "lth", "la2", "gsq", "gth")))
        cb = at("cb", 0, [NH, SEQ])
        prob = at("prob", 4 * SEQ, [3, SEQ])
        probT = at("probT", 7 * SEQ, [2, SEQ])
        am = at("am", TOP, [8, 4, P])
        tm, wm, xl, pm = (at(n, TOP + 4096 + 1024 * i, [8, P]) for i, n in enumerate(("tm", "wm", "xl", "pm")))
        tok = at("tok", TOP + 8192, [4, TB, P])
        m1 = at("m1", TOP + 10240, [SEQ])
        kr = at("kr", 0, [2, SEQ])
        bg, kg, bon, gg, e1, sg, cum, cumx, e2, e3, aa, kkn, kh, bb = (
            at(n, 1024 + 512 * i, [SEQ]) for i, n in enumerate(
                ("bg", "kg", "bon", "gg", "e1", "sg", "cum", "cumx", "e2", "e3", "aa", "kkn", "kh", "bb")))
        av, vp, us = (at(n, 1024 + 512 * i, [8, HD]) for n, i in (("av", 5), ("vp", 6), ("us", 7)))
        yr = at("yr", 1024 + 512 * 8, [SEQ])
        st = at("st", 1024 + 512 * 9, [NCH, HD])
        gsd = at("gsd", 1024 + 512 * 12, [SEQ])
        ym = at("ym", 1024 + 512 * 13, [SEQ])

        psum = ctx.enter_context(nc.psum_tensor("psum", [P, 8, SEQ], F32))

        s = make_semaphores(lambda name: ctx.enter_context(nc.semaphore(name)))
        b = Buffers()
        b.s, b.x, b.raw, b.whi, b.wlo, b.scr = s, x, raw, whi, wlo, scr
        b.psum, b.diag, b.sm, b.cst, b.masks, b.sd = psum, diag, sm, cst, masks, sd
        b.rinv, b.wf_hi, b.wf_lo, b.tiny, b.h_hi, b.h_lo = rinv, wf_hi, wf_lo, tiny, h_hi, h_lo
        b.y_ffn, b.act_hi, b.act_lo, b.y_mix, b.gate, b.p_raw = y_ffn, act_hi, act_lo, y_mix, gate, p_raw
        b.p_hi, b.p_lo, b.z, b.lx, b.lg, b.fq = p_hi, p_lo, z, lx, lg, fq
        b.fk, b.fv, b.sq, b.sk, b.sv, b.xc = fk, fv, sq, sk, sv, xc
        b.gr, b.gi, b.la, b.lth, b.la2, b.gsq = gr, gi, la, lth, la2, gsq
        b.gth, b.cb, b.prob, b.probT, b.am, b.tm = gth, cb, prob, probT, am, tm
        b.wm, b.xl, b.pm, b.tok, b.m1, b.kr = wm, xl, pm, tok, m1, kr
        b.bg, b.kg, b.bon, b.gg, b.e1, b.sg = bg, kg, bon, gg, e1, sg
        b.cum, b.cumx, b.e2, b.e3, b.aa, b.kkn = cum, cumx, e2, e3, aa, kkn
        b.kh, b.bb, b.av, b.vp, b.us, b.yr = kh, bb, av, vp, us, yr
        b.st, b.gsd, b.ym = st, gsd, ym
        load_input(nc, x_in, consts, b)
        with nc.Fori(0, DEPTH) as layer:
            run_layer(nc, layer, p_in, units, small, b)
            for sem in s.of_layer:
                nc.sync.sem_clear(sem)
            nc.all_engine_barrier()
        store_output(nc, out, b)


def load_input(nc, x_in, consts, b):
    s, x, cst, scr, raw, psum = b.s, b.x, b.cst, b.scr, b.raw, b.psum
    ident = cst[:, CST["ident"]:CST["ident"] + P]
    xt = raw[:, :, :].rearrange("p a n -> p (a n)").rearrange("p (t d) -> p t d", t=TB)
    with nc.Block() as block:
        @block.sync
        def _(sp):
            sp.dma_start(cst[:, :], consts[:, 0:NCST_F32]).then_inc(s.in_cst, 16)
            sp.dma_start(scr[:, :, :].rearrange("p a n -> p (a n)")[:, 0:NCST - NCST_F32], consts[:, NCST_F32:NCST]
                         ).then_inc(s.in_masks, 16)
            for t in range(TB):
                sp.dma_start(xt[:, t, :], x_in[t * P:(t + 1) * P, :]).then_inc(s.in_x[t], 16)

        @block.tensor
        def _(pe):
            pe.wait_ge(s.in_cst, 16)
            for k in range(KD):
                for t in range(TB):
                    if k == 0:
                        pe.wait_ge(s.in_x[t], 16)
                    last = nc.tensor.transpose(psum[:, k, t * P:(t + 1) * P], xt[:, t, k * P:(k + 1) * P], ident)
                last.then_inc(s.in_tr, 1)

        @block.vector
        def _(dve):
            dve.wait_ge(s.in_masks, 16)
            nc.vector.tensor_copy(b.masks[:, :], scr[:, :, :].rearrange("p a n -> p (a n)")[:, 0:NCST - NCST_F32])
            for k in range(KD):
                dve.wait_ge(s.in_tr, k + 1)
                nc.vector.tensor_copy(x[:, k, :], psum[:, k, :])


def store_output(nc, out, b):
    s, x, cst, raw, psum = b.s, b.x, b.cst, b.raw, b.psum
    ident = cst[:, CST["ident"]:CST["ident"] + P]
    xt = raw[:, :, :].rearrange("p a n -> p (a n)").rearrange("p (t d) -> p t d", t=TB)
    with nc.Block() as block:
        @block.tensor
        def _(pe):
            for t in range(TB):
                for k in range(KD):
                    last = nc.tensor.transpose(psum[:, 2 * t + k // 4, (k % 4) * P:(k % 4 + 1) * P],
                                               x[:, k, t * P:(t + 1) * P], ident)
                last.then_inc(s.out_tr, 1)

        @block.vector
        def _(dve):
            for t in range(TB):
                dve.wait_ge(s.out_tr, t + 1)
                nc.vector.tensor_copy(xt[:, t, :].rearrange("p (a n) -> p a n", a=2),
                                      psum[:, 2 * t:2 * t + 2, :]).then_inc(s.out_f, 1)

        @block.sync
        def _(sp):
            for t in range(TB):
                sp.wait_ge(s.out_f, t + 1)
                sp.dma_start(out[t * P:(t + 1) * P, :], xt[:, t, :]).then_inc(s.out_dma, 16)
            sp.wait_ge(s.out_dma, 16 * TB)




def run_layer(nc, layer, p_in, units, small, b):
    s, x, raw, whi, wlo, scr, psum = b.s, b.x, b.raw, b.whi, b.wlo, b.scr, b.psum
    h_hi, h_lo, y_ffn, y_mix, gate, act_hi, act_lo = b.h_hi, b.h_lo, b.y_ffn, b.y_mix, b.gate, b.act_hi, b.act_lo
    z, lx, lg, fq, fk, fv, sq, sk, sv = b.z, b.lx, b.lg, b.fq, b.fk, b.fv, b.sq, b.sk, b.sv
    sm, cst, diag, sd, rinv, tiny = b.sm, b.cst, b.diag, b.sd, b.rinv, b.tiny
    V, A, T = nc.vector, nc.scalar, nc.tensor

    def vec(name, j=0, w=1):
        return sm[:, VEC[name] + j:VEC[name] + j + w]

    def mat(name, a, w):
        return sm[:, SM[name] + a:SM[name] + a + w]

    def con(name, a=0, w=P):
        if CST[name] >= NCST_F32:
            return b.masks[:, CST[name] - NCST_F32 + a:CST[name] - NCST_F32 + a + w]
        return cst[:, CST[name] + a:CST[name] + a + w]
    ident, ones, bones = con("ident"), con("ones"), con("bones")
    eps, gn_eps, one = con("cols", 0, 1), con("cols", 1, 1), con("cols", 2, 1)
    YG = [lambda j: lx[:, j, 3:3 + SEQ], lambda j: fq[:, j, :], lambda j: z[:, 4 + j, 1:1 + SEQ], lambda j: sq[:, j, :]]

    la8n, la8p = tiny[:, 0:2], tiny[:, 2:4]
    lam_t = [tiny[:, 4 + 2 * i:6 + 2 * i] for i in range(6)]
    f_y, f_e, f_l, ctok = (tiny[:, 16 + 16 * i:32 + 16 * i] for i in range(4))
    nsink, nmax, esink = tiny[:, 80:84], tiny[:, 84:88], tiny[:, 88:92]
    kam1 = tiny[:, 92:94]
    rsum = tiny[:, 96:128]
    rinv_a = tiny[:, 128:160]

    def ubase(stage):
        return {0: U_FFN1, 1: U_FFN2}[stage]

    def sp_program(sp):
        sp.dma_start(sm[:, :], small[bass.ds(layer, 1)].rearrange("a p n -> (a p) n")).then_inc(s.small_in, 16)
        lu = units[bass.ds(layer, 1)].rearrange("a u p n -> (a u) p n")
        for j in range(2):
            sp.dma_start(raw[:, j, :], lu[j]).then_inc(s.raw0 if j == 0 else s.raw1, 16)
        with sp.Fori(0, NUNITS // 2 - 1) as i:
            for j in range(2):
                src = units[bass.ds(layer, 1), bass.ds(2 * i + (2 + j), 1)].rearrange("a u p n -> (a u p) n")
                sp.wait_ge(s.lo_done, 2 * i + (j + 1))
                sp.dma_start(raw[:, j, :], src).then_inc(s.raw0 if j == 0 else s.raw1, 16)

    def pool_program(pool):
        def lo(j, u):
            pool.wait_ge(s.hi_done, u + 1)
            nc.gpsimd.tensor_tensor(wlo[:, j, :], raw[:, j, :], whi[:, j, :], ALU.subtract).then_inc(s.lo_done, 1)
        with pool.Fori(0, NUNITS // 2) as i:
            for j in range(2):
                lo(j, 2 * i + j)

    def pe_program(pe):
        def blk(slot, n):
            return whi[:, slot, n * P:(n + 1) * P], wlo[:, slot, n * P:(n + 1) * P]

        def mm3(dst, w, a_hi, a_lo, start, stop):
            T.matmul(dst, w[0], a_hi, start=start, stop=False)
            T.matmul(dst, w[0], a_lo, start=False, stop=False)
            return T.matmul(dst, w[1], a_hi, start=False, stop=stop)

        def mm3t(dst, a_hi, a_lo, w_hi, w_lo, start, stop):
            T.matmul(dst, a_hi, w_hi, start=start, stop=False)
            T.matmul(dst, a_hi, w_lo, start=False, stop=False)
            return T.matmul(dst, a_lo, w_hi, start=False, stop=stop)

        def stat(n, k, bank):
            i = SQ_BASE[n] + k
            pe.wait_ge(s.sq_ready, i + 1)
            if k == 0 and n:
                pe.wait_ge(s.norm_sd, n)
            for t in range(TB):
                last = T.matmul(psum[:, bank, t:t + 1], scr[:, i % 4, t * P:(t + 1) * P], ones[:, 0:1],
                                start=(k == 0 and t == 0), stop=(k == NORM_TILES[n] - 1 and t == TB - 1),
                                skip_group_check=True)
            last.then_inc(s.stat_mm, 1)

        def rstd(n, bank):
            pe.wait_ge(s.norm_diag, n + 1)
            if n:
                pe.wait_ge(s.rstd_used, n)
            T.matmul(psum[:, bank, :], ones, diag[:, :, :].rearrange("p t q -> p (t q)"),
                     start=True, stop=True).then_inc(s.norm_rstd, 1)

        def norm(n, sbank=7, rbank=6):
            for k in range(NORM_TILES[n]):
                stat(n, k, sbank)
            rstd(n, rbank)

        def project(u, bank, done_last=True):
            for k in range(KD):
                if u in (U_FFN1, U_MIX, U_OUT, U_FFN2, U_PE):
                    pe.wait_ge(s.h_rdy, h_count(u, k))
                for j in range(2):
                    last = mm3(psum[:, bank + j, :], blk(u % 2, 2 * k + j), h_hi[:, k, :], h_lo[:, k, :],
                               k == 0, k == KD - 1)
            return last

        def h_count(u, k):
            return {U_FFN1: 0, U_MIX: 8, U_OUT: 16, U_FFN2: 24, U_PE: 32}[u] + k + 1

        def ffn(f):
            u0 = ubase(f)
            n_post = (N_FFN1P, N_FFN2P)[f]
            for k in range(KD):
                pe.wait_ge(s.h_rdy, h_count(u0, k))
            with pe.Fori(0, UP_STEPS) as i:
                pe.wait_ge(s.lo_done, 2 * i + (u0 + 1))
                pe.wait_ge(s.silu_done, i + (UP_STEPS * f + 1))
                for k in range(KD):
                    for j in range(2):
                        last = mm3(psum[:, j, :], blk(u0 % 2, 2 * k + j), h_hi[:, k, :], h_lo[:, k, :],
                                   k == 0, k == KD - 1)
                last.then_inc(s.unit_done, 1)
                pe.wait_ge(s.lo_done, 2 * i + (u0 + 2))
                pe.wait_ge(s.act_f, i + (UP_STEPS * f + 1))
                for k in range(KD):
                    for j in range(2):
                        last = mm3(psum[:, 2 + j, :], blk((u0 + 1) % 2, 2 * k + j), h_hi[:, k, :], h_lo[:, k, :],
                                   k == 0, k == KD - 1)
                last.then_inc(s.unit_done, 1)
            d0 = u0 + 2 * UP_STEPS
            pe.wait_ge(s.silu_done, UP_STEPS * (f + 1) + 1)
            pe.wait_ge(s.act_f, UP_STEPS * (f + 1) + 1)

            def down(slot, m, start):
                for ff in range(2):
                    for d in range(KD):
                        last = mm3(psum[:, d, :], blk(slot, ff * KD + d), act_tile(act_hi, m, ff), act_tile(act_lo, m, ff),
                                   start and ff == 0, False)
                last.then_inc(s.unit_done, 1)

            def act_tile(t, m, ff):
                if isinstance(m, int):
                    return t[:, 2 * m + ff, :]
                return t[:, bass.ds(2 * m + ff, 1), :].rearrange("p a n -> p (a n)")
            pe.wait_ge(s.lo_done, d0 + 1)
            pe.wait_ge(s.act_rdy, UP_STEPS * f + 2)
            down(d0 % 2, 0, True)
            with pe.Fori(0, 4) as i:
                for j in (1, 2):
                    pe.wait_ge(s.lo_done, 2 * i + (d0 + j + 1))
                    pe.wait_ge(s.act_rdy, 2 * i + (UP_STEPS * f + j + 2))
                    down((d0 + j) % 2, 2 * i + j, False)
            pe.wait_ge(s.lo_done, d0 + 10)
            pe.wait_ge(s.act_rdy, UP_STEPS * f + 11)
            down((d0 + 9) % 2, 9, False)
            pe.wait_ge(s.lo_done, d0 + 11)
            pe.wait_ge(s.act_rdy, UP_STEPS * (f + 1) + 1)
            slot = (d0 + 10) % 2
            for d in range(KD):
                for ff in range(2):
                    last = mm3(psum[:, d, :], blk(slot, ff * KD + d), act_hi[:, 20 + ff, :], act_lo[:, 20 + ff, :],
                               False, ff == 1)
                last.then_inc(s.down_d, 1)
                if d == KD - 1:
                    pe.wait_ge(s.down_d, KD * (f + 1))
                    pe.sem_inc(s.unit_done, 1)
                if d >= 2:
                    if d == 2:
                        pe.wait_ge(s.y_evac, Y_BASE[n_post] + 1)
                    stat(n_post, d - 2, 0)
            stat(n_post, KD - 2, 0)
            stat(n_post, KD - 1, 0)
            pe.wait_ge(s.y_evac, Y_BASE[n_post] + 2)
            rstd(n_post, 1)

        def unit_ready(u):
            pe.wait_ge(s.lo_done, u + 1)

        pe.wait_ge(s.small_in, 16)
        norm(N_FFN1)
        ffn(0)
        norm(N_MIX)
        for m, name in enumerate(MIX_UNITS):
            u = U_MIX + m
            bank = 2 * (m % 2)
            unit_ready(u)
            if m >= 2:
                pe.wait_ge(s.tile_evac, 2 * (m - 1))
            if name == "fv":
                for t in range(TB):
                    for k in range(KD):
                        c = slice(t * P, (t + 1) * P)
                        last = mm3t(psum[:, bank + t // 2, (t % 2) * GW:(t % 2 + 1) * GW], h_hi[:, k, c], h_lo[:, k, c],
                                    whi[:, u % 2, k * GW:(k + 1) * GW], wlo[:, u % 2, k * GW:(k + 1) * GW],
                                    k == 0, k == KD - 1)
            elif name == "skv":
                for k in range(KD):
                    mm3(psum[:, bank, :], blk(u % 2, 2 * k), h_hi[:, k, :], h_lo[:, k, :], k == 0, k == KD - 1)
                for t in range(TB):
                    for k in range(KD):
                        c = slice(t * P, (t + 1) * P)
                        w = blk(u % 2, 2 * k + 1)
                        last = mm3t(psum[:, bank + 1, t * P:(t + 1) * P], h_hi[:, k, c], h_lo[:, k, c], w[0], w[1],
                                    k == 0, k == KD - 1)
            else:
                last = project(u, bank)
            last.then_inc(s.unit_done, 1)
        pe.wait_ge(s.wf_rdy, 2)
        for t in range(TB):
            for k in range(KD):
                c = slice(t * P, (t + 1) * P)
                last = mm3t(psum[:, 5, t * NH:(t + 1) * NH], h_hi[:, k, c], h_lo[:, k, c],
                            b.wf_hi[:, k * NH:(k + 1) * NH], b.wf_lo[:, k * NH:(k + 1) * NH], k == 0, k == KD - 1)
        last.then_inc(s.f_mm, 1)

        pe.wait_ge(s.tile_evac, 2 * len(MIX_UNITS))
        for j in range(2):
            pe.wait_ge(s.lru_xc, j + 1)
            for g, w in enumerate(("bda", "bdx")):
                T.matmul(psum[:, 2 * j + g, :], mat(w, j * P, P), b.xc[:, j, :], start=True, stop=True
                         ).then_inc(s.lru_mm, 1)

        pe.wait_ge(s.f_lf, 1)
        for t in range(TB):
            for t2 in range(t + 1):
                last = T.matmul(psum[:, 5, 64 + t * NH:64 + (t + 1) * NH], con("tri") if t2 == t else ones,
                                f_l[:, t2 * NH:(t2 + 1) * NH], start=(t2 == 0), stop=(t2 == t))
        last.then_inc(s.c_mm, 1)
        for h in range(NH):
            pe.wait_ge(s.cb_diag, h + 1)
            if h:
                pe.wait_ge(s.cb_rdy, h)
            T.matmul(psum[:, 6, :], ones, diag[:, :, :].rearrange("p t q -> p (t q)"), start=True, stop=True
                     ).then_inc(s.cb_mm, 1)

        def scores(n):
            kind, h, i = n // 16, (n // 4) % 4, n % 4
            bank = n % 3
            if n >= 3:
                pe.wait_ge(s.at_sc, n - 2)
            elif n == 0:
                pe.wait_ge(s.lru_gt, 4)
            q = slice(i * P, (i + 1) * P)
            if kind == 0:
                r = slice(HD * (h % 2), HD * (h % 2) + HD)
                w = (i + 1) * P
                T.matmul(psum[:, bank, 0:w], fq[r, h // 2, q], fk[r, h // 2, 0:w], start=True, stop=False)
                last = T.matmul(psum[:, bank, w - P:w], ident, con("causal"), start=False, stop=True)
            else:
                r = slice(HD * (h // 2), HD * (h // 2) + HD)
                k0 = max(i - 1, 0) * P
                w = (i + 1) * P - k0
                last = T.matmul(psum[:, bank, 0:w], sq[r, h % 2, q], sk[r, k0:k0 + w], start=True, stop=True)
            last.then_inc(s.at_s, 1)

        def key_blocks(n):
            kind, i = n // 16, n % 4
            return list(range(0, i + 1)) if kind == 0 else list(range(max(i - 1, 0), i + 1))

        def turn(n):
            pe.wait_ge(s.at_p, n + 1)
            if n >= 2:
                pe.wait_ge(s.at_pt, n - 1)
            for j, _ in enumerate(key_blocks(n)):
                last = T.transpose(psum[:, 3 + n % 2, j * P:(j + 1) * P], b.prob[:, n % 3, j * P:(j + 1) * P], ident)
            last.then_inc(s.at_tr, 1)

        def weigh(n):
            kind, h, i = n // 16, (n // 4) % 4, n % 4
            pair = n // 8
            pe.wait_ge(s.at_pt, n + 1)
            if n % 8 == 0 and pair >= 2:
                pe.wait_ge(s.at_y, pair - 1)
            rows = slice(HD * (h % 2), HD * (h % 2) + HD)
            blocks = key_blocks(n)
            for j, kb in enumerate(blocks):
                v = fv[:, kb, h * HD:(h + 1) * HD] if kind == 0 else sv[:, kb, (h // 2) * HD:(h // 2) * HD + HD]
                last = T.matmul(psum[rows, (5, 7)[pair % 2], i * P:(i + 1) * P], v, b.probT[:, n % 2, j * P:(j + 1) * P],
                                start=(j == 0), stop=(j == len(blocks) - 1))
            last.then_inc(s.at_pv, 1)

        NU = 32
        for n in range(NU + 2):
            if n == 2:
                pe.wait_ge(s.c_rdy, 1)
            if n < NU:
                scores(n)
            if n >= 1 and n - 1 < NU:
                turn(n - 1)
            if n >= 2:
                weigh(n - 2)

        pe.wait_ge(s.at_y, 4)
        for p in range(2):
            if p:
                pe.wait_ge(s.rw_done, 1)
            c = slice(p * P, (p + 1) * P)
            pe.wait_ge(s.rw_tanh, 2)
            T.matmul(psum[:, 0, :], mat("wa2", p * P, P)[0:64], z[0:64, 0, 1:1 + SEQ], start=True, stop=True
                     ).then_inc(s.rw_lora, 1)
            T.matmul(psum[:, 1, :], mat("wa2", p * P, P)[64:128], z[64:128, 0, 1:1 + SEQ], start=True, stop=True
                     ).then_inc(s.rw_lora, 1)
            T.matmul(psum[:, 2, :], mat("g2", p * P, P), z[:, 1, 1:1 + SEQ], start=True, stop=True
                     ).then_inc(s.rw_lora, 1)
            pe.wait_ge(s.rw_sqk, p + 1)
            T.matmul(psum[:, 3, :], bones, scr[:, 0, :], start=True, stop=True).then_inc(s.rw_ss, 1)
            pe.wait_ge(s.rw_ops, p + 1)
            T.matmul(psum[:, 3, :], bones, scr[:, 1, :], start=True, stop=True).then_inc(s.rw_bonus, 1)
            for q, src in enumerate((b.kr[:, 0, :], b.bg[:, :], b.kg[:, :], z[:, 6 + p, 1:1 + SEQ])):
                for t in range(TB):
                    last = T.transpose(psum[:, 4 + q, t * P:(t + 1) * P], src[:, t * P:(t + 1) * P], ident)
                last.then_inc(s.rw_tr, 1)
            for q in range(8):
                hh, t = q % 2, q // 2
                r = slice(HD * hh, HD * hh + HD)
                n = 8 * p + q
                if q >= 3:
                    pe.wait_ge(s.rw_am, n - 2)
                else:
                    pe.wait_ge(s.rw_gates, 3 * (p + 1))
                kk_r = b.kr[r, :, t * P:(t + 1) * P]
                for g, src in enumerate((b.bg, b.kg)):
                    last = T.matmul(psum[:, q % 3, g * 2 * P:(g + 1) * 2 * P], src[r, t * P:(t + 1) * P], kk_r,
                                    start=True, stop=True)
                last.then_inc(s.rw_A, 1)
            pe.wait_ge(s.rw_am, 8 * (p + 1))
            pe.wait_ge(s.rw_tok, 4 * (p + 1))
            for l in range(6):
                n = 6 * p + l
                pe.wait_ge(s.rw_xl, n + 1)
                if l:
                    pe.wait_ge(s.rw_updw, 6 * p + l)
                    pe.wait_ge(s.rw_updt, 5 * p + l)
                for q in range(8):
                    last = T.matmul(psum[:, q // 4, (q % 4) * P:(q % 4 + 1) * P], b.xl[:, q, :], b.tm[:, q, :],
                                    start=True, stop=True)
                last.then_inc(s.rw_P, 1)
                pe.wait_ge(s.rw_Pe, n + 1)
                for q in range(8):
                    last = T.matmul(psum[:, 4 + q // 4, (q % 4) * P:(q % 4 + 1) * P], b.pm[:, q, :], b.wm[:, q, :],
                                    start=True, stop=True)
                if l < 5:
                    for q in range(8):
                        last = T.matmul(psum[:, 2 + q // 4, (q % 4) * P:(q % 4 + 1) * P], b.wm[:, q, :], b.pm[:, q, :],
                                        start=True, stop=True)
                last.then_inc(s.rw_TP, 1)
            pe.wait_ge(s.rw_updw, 6 * (p + 1))
            for q in range(8):
                hh, t = q % 2, q // 2
                last = T.matmul(psum[:, 0, q * HD:(q + 1) * HD], b.am[:, q, 2, :], b.tok[:, 3, t, hh * HD:(hh + 1) * HD],
                                start=True, stop=True)
            last.then_inc(s.rw_av, 1)
            for q in range(8):
                hh, t = q % 2, q // 2
                last = T.matmul(psum[hh * HD:(hh + 1) * HD, 1, t * P:(t + 1) * P],
                                b.tok[:, 0, t, hh * HD:(hh + 1) * HD], b.wm[:, q, :], start=True, stop=True)
            last.then_inc(s.rw_m1, 1)
            pe.wait_ge(s.rw_avE, p + 1)
            for q in range(8):
                last = T.matmul(psum[:, 2, q * HD:(q + 1) * HD], b.wm[:, q, :], b.av[:, q, :], start=True, stop=True)
            last.then_inc(s.rw_vp, 1)
            pe.wait_ge(s.rw_m1E, p + 1)
            for cc in range(NCH):
                r, t = slice(64 * (cc % 2), 64 * (cc % 2) + 64), cc // 2
                pe.wait_ge(s.rw_s, 8 * p + cc + 1)
                for hh in range(2):
                    hr = slice(hh * HD, (hh + 1) * HD)
                    last = T.matmul(psum[r, 3 + 4 * hh, 0:HD], b.m1[hr, cc * CH:(cc + 1) * CH], b.st[hr, cc, :],
                                    start=True, stop=True)
                last.then_inc(s.rw_u, 1)
                pe.wait_ge(s.rw_usb, 8 * p + cc + 1)
                if cc < NCH - 1:
                    for hh in range(2):
                        hr = slice(hh * HD, (hh + 1) * HD)
                        T.matmul(psum[hr, 4, 0:HD], b.tok[r, 1, t, hr], b.us[r, 2 * t + hh, :], start=True, stop=False)
                        last = T.matmul(psum[hr, 4, 0:HD], b.tok[r, 2, t, hr], b.tok[r, 3, t, hr], start=False, stop=True)
                    last.then_inc(s.rw_x, 1)
            for hh in range(2):
                hr = slice(hh * HD, (hh + 1) * HD)
                for t in range(TB):
                    q = 2 * t + hh
                    for cc in (2 * t, 2 * t + 1):
                        r = slice(cc % 2 * CH, (cc % 2 + 1) * CH)
                        dst = psum[hr, 5, cc * CH:(cc + 1) * CH]
                        T.matmul(dst, b.us[:, q, :], b.am[:, q, 1, r], start=True, stop=False)
                        T.matmul(dst, b.tok[:, 3, t, hr], b.am[:, q, 3, r], start=False, stop=False)
                        last = T.matmul(dst, b.st[hr, cc, :], b.kr[hr, 1, cc * CH:(cc + 1) * CH], start=False, stop=True)
            last.then_inc(s.rw_y, 1)
            pe.wait_ge(s.rw_yE, p + 1)
            T.matmul(psum[:, 6, :], bones, b.yr[:, :], start=True, stop=True).then_inc(s.rw_mean, 1)
            pe.wait_ge(s.rw_ysq, p + 1)
            T.matmul(psum[:, 7, :], bones, scr[:, 0, :], start=True, stop=True).then_inc(s.rw_var, 1)
        pe.wait_ge(s.rw_done, 2)
        for g in range(4):
            norm(N_GRP + g)
        for m in range(4):
            u = U_OUT + m
            unit_ready(u)
            if m >= 2:
                pe.wait_ge(s.y_evac, Y_BASE[N_MIXP] + 2 * (m - 1))
            project(u, 2 * (m % 2)).then_inc(s.unit_done, 1)
        norm(N_MIXP)
        norm(N_FFN2)
        ffn(1)
        norm(N_PE)
        pe.wait_ge(s.p_in, 16)
        for j in range(2):
            for t in range(TB):
                last = T.transpose(psum[:, 4 + j, t * P:(t + 1) * P], b.p_raw[:, t, j * P:(j + 1) * P], ident)
            last.then_inc(s.p_tr, 1)
        for m in range(4):
            u = U_PE + m
            unit_ready(u)
            if m >= 2:
                pe.wait_ge(s.gate_rdy, 2 * (m - 1))
            project(u, 2 * (m % 2)).then_inc(s.unit_done, 1)
        unit_ready(U_PE + 4)
        pe.wait_ge(s.p_rdy, 2)
        for d in range(KD):
            if d < 4:
                pe.wait_ge(s.gate_rdy, 4 + d + 1)
            else:
                pe.wait_ge(s.y_evac, Y_BASE[N_PEP] + d - 3)
            for k in range(2):
                last = mm3(psum[:, d % 4, :], blk((U_PE + 4) % 2, k * KD + d), b.p_hi[:, k, :], b.p_lo[:, k, :],
                           k == 0, k == 1)
            last.then_inc(s.pt_mm, 1)
        norm(N_PEP)

    def act_program(act):
        steps = [0]

        def link(ins):
            steps[0] += 1
            ins.then_inc(s.act_step, 1)
            act.wait_ge(s.act_step, steps[0])

        def hi(slot, raw_count, done):
            act.wait_ge(s.raw0 if slot == 0 else s.raw1, raw_count)
            if done is not None:
                act.wait_ge(s.unit_done, done)
            A.activation(whi[:, slot, :], raw[:, slot, :], ACT.Copy).then_inc(s.hi_done, 1)

        def hi_u(u):
            if u < NUNITS:
                hi(u % 2, 16 * (u // 2 + 1), u - 1 if u >= 2 else None)

        def square(n, k, src):
            i = SQ_BASE[n] + k
            if i >= 4:
                act.wait_ge(s.stat_mm, i - 3)
            A.activation(scr[:, i % 4, :], src, ACT.Square).then_inc(s.sq_ready, 1)

        def root(n, bank, width):
            act.wait_ge(s.stat_mm, SQ_BASE[n] + NORM_TILES[n])
            if n:
                act.wait_ge(s.norm_r, n)
            A.activation(sd[:, :], psum[:, bank, 0:TB], ACT.Sqrt, bias=eps, scale=1.0 / width).then_inc(s.norm_sd, 1)

        def h_part(n_apply, k):
            act.wait_ge(s.h_f, n_apply + 1)
            A.activation(h_hi[:, k, :], scr[:, n_apply % 4, :], ACT.Copy).then_inc(s.h_hi_rdy, 1)

        def norm_of_x(n, upd, apply0):
            for k in range(KD):
                if upd:
                    act.wait_ge(s.x_upd, KD * (upd - 1) + k + 1)
                square(n, k, x[:, k, :])
            root(n, 7, D)
            for k in range(KD):
                h_part(apply0 + k, k)

        def ffn(f):
            u0 = ubase(f)
            n_post = (N_FFN1P, N_FFN2P)[f]
            with act.Fori(0, UP_STEPS) as i:
                act.wait_ge(s.unit_done, 2 * i + (u0 + 1))
                act.wait_ge(s.act_f, i + (UP_STEPS * f + 1))
                A.activation(scr[:, 0:2, :], psum[:, 0:2, :], ACT.Silu).then_inc(s.silu_done, 1)
                hi(u0 % 2, 16 * i + 16 * ((u0 + 2) // 2 + 1), None)
                act.wait_ge(s.act_f, i + (UP_STEPS * f + 2))
                A.activation(act_hi[:, bass.ds(2 * i, 2), :], scr[:, 2:4, :], ACT.Copy).then_inc(s.act_hi_rdy, 1)
                act.wait_ge(s.unit_done, 2 * i + (u0 + 2))
                hi((u0 + 1) % 2, 16 * i + 16 * ((u0 + 3) // 2 + 1), None)
            d0 = u0 + 2 * UP_STEPS
            with act.Fori(0, 5) as i:
                for j in range(2):
                    act.wait_ge(s.unit_done, 2 * i + (d0 + j + 1))
                    hi((d0 + j) % 2, 16 * i + 16 * ((d0 + 2 + j) // 2 + 1), None)
            for d in range(KD):
                act.wait_ge(s.down_d, KD * f + d + 1)
                square(n_post, d, psum[:, d, :])
                A.activation(y_ffn[:, d, :], psum[:, d, :], ACT.Copy,
                             scale=vec(("ffn1_post", "ffn2_post")[f], d)).then_inc(s.y_evac, 1)
            hi_u(d0 + DOWN + 1)
            root(n_post, 0, D)

        act.sem_inc(s.silu_done, 1)
        act.wait_ge(s.small_in, 16)
        hi_u(0)
        hi_u(1)
        norm_of_x(N_FFN1, 0, 0)
        A.activation(b.wf_hi[:, :], mat("wf", 0, 32), ACT.Copy).then_inc(s.wf_rdy, 1)
        link(A.activation(lam_t[0], vec("lam", 0, 2), ACT.Abs))
        A.activation(lam_t[1], lam_t[0], ACT.Exp, scale=-1.0).then_inc(s.lam_e, 1)
        ffn(0)
        norm_of_x(N_MIX, 1, 8)
        for m, name in enumerate(MIX_UNITS):
            u = U_MIX + m
            act.wait_ge(s.unit_done, u + 1)
            bank = 2 * (m % 2)
            two = psum[:, bank:bank + 2, :]
            if name in ("wag", "k", "r", "v"):
                A.activation(z[:, 2 * m:2 * m + 2, 1:1 + SEQ], two, ACT.Copy).then_inc(s.tile_evac, 2)
            elif name == "lx":
                A.activation(lx[:, :, 3:3 + SEQ], two, ACT.Copy).then_inc(s.tile_evac, 2)
            elif name == "fq":
                A.activation(fq[:, :, :], two, ACT.Copy, scale=HD ** -0.5).then_inc(s.tile_evac, 2)
            elif name == "sq":
                A.activation(sq[:, :, :], two, ACT.Copy, scale=HD ** -0.5).then_inc(s.tile_evac, 2)
            elif name == "skv":
                A.activation(sk[:, :], psum[:, bank, :], ACT.Copy).then_inc(s.tile_evac, 1)
                A.activation(sv[:, :, :].rearrange("p t n -> p (t n)"), psum[:, bank + 1, :], ACT.Copy
                             ).then_inc(s.tile_evac, 1)
            else:
                dst = {"lg": lg, "fk": fk}.get(name)
                dst = dst[:, :, :] if dst is not None else fv[:, :, :].rearrange("p (a t) n -> p a (t n)", a=2)
                A.activation(dst, two, ACT.Copy).then_inc(s.tile_evac, 2)
            hi_u(u + 2)
        for j in range(2):
            for g, (dst, bias) in enumerate(((b.gr, "ba"), (b.gi, "bx"))):
                act.wait_ge(s.lru_mm, 2 * j + g + 1)
                A.activation(dst[:, j, :], psum[:, 2 * j + g, :], ACT.Sigmoid, bias=vec(bias, j)).then_inc(s.lru_gt, 1)
        link(A.activation(b.gsq[:, :, :], lg[:, :, :], ACT.Square))
        act.wait_ge(s.lam_sp, 1)
        act.wait_ge(s.lru_gt, 4)
        for j in range(2):
            A.activation(b.la[:, j, :], b.gr[:, j, :], ACT.Exp, scale=la8n[:, j:j + 1]).then_inc(s.lru_a, 1)
            A.activation(b.lth[:, j, :], b.gr[:, j, :], ACT.Tanh, scale=la8p[:, j:j + 1]).then_inc(s.lru_a, 1)
        act.wait_ge(s.lru_a, 4)
        for j in range(2):
            A.activation(b.la2[:, j, :], b.la[:, j, :], ACT.Square).then_inc(s.lru_a, 1)
        act.wait_ge(s.lru_poly, 1)
        A.activation(b.gth[:, :, :], b.gsq[:, :, :], ACT.Tanh, scale=float(np.sqrt(2 / np.pi))).then_inc(s.lru_th, 1)
        for j in range(2):
            act.wait_ge(s.lru_t, j + 1)
            A.activation(b.la2[:, j, :], b.la2[:, j, :], ACT.Sqrt).then_inc(s.lru_s, 1)
        act.wait_ge(s.f_y, 1)
        link(A.activation(f_e, f_y, ACT.Abs))
        link(A.activation(f_e, f_e, ACT.Exp, scale=-1.0))
        A.activation(f_e, f_e, ACT.Ln, bias=one).then_inc(s.f_ln, 1)

        def exps(n):
            kind, h, i = n // 16, (n // 4) % 4, n % 4
            act.wait_ge(s.at_max, n + 1)
            w = (i + 1) * P if kind == 0 else min(i + 1, 2) * P
            c = n % 4
            if kind == 1:
                A.activation(esink[:, c:c + 1], vec("sink", h), ACT.Exp, bias=nmax[:, c:c + 1]).then_inc(s.at_es, 1)
            A.activation(b.prob[:, n % 3, 0:w], b.prob[:, n % 3, 0:w], ACT.Exp, bias=nmax[:, c:c + 1],
                         accum_out=rsum[:, n:n + 1]).then_inc(s.at_exp, 1)

        def turned(n):
            kind, i = n // 16, n % 4
            w = (i + 1) * P if kind == 0 else min(i + 1, 2) * P
            act.wait_ge(s.at_tr, n + 1)
            if n >= 2:
                act.wait_ge(s.at_pv, n - 1)
            A.activation(b.probT[:, n % 2, 0:w], psum[:, 3 + n % 2, 0:w], ACT.Copy).then_inc(s.at_pt, 1)
        for n in range(33):
            if n < 32:
                exps(n)
            if n >= 1:
                turned(n - 1)
        act.wait_ge(s.z_mixed, 2)
        A.activation(z[0:64, 0, 1:1 + SEQ], z[0:64, 0, 1:1 + SEQ], ACT.Tanh).then_inc(s.rw_tanh, 1)
        A.activation(z[:, 1, 1:1 + SEQ], z[:, 1, 1:1 + SEQ], ACT.Sigmoid).then_inc(s.rw_tanh, 1)
        for p in range(2):
            act.wait_ge(s.rw_lora, 3 * p + 1)
            A.activation(b.sg[:, :], psum[:, 0, :], ACT.Sigmoid, bias=vec("w0", p)).then_inc(s.rw_gates, 1)
            act.wait_ge(s.rw_lora, 3 * p + 2)
            A.activation(b.aa[:, :], psum[:, 1, :], ACT.Sigmoid, bias=vec("a0", p)).then_inc(s.rw_gates, 1)
            act.wait_ge(s.rw_lora, 3 * p + 3)
            A.activation(b.gg[:, :], psum[:, 2, :], ACT.Copy).then_inc(s.rw_gates, 1)
            act.wait_ge(s.rw_kkr, p + 1)
            A.activation(scr[:, 0, :], b.kkn[:, :], ACT.Square).then_inc(s.rw_sqk, 1)
            act.wait_ge(s.rw_cum, p + 1)
            A.activation(b.e1[:, :], b.cum[:, :], ACT.Exp, scale=-DECAY).then_inc(s.rw_E, 1)
            A.activation(b.e2[:, :], b.cum[:, :], ACT.Exp, scale=DECAY).then_inc(s.rw_E, 1)
            A.activation(b.e3[:, :], b.cumx[:, :], ACT.Exp, scale=-DECAY).then_inc(s.rw_E, 1)
            act.wait_ge(s.rw_ss, p + 1)
            A.activation(b.bb[:, :], psum[:, 3, :], ACT.Sqrt).then_inc(s.rw_nrm, 1)
            for q in range(4):
                act.wait_ge(s.rw_tr, 4 * p + q + 1)
                A.activation(b.tok[:, q, :, :].rearrange("p t n -> p (t n)"), psum[:, 4 + q, :], ACT.Copy
                             ).then_inc(s.rw_tok, 1)
            for l in range(6):
                act.wait_ge(s.rw_P, 6 * p + l + 1)
                A.activation(b.pm[:, :, :].rearrange("p q n -> p (q n)").rearrange("p (a n) -> p a n", a=2),
                             psum[:, 0:2, :], ACT.Copy).then_inc(s.rw_Pe, 1)
            act.wait_ge(s.rw_av, p + 1)
            A.activation(b.av[:, :, :].rearrange("p q n -> p (q n)"), psum[:, 0, :], ACT.Copy).then_inc(s.rw_avE, 1)
            act.wait_ge(s.rw_m1, p + 1)
            A.activation(b.m1[:, :], psum[:, 1, :], ACT.Copy).then_inc(s.rw_m1E, 1)
            act.wait_ge(s.rw_vp, p + 1)
            A.activation(b.vp[:, :, :].rearrange("p q n -> p (q n)"), psum[:, 2, :], ACT.Copy).then_inc(s.rw_vpE, 1)
            act.wait_ge(s.rw_y, p + 1)
            A.activation(b.yr[:, :], psum[:, 5, :], ACT.Copy).then_inc(s.rw_yE, 1)
            act.wait_ge(s.rw_ym, p + 1)
            A.activation(scr[:, 0, :], b.ym[:, :], ACT.Square).then_inc(s.rw_ysq, 1)
            act.wait_ge(s.rw_var, p + 1)
            A.activation(b.gsd[:, :], psum[:, 7, :], ACT.Sqrt, bias=gn_eps, scale=1.0 / HD).then_inc(s.rw_sd, 1)
        act.wait_ge(s.rw_done, 2)
        for g in range(4):
            for j in range(2):
                square(N_GRP + g, j, YG[g](j))
            root(N_GRP + g, 7, GW)
            for j in range(2):
                h_part(16 + 2 * g + j, 2 * g + j)
        for m in range(4):
            u = U_OUT + m
            act.wait_ge(s.unit_done, u + 1)
            for j in range(2):
                d = 2 * m + j
                bank = 2 * (m % 2) + j
                square(N_MIXP, d, psum[:, bank, :])
                A.activation(y_mix[:, d, :], psum[:, bank, :], ACT.Copy, scale=vec("mix_post", d)).then_inc(s.y_evac, 1)
            hi_u(u + 2)
        root(N_MIXP, 7, D)
        norm_of_x(N_FFN2, 2, 24)
        ffn(1)
        act.dma_start(b.p_raw[:, :, :], p_in[bass.ds(layer, 1)].rearrange("a (t p) d -> p (a t) d", p=P)
                      ).then_inc(s.p_in, 16)
        norm_of_x(N_PE, 3, 32)
        for j in range(2):
            act.wait_ge(s.p_tr, j + 1)
            A.activation(b.p_hi[:, j, :], psum[:, 4 + j, :], ACT.Copy).then_inc(s.p_hi, 1)
        for m in range(4):
            u = U_PE + m
            act.wait_ge(s.unit_done, u + 1)
            for j in range(2):
                A.activation(gate[:, 2 * m + j, :], psum[:, 2 * (m % 2) + j, :], ACT.Sigmoid).then_inc(s.gate_rdy, 1)
            hi_u(u + 2)
        for d in range(KD):
            act.wait_ge(s.pt_mm, d + 1)
            square(N_PEP, d, psum[:, d % 4, :])
            A.activation(y_mix[:, d, :], psum[:, d % 4, :], ACT.Copy, scale=vec("pe_post", d)).then_inc(s.y_evac, 1)
        root(N_PEP, 7, D)

    def dve_program(dve):
        steps = [0]

        def link(ins):
            steps[0] += 1
            ins.then_inc(s.dve_step, 1)
            dve.wait_ge(s.dve_step, steps[0])

        def invert(n):
            dve.wait_ge(s.norm_sd, n + 1)
            V.reciprocal(rinv[:, :], sd[:, :]).then_inc(s.norm_r, 1)
            dve.wait_ge(s.norm_r, n + 1)
            if n:
                dve.wait_ge(s.norm_rstd, n)
            V.tensor_tensor(diag[:, :, :], ident[:, None, :].broadcast_to([P, TB, P]),
                            rinv[:, :, None].broadcast_to([P, TB, P]), ALU.mult).then_inc(s.norm_diag, 1)

        def apply(n, tiles, bank, apply0, gain):
            dve.wait_ge(s.norm_rstd, n + 1)
            cnt = len(tiles)
            for k in range(cnt + 1):
                if k < cnt:
                    src, g, _ = tiles[k]
                    i = V.scalar_tensor_tensor(scr[:, (apply0 + k) % 4, :], src, g, psum[:, bank, :], ALU.mult, ALU.mult)
                    i.then_inc(s.h_f, 1)
                    if k == cnt - 1:
                        dve.wait_ge(s.h_f, apply0 + cnt)
                        dve.sem_inc(s.rstd_used, 1)
                if k >= 1:
                    dst = tiles[k - 1][2]
                    dve.wait_ge(s.h_hi_rdy, apply0 + k)
                    V.tensor_tensor(h_lo[:, dst, :], scr[:, (apply0 + k - 1) % 4, :], h_hi[:, dst, :], ALU.subtract
                                    ).then_inc(s.h_rdy, 1)

        def apply_x(n, apply0, gain):
            apply(n, [(x[:, k, :], vec(gain, k), k) for k in range(KD)], 6, apply0, gain)

        def residual(n, y, bank, half, upd):
            dve.wait_ge(s.y_evac, Y_BASE[n] + KD)
            dve.wait_ge(s.norm_rstd, n + 1)
            for k in range(KD + 1):
                if k < KD:
                    V.scalar_tensor_tensor(y[:, k, :], y[:, k, :], 0.5 if half else 1.0, psum[:, bank, :],
                                           ALU.mult, ALU.mult).then_inc(s.dve_step, 1)
                if k >= 1:
                    dve.wait_ge(s.dve_step, steps[0] + k)
                    if k == KD:
                        dve.sem_inc(s.rstd_used, 1)
                    V.tensor_tensor(x[:, k - 1, :], x[:, k - 1, :], y[:, k - 1, :], ALU.add).then_inc(s.x_upd, 1)
            steps[0] += KD
            dve.wait_ge(s.x_upd, upd * KD)

        def ffn(f):
            with dve.Fori(0, UP_STEPS) as i:
                dve.wait_ge(s.silu_done, i + (UP_STEPS * f + 2))
                dve.wait_ge(s.unit_done, 2 * i + (ubase(f) + 2))
                dve.wait_ge(s.act_rdy, i + (UP_STEPS * f + 1))
                V.tensor_tensor(scr[:, 2:4, :], scr[:, 0:2, :], psum[:, 2:4, :], ALU.mult).then_inc(s.act_f, 1)
                dve.wait_ge(s.act_hi_rdy, i + (UP_STEPS * f + 1))
                V.tensor_tensor(act_lo[:, bass.ds(2 * i, 2), :], scr[:, 2:4, :], act_hi[:, bass.ds(2 * i, 2), :],
                                ALU.subtract).then_inc(s.act_rdy, 1)

        dve.sem_inc(s.act_f, 1)
        dve.sem_inc(s.act_rdy, 1)
        dve.wait_ge(s.small_in, 16)
        invert(N_FFN1)
        apply_x(N_FFN1, 0, "ffn1_pre")
        dve.wait_ge(s.wf_rdy, 1)
        V.tensor_tensor(b.wf_lo[:, :], mat("wf", 0, 32), b.wf_hi[:, :], ALU.subtract).then_inc(s.wf_rdy, 1)
        dve.wait_ge(s.lam_e, 1)
        e, w, w2, acc = lam_t[1], lam_t[2], lam_t[3], lam_t[4]
        link(V.tensor_scalar(w, e, 2.0, None, ALU.add))
        link(V.reciprocal(w2, w))
        link(V.tensor_tensor(w, w2, e, ALU.mult))
        link(V.tensor_tensor(w2, w, w, ALU.mult))
        link(V.memset(acc, 1.0 / 19))
        for n in range(17, 0, -2):
            link(V.tensor_tensor(acc, acc, w2, ALU.mult))
            link(V.tensor_scalar(acc, acc, 1.0 / n, None, ALU.add))
        link(V.tensor_tensor(acc, acc, w, ALU.mult))
        link(V.tensor_scalar(w, vec("lam", 0, 2), -1.0, 0.0, ALU.mult, ALU.max))
        link(V.scalar_tensor_tensor(acc, acc, 2.0, w, ALU.mult, ALU.add))
        link(V.tensor_scalar(la8n, acc, -8.0, None, ALU.mult))
        V.tensor_scalar(la8p, acc, 8.0, None, ALU.mult).then_inc(s.lam_sp, 1)
        link(V.tensor_scalar(nsink, vec("sink", 0, 4), -1.0, None, ALU.mult))
        link(V.tensor_scalar(kam1, vec("ka", 0, 2), -1.0, 1.0, ALU.mult, ALU.add))
        ffn(0)
        invert(N_FFN1P)
        residual(N_FFN1P, y_ffn, 1, True, 1)
        invert(N_MIX)
        apply_x(N_MIX, 8, "mix_pre")
        dve.wait_ge(s.down_d, KD)
        link(V.memset(z[:, :, 0:1], 0.0))
        link(V.memset(lx[:, :, 0:3], 0.0))
        for m in range(4):
            dve.wait_ge(s.tile_evac, 2 * (m + 1))
            d2 = scr[:, 0:2, :]
            link(V.tensor_tensor(d2, z[:, 2 * m:2 * m + 2, 0:SEQ], z[:, 2 * m:2 * m + 2, 1:1 + SEQ], ALU.subtract))
            for j in range(2):
                V.scalar_tensor_tensor(z[:, 2 * m + j, 1:1 + SEQ], scr[:, j, :], vec("mu", 2 * m + j),
                                       z[:, 2 * m + j, 1:1 + SEQ], ALU.mult, ALU.add).then_inc(s.z_mixed, 1)
            dve.wait_ge(s.z_mixed, 2 * (m + 1))
        dve.wait_ge(s.tile_evac, 10)
        for j in range(2):
            link(V.tensor_scalar(b.xc[:, j, :], lx[:, j, 0:SEQ], vec("conv_w", j), vec("conv_b", j), ALU.mult, ALU.add))
            for t in range(1, 4):
                i = V.scalar_tensor_tensor(b.xc[:, j, :], lx[:, j, t:t + SEQ], vec("conv_w", 2 * t + j), b.xc[:, j, :],
                                           ALU.mult, ALU.add)
                if t < 3:
                    link(i)
                else:
                    i.then_inc(s.lru_xc, 1)
        dve.wait_ge(s.lru_a, 1)
        link(V.tensor_scalar(b.gsq[:, :, :], b.gsq[:, :, :], 0.044715, 1.0, ALU.mult, ALU.add))
        V.tensor_tensor(b.gsq[:, :, :], b.gsq[:, :, :], lg[:, :, :], ALU.mult).then_inc(s.lru_poly, 1)
        dve.wait_ge(s.lru_a, 6)
        for j in range(2):
            V.scalar_tensor_tensor(b.la2[:, j, :], b.la2[:, j, :], 1.0, b.lth[:, j, :], ALU.add, ALU.mult
                                   ).then_inc(s.lru_t, 1)
        link(V.tensor_tensor(b.gi[:, :, :], b.gi[:, :, :], b.xc[:, :, :], ALU.mult))
        dve.wait_ge(s.lru_s, 2)
        link(V.tensor_tensor(b.gi[:, :, :], b.gi[:, :, :], b.la2[:, :, :], ALU.mult))
        for j in range(2):
            link(V.tensor_tensor_scan(b.gr[:, j, :], b.la[:, j, :], b.gi[:, j, :], 0.0, ALU.mult, ALU.add))
        dve.wait_ge(s.lru_th, 1)
        link(V.scalar_tensor_tensor(b.gth[:, :, :], b.gth[:, :, :], 1.0, lg[:, :, :], ALU.add, ALU.mult))
        V.scalar_tensor_tensor(lx[:, :, 3:3 + SEQ], b.gr[:, :, :], 0.5, b.gth[:, :, :], ALU.mult, ALU.mult
                               ).then_inc(s.lru_y, 1)
        dve.wait_ge(s.f_mm, 1)
        V.tensor_tensor(f_y, psum[:, 5, 0:16], vec("fb", 0, 16), ALU.add).then_inc(s.f_y, 1)
        dve.wait_ge(s.f_ln, 1)
        V.scalar_tensor_tensor(f_l, f_y, 0.0, f_e, ALU.min, ALU.subtract).then_inc(s.f_lf, 1)
        dve.wait_ge(s.c_mm, 1)
        V.tensor_copy(ctok, psum[:, 5, 64:80]).then_inc(s.c_rdy, 1)
        dve.wait_ge(s.c_rdy, 1)
        dve.wait_ge(s.norm_rstd, 3)
        for h in range(NH):
            col = ctok.rearrange("p (t h) -> p h t", h=NH)[:, h, :]
            V.tensor_tensor(diag[:, :, :], ident[:, None, :].broadcast_to([P, TB, P]),
                            col[:, :, None].broadcast_to([P, TB, P]), ALU.mult).then_inc(s.cb_diag, 1)
            dve.wait_ge(s.cb_mm, h + 1)
            V.tensor_scalar(b.cb[:, h, :], psum[:, 6, :], -1.0, None, ALU.mult).then_inc(s.cb_rdy, 1)
        dve.wait_ge(s.cb_rdy, NH)

        def top(n):
            kind, h, i = n // 16, (n // 4) % 4, n % 4
            w = (i + 1) * P if kind == 0 else min(i + 1, 2) * P
            dst = b.prob[:, n % 3, 0:w]
            dve.wait_ge(s.at_s, n + 1)
            if n >= 3:
                dve.wait_ge(s.at_tr, n - 2)
            if kind == 0:
                V.scalar_tensor_tensor(dst, psum[:, n % 3, 0:w], ctok[:, i * NH + h:i * NH + h + 1], b.cb[:, h, 0:w],
                                       ALU.add, ALU.add).then_inc(s.at_sc, 1)
            else:
                V.tensor_tensor(dst, psum[:, n % 3, 0:w], con("band", 2 * P - w, w), ALU.add).then_inc(s.at_sc, 1)
            dve.wait_ge(s.at_sc, n + 1)
            i = V.tensor_reduce(nmax[:, n % 4:n % 4 + 1], dst, AX.X, ALU.max, negate=True)
            if kind == 1:
                link(i)
                i = V.tensor_tensor(nmax[:, n % 4:n % 4 + 1], nmax[:, n % 4:n % 4 + 1], nsink[:, h:h + 1], ALU.min)
            i.then_inc(s.at_max, 1)

        def share(n):
            kind, h, i = n // 16, (n // 4) % 4, n % 4
            w = (i + 1) * P if kind == 0 else min(i + 1, 2) * P
            dve.wait_ge(s.at_exp, n + 1)
            if kind == 1:
                link(V.tensor_tensor(rsum[:, n:n + 1], rsum[:, n:n + 1], esink[:, n % 4:n % 4 + 1], ALU.add))
            link(V.reciprocal(rinv_a[:, n:n + 1], rsum[:, n:n + 1]))
            V.tensor_scalar(b.prob[:, n % 3, 0:w], b.prob[:, n % 3, 0:w], rinv_a[:, n:n + 1], None, ALU.mult
                            ).then_inc(s.at_p, 1)

        def collect(pair):
            dve.wait_ge(s.at_pv, 8 * (pair + 1))
            dst = (fq if pair < 2 else sq)[:, pair % 2, :]
            V.tensor_copy(dst, psum[:, (5, 7)[pair % 2], :]).then_inc(s.at_y, 1)
        for n in range(34):
            if n < 32:
                top(n)
            if 1 <= n <= 32:
                share(n - 1)
            if n >= 16 and n % 16 == 2:
                collect(2 * (n // 16) - 2)
                collect(2 * (n // 16) - 1)
            if n == 33:
                collect(2)
                collect(3)
        for p in range(2):
            zt = [z[:, 2 * m + p, 1:1 + SEQ] for m in range(4)]
            k_, r_, v_ = zt[1], zt[2], zt[3]
            if p == 0:
                dve.wait_ge(s.at_pv, 32)
            V.tensor_scalar(b.kkn[:, :], k_, vec("kk", p), None, ALU.mult).then_inc(s.rw_kkr, 1)
            dve.wait_ge(s.rw_gates, 3 * p + 1)
            link(V.tensor_tensor_scan(b.cum[:, :], con("reset", 0, SEQ), b.sg[:, :], 0.0, ALU.mult, ALU.add))
            V.tensor_tensor(b.cumx[:, :], b.cum[:, :], b.sg[:, :], ALU.subtract).then_inc(s.rw_cum, 1)
            dve.wait_ge(s.rw_gates, 3 * p + 2)
            link(V.tensor_scalar(b.kh[:, :], b.aa[:, :], vec("ka", p), kam1[:, p:p + 1], ALU.mult, ALU.add))
            link(V.tensor_tensor(b.kh[:, :], b.kh[:, :], k_, ALU.mult))
            link(V.scalar_tensor_tensor(scr[:, 1, :], r_, vec("rk", p), b.kh[:, :], ALU.mult, ALU.mult))
            dve.wait_ge(s.rw_nrm, p + 1)
            link(V.tensor_scalar(b.bb[:, :], b.bb[:, :], 1e-12, None, ALU.max))
            link(V.reciprocal(b.bb[:, :], b.bb[:, :]))
            dve.wait_ge(s.rw_kkr, p + 1)
            link(V.tensor_tensor(b.kkn[:, :], b.kkn[:, :], b.bb[:, :], ALU.mult))
            link(V.tensor_tensor(b.bb[:, :], b.kkn[:, :], b.aa[:, :], ALU.mult))
            dve.wait_ge(s.rw_E, 3 * (p + 1))
            link(V.tensor_tensor(b.bg[:, :], b.bb[:, :], b.e2[:, :], ALU.mult))
            link(V.tensor_tensor(b.kg[:, :], b.kh[:, :], b.e2[:, :], ALU.mult))
            link(V.scalar_tensor_tensor(b.kr[:, 0, :], b.kkn[:, :], -1.0, b.e3[:, :], ALU.mult, ALU.mult))
            V.tensor_tensor(b.kr[:, 1, :], r_, b.e1[:, :], ALU.mult).then_inc(s.rw_ops, 1)
            dve.wait_ge(s.rw_bonus, p + 1)
            V.tensor_tensor(b.bon[:, :], psum[:, 3, :], v_, ALU.mult).then_inc(s.rw_bon, 1)
            m4 = con("mask4", 0, 4 * P)
            for q in range(8):
                dve.wait_ge(s.rw_A, 8 * p + q + 1)
                V.tensor_tensor(b.am[:, q, :, :].rearrange("p g n -> p (g n)"), psum[:, q % 3, :], m4, ALU.mult
                                ).then_inc(s.rw_am, 1)
            V.tensor_copy(b.tm[:, :, :], ident[:, None, :].broadcast_to([P, 8, P])).then_inc(s.dve_step, 1)
            V.tensor_copy(b.wm[:, :, :], ident[:, None, :].broadcast_to([P, 8, P])).then_inc(s.dve_step, 1)
            steps[0] += 2
            dve.wait_ge(s.dve_step, steps[0])
            dve.wait_ge(s.rw_am, 8 * (p + 1))
            for l in range(6):
                V.tensor_tensor(b.xl[:, :, :], b.am[:, :, 0, :],
                                con("level", l * P)[:, None, :].broadcast_to([P, 8, P]), ALU.mult).then_inc(s.rw_xl, 1)
                dve.wait_ge(s.rw_TP, 6 * p + l + 1)
                two = "p q n -> p (q n)"
                w_, t_ = (m[:, :, :].rearrange(two).rearrange("p (a n) -> p a n", a=2) for m in (b.wm, b.tm))
                V.tensor_tensor(w_, w_, psum[:, 4:6, :], ALU.add).then_inc(s.rw_updw, 1)
                if l < 5:
                    V.tensor_tensor(t_, t_, psum[:, 2:4, :], ALU.add).then_inc(s.rw_updt, 1)
                dve.wait_ge(s.rw_updw, 6 * p + l + 1)
                dve.wait_ge(s.rw_updt, 5 * p + min(l + 1, 5))
            V.memset(b.st[:, 0, :], 0.0).then_inc(s.rw_s, 1)
            dve.wait_ge(s.rw_vpE, p + 1)
            for cc in range(NCH):
                r, t = slice(64 * (cc % 2), 64 * (cc % 2) + 64), cc // 2
                dve.wait_ge(s.rw_u, 8 * p + cc + 1)
                V.tensor_tensor(b.us[r, 2 * t:2 * t + 2, :], psum[r, 3:8:4, 0:HD], b.vp[r, 2 * t:2 * t + 2, :], ALU.add
                                ).then_inc(s.rw_usb, 1)
                if cc < NCH - 1:
                    dve.wait_ge(s.rw_x, 7 * p + cc + 1)
                    dve.wait_ge(s.rw_s, 8 * p + cc + 1)
                    link(V.tensor_tensor(b.st[:, cc + 1, :], psum[:, 4, 0:HD], b.st[:, cc, :], ALU.add))
                    last = (cc + 1) * CH - 1
                    V.tensor_scalar(b.st[:, cc + 1, :], b.st[:, cc + 1, :], b.e1[:, last:last + 1], None, ALU.mult
                                    ).then_inc(s.rw_s, 1)
            dve.wait_ge(s.rw_mean, p + 1)
            V.scalar_tensor_tensor(b.ym[:, :], psum[:, 6, :], -1.0 / HD, b.yr[:, :], ALU.mult, ALU.add
                                   ).then_inc(s.rw_ym, 1)
            dve.wait_ge(s.rw_sd, p + 1)
            link(V.reciprocal(b.gsd[:, :], b.gsd[:, :]))
            dve.wait_ge(s.rw_ym, p + 1)
            link(V.tensor_tensor(b.ym[:, :], b.ym[:, :], b.gsd[:, :], ALU.mult))
            link(V.tensor_scalar(b.ym[:, :], b.ym[:, :], vec("ln_g", p), vec("ln_b", p), ALU.mult, ALU.add))
            dve.wait_ge(s.rw_bon, p + 1)
            link(V.tensor_tensor(b.ym[:, :], b.ym[:, :], b.bon[:, :], ALU.add))
            V.tensor_tensor(r_, b.ym[:, :], b.gg[:, :], ALU.mult).then_inc(s.rw_done, 1)
        dve.wait_ge(s.rw_done, 2)
        for g in range(4):
            invert(N_GRP + g)
            apply(N_GRP + g, [(YG[g](j), vec("grp_gain", 2 * g + j), 2 * g + j) for j in range(2)], 6, 16 + 2 * g, "")
        invert(N_MIXP)
        residual(N_MIXP, y_mix, 6, False, 2)
        invert(N_FFN2)
        apply_x(N_FFN2, 24, "ffn2_pre")
        ffn(1)
        invert(N_FFN2P)
        residual(N_FFN2P, y_ffn, 1, True, 3)
        invert(N_PE)
        apply_x(N_PE, 32, "pe_pre")
        for j in range(2):
            dve.wait_ge(s.p_hi, j + 1)
            V.tensor_tensor(b.p_lo[:, j, :], psum[:, 4 + j, :], b.p_hi[:, j, :], ALU.subtract).then_inc(s.p_rdy, 1)
        for d in range(KD):
            dve.wait_ge(s.y_evac, Y_BASE[N_PEP] + d + 1)
            dve.wait_ge(s.gate_rdy, KD)
            link(V.tensor_tensor(y_mix[:, d, :], y_mix[:, d, :], gate[:, d, :], ALU.mult))
        invert(N_PEP)
        residual(N_PEP, y_mix, 6, False, 4)

    with nc.Block() as block:
        @block.sync
        def _(sp):
            sp_program(sp)

        @block.gpsimd
        def _(pool):
            pool_program(pool)

        @block.tensor
        def _(pe):
            pe_program(pe)

        @block.scalar
        def _(act):
            act_program(act)

        @block.vector
        def _(dve):
            dve_program(dve)


def kernel(**inputs):
    import numpy as _np
    import concourse.bacc as _bacc
    from concourse import mybir as _mybir
    from concourse.bass_utils import run_bass_kernel_spmd as _run
    a = {k: _np.asarray(v) for k, v in inputs.items()}

    def cols(w, lo, n=GW):
        return w[:, lo:lo + n].reshape(KD, P, n).transpose(1, 0, 2).reshape(P, KD * n)

    def ffn_units(wg, wu, wd):
        for i in range(UP_STEPS):
            yield cols(wg, i * GW)
            yield cols(wu, i * GW)
        for m in range(DOWN):
            yield wd[2 * m * P:2 * (m + 1) * P].reshape(2, P, D).transpose(1, 0, 2).reshape(P, UNIT)

    off = {"lx": 0, "lg": 256, "fq": 512, "fk": 768, "fv": 1024, "r": 1284, "k": 1540, "v": 1796,
           "wag": 2052, "sq": 2308, "skv": 2564}
    units = _np.empty((DEPTH, NUNITS, P, UNIT), _np.float32)
    small = _np.zeros((DEPTH, P, NSMALL), _np.float32)
    for l in range(DEPTH):
        w_in = a["w_in"][l]
        todo = list(ffn_units(a["ffn1_wg"][l], a["ffn1_wu"][l], a["ffn1_wd"][l]))
        for name in MIX_UNITS:
            if name == "sq":
                w = w_in[:, 2308:2564].reshape(D, NH, HD)[:, [0, 2, 1, 3]].reshape(D, GW)
                todo.append(cols(w, 0))
            else:
                todo.append(cols(w_in, off[name]))
        todo += [cols(a["w_out"][l], m * GW) for m in range(4)]
        todo += list(ffn_units(a["ffn2_wg"][l], a["ffn2_wu"][l], a["ffn2_wd"][l]))
        todo += [cols(a["pe_wg"][l], m * GW) for m in range(4)]
        todo.append(a["pe_wp"][l].reshape(2, P, D).transpose(1, 0, 2).reshape(P, UNIT))
        for u, t in enumerate(todo):
            units[l, u] = t

        def put(name, v):
            v = _np.asarray(v).reshape(-1, P).T
            small[l, :, VEC[name]:VEC[name] + v.shape[1]] = v
        for name in ("ffn1_pre", "ffn1_post", "mix_pre", "mix_post", "grp_gain", "ffn2_pre", "ffn2_post",
                     "pe_pre", "pe_post"):
            put(name, a[name][l])
        put("conv_w", a["lru_conv_w"][l])
        put("conv_b", a["lru_conv_b"][l])
        put("ba", a["lru_ba"][l])
        put("bx", a["lru_bx"][l])
        put("lam", a["lru_lambda"][l])
        mu = a["rw_mu"][l]
        put("mu", _np.concatenate([mu[768:1024], mu[256:512], mu[0:256], mu[512:768]]))
        for name in ("w0", "a0", "kk", "ka", "rk", "ln_g", "ln_b"):
            put(name, a["rw_" + name][l])
        small[l, :, VEC["fb"]:VEC["fb"] + 16] = _np.tile(a["fox_fb"][l], 4)[None]
        small[l, :, VEC["sink"]:VEC["sink"] + 4] = a["sw_sinks"][l][None]
        for h in range(NH):
            r, c = HD * (h % 2), P * (h // 2) + HD * (h % 2)
            small[l, r:r + HD, SM["bda"] + c:SM["bda"] + c + HD] = a["lru_wa"][l, h]
            small[l, r:r + HD, SM["bdx"] + c:SM["bdx"] + c + HD] = a["lru_wx"][l, h]
        small[l, 0:64, SM["wa2"]:SM["wa2"] + GW] = a["rw_w2"][l]
        small[l, 64:128, SM["wa2"]:SM["wa2"] + GW] = a["rw_a2"][l]
        small[l, :, SM["g2"]:SM["g2"] + GW] = a["rw_g2"][l]
        small[l, :, SM["wf"]:SM["wf"] + 32] = cols(w_in, 1280, NH)

    nc = _bacc.Bacc("TRN2", target_bir_lowering=False, num_devices=1)
    arrays = {"x_in": _np.ascontiguousarray(a["x"].reshape(SEQ, D)),
              "p_in": _np.ascontiguousarray(a["p"].reshape(DEPTH, SEQ, DPLE)),
              "units_in": units, "small_in_t": small, "consts_in": host_constants()}
    args = [nc.dram_tensor(n, v.shape, _mybir.dt.from_np(v.dtype), kind="ExternalInput").ap()
            for n, v in arrays.items()]
    args.append(nc.dram_tensor("out_0", (SEQ, D), F32, kind="ExternalOutput").ap())
    build(nc, *args)
    r = _run(nc, [arrays], core_ids=[0])
    return r.results[0]["out_0"].reshape(1, SEQ, D)
```

```python
from contextlib import ExitStack

import numpy as np
import concourse.bass as bass
from concourse import mybir

F32 = mybir.dt.float32
F32R = mybir.dt.float32r
ALU = mybir.AluOpType
ACT = mybir.ActivationFunctionType
AX = mybir.AxisListType

P = 128
SEQ = 512
TB = SEQ // P
D = 1024
KD = D // P
DFF = 2816
KF = DFF // P
DEPTH = 2
GW = 256
NH = 4
HD = 64
DPLE = 256
UNIT = 2048
UP_STEPS = KF // 2
DOWN = KF // 2
FFN_UNITS = 2 * UP_STEPS + DOWN
MIX_UNITS = ["wag", "k", "r", "v", "lx", "lg", "fq", "fk", "fv", "sq", "skv"]
U_FFN1 = 0
U_MIX = FFN_UNITS
U_OUT = U_MIX + len(MIX_UNITS)
U_FFN2 = U_OUT + 4
U_WP = U_FFN2 + FFN_UNITS
U_WG = U_WP + 1
NUNITS = U_WG + 4
EPS = 1e-6
GN_EPS = 64e-5
DECAY = float(np.exp(-0.5))
NEG = -1.0e30
CH = 64
NCH = SEQ // CH

VEC = {}
_at = 0
for _n, _w in (("ffn1_pre", 8), ("ffn1_post", 8), ("mix_pre", 8), ("mix_post", 8), ("grp_gain", 8),
               ("ffn2_pre", 8), ("ffn2_post", 8), ("pe_pre", 8), ("pe_post", 8), ("conv_w", 8),
               ("conv_b", 2), ("ba", 2), ("bx", 2), ("lam", 2), ("mu", 8), ("w0", 2), ("a0", 2),
               ("kk", 2), ("ka", 2), ("rk", 2), ("ln_g", 2), ("ln_b", 2), ("fb", 16), ("sink", 4)):
    VEC[_n] = _at
    _at += _w
NVEC = _at
SM = {}
for _n, _w in (("bda", 256), ("bdx", 256), ("wa2", 256), ("g2", 256), ("wf", 32)):
    SM[_n] = _at
    _at += _w
NSMALL = _at
CST = {}
_at = 0
for _n, _w in (("ident", 128), ("ones", 128), ("bones", 128), ("causal", 128), ("band", 256), ("tri", 128),
               ("cols", 4), ("mask4", 512), ("level", 6 * 128), ("reset", 512)):
    CST[_n] = _at
    _at += _w
NCST = _at
NCST_F32 = CST["mask4"]
N_FFN1, N_FFN1P, N_MIX, N_MIXP, N_FFN2, N_FFN2P, N_PE, N_PEP = range(8)
NORM_TILES = [KD] * 8
SQ_BASE = [sum(NORM_TILES[:n]) for n in range(len(NORM_TILES))]
Y_BASE = {N_FFN1P: 0, N_MIXP: 8, N_FFN2P: 16, N_PEP: 24}

LAYER_SEMS = ["small_in", "raw0", "raw1", "hi_done", "lo_done", "unit_done", "sq_ready", "stat_mm", "norm_sd",
        "norm_r", "norm_rstd", "rstd_used", "h_f", "h_hi_rdy", "h_rdy", "x_upd", "silu_done",
        "act_f", "act_hi_rdy", "act_rdy", "down_d", "y_evac", "dve_step", "act_step", "tile_evac",
        "wf_rdy", "f_mm", "f_t", "f_tr", "f_y", "f_ln", "f_lf", "c_mm", "c_rdy", "cb_mm", "cb_rdy",
        "lam_e", "lam_sp", "lru_xc", "lru_mm", "lru_gt", "lru_a", "lru_t", "lru_s", "lru_poly", "lru_th",
        "lru_y", "at_s", "at_sc", "at_max", "at_es", "at_exp", "at_p", "at_tr", "at_pt", "at_pv",
        "at_y", "z_mixed", "rw_tanh", "rw_lora", "rw_gates", "rw_cum", "rw_E", "rw_kkr", "rw_sqk", "rw_ss",
        "rw_nrm", "rw_ops", "rw_bonus", "rw_tr", "rw_tok", "rw_bon", "rw_A", "rw_am", "rw_xl", "rw_P",
        "rw_Pe", "rw_TP", "rw_updw", "rw_updt", "rw_av", "rw_avE", "rw_m1", "rw_m1E", "rw_vp", "rw_vpE", "rw_u",
        "rw_usb", "rw_x", "rw_s", "rw_y", "rw_yE", "rw_mean", "rw_ym", "rw_ysq", "rw_var", "rw_sd", "rw_kn", "rw_knb", "rw_gs", "rw_gsb",
        "rw_done", "p_in", "p_hi", "p_rdy", "pt_mm", "gate_rdy", "grp_sq", "grp_mm", "grp_sd", "grp_r",
        "grp_rstd"]


ATT_UNITS = 2 * NH * TB
ATT_TICKS = 2 + ATT_UNITS + 4
R_PREP = 4
DENSE = ["R"] * 7
CHAIN = ["R", "T"] * (2 + 2 * NCH - 1)
TAIL = ["R", "T"] * 3
PREP = ["R", "T", "T"] * R_PREP
MERGE = ["T"] + DENSE[:1] + ["T"] + DENSE[1:] + CHAIN + TAIL + PREP + DENSE
_left = ATT_TICKS - MERGE.count("T")
MERGE += ["R", "T"] * _left + ["G"] + ["R"] * 2 + ["G"] + ["R"] * 2 + ["G"]
MERGE += ["R"] * (2 * (R_PREP + 7 + 2 + 2 * NCH - 1 + 3) - R_PREP - MERGE.count("R") - 2) + ["G", "R", "R"]


class Buffers:
    pass


class Semaphores:
    pass


def make_semaphores(make):
    s = Semaphores()
    s.in_cst, s.in_masks, s.out_dma = make("in_cst"), make("in_masks"), make("out_dma")
    s.in_x = [make(f"in_x{n}") for n in range(KD // 2)]
    s.of_layer = [make(name) for name in LAYER_SEMS]
    (s.small_in, s.raw0, s.raw1, s.hi_done, s.lo_done, s.unit_done, s.sq_ready,
     s.stat_mm, s.norm_sd, s.norm_r, s.norm_rstd, s.rstd_used, s.h_f,
     s.h_hi_rdy, s.h_rdy, s.x_upd, s.silu_done, s.act_f, s.act_hi_rdy, s.act_rdy,
     s.down_d, s.y_evac, s.dve_step, s.act_step, s.tile_evac, s.wf_rdy, s.f_mm, s.f_t, s.f_tr,
     s.f_y, s.f_ln, s.f_lf, s.c_mm, s.c_rdy, s.cb_mm,
     s.cb_rdy, s.lam_e, s.lam_sp, s.lru_xc, s.lru_mm, s.lru_gt, s.lru_a,
     s.lru_t, s.lru_s, s.lru_poly, s.lru_th, s.lru_y, s.at_s,
     s.at_sc, s.at_max, s.at_es, s.at_exp, s.at_p, s.at_tr, s.at_pt, s.at_pv,
     s.at_y, s.z_mixed, s.rw_tanh, s.rw_lora, s.rw_gates, s.rw_cum, s.rw_E,
     s.rw_kkr, s.rw_sqk, s.rw_ss, s.rw_nrm, s.rw_ops, s.rw_bonus, s.rw_tr,
     s.rw_tok, s.rw_bon, s.rw_A, s.rw_am, s.rw_xl, s.rw_P, s.rw_Pe, s.rw_TP,
     s.rw_updw, s.rw_updt, s.rw_av, s.rw_avE, s.rw_m1, s.rw_m1E, s.rw_vp,
     s.rw_vpE, s.rw_u, s.rw_usb, s.rw_x, s.rw_s, s.rw_y, s.rw_yE, s.rw_mean,
     s.rw_ym, s.rw_ysq, s.rw_var, s.rw_sd, s.rw_kn, s.rw_knb, s.rw_gs, s.rw_gsb,
     s.rw_done, s.p_in,
     s.p_hi, s.p_rdy, s.pt_mm, s.gate_rdy, s.grp_sq, s.grp_mm, s.grp_sd, s.grp_r,
     s.grp_rstd) = s.of_layer
    return s


def host_constants():
    c = np.zeros((P, NCST), np.float32)
    i = np.arange(P)
    c[:, CST["ident"]:CST["ident"] + P] = np.eye(P)
    c[:, CST["ones"]:CST["ones"] + P] = 1
    same = (i[:, None] // CH) == (i[None, :] // CH)
    c[:, CST["bones"]:CST["bones"] + P] = same
    strict = same & (i[:, None] < i[None, :])
    incl = same & (i[:, None] <= i[None, :])
    for n, m in enumerate((strict, incl, strict, incl)):
        c[:, CST["mask4"] + n * P:CST["mask4"] + (n + 1) * P] = m
    for l in range(6):
        b = (i >> l) & 1
        m = ((i[:, None] >> (l + 1)) == (i[None, :] >> (l + 1))) & (b[:, None] == 0) & (b[None, :] == 1)
        c[:, CST["level"] + l * P:CST["level"] + (l + 1) * P] = m
    c[:, CST["causal"]:CST["causal"] + P] = np.where(i[None, :] <= i[:, None], 0, NEG)
    w = np.arange(2 * P)
    first = (i[:, None] // CH) * CH + CH
    c[:, CST["band"]:CST["band"] + 2 * P] = np.where((w[None] >= first) & (w[None] < first + P), 0, NEG)
    c[:, CST["tri"]:CST["tri"] + P] = i[:, None] <= i[None, :]
    c[:, CST["reset"]:CST["reset"] + SEQ] = (np.arange(SEQ) % CH != 0)[None]
    c[:, CST["cols"]:CST["cols"] + 4] = np.array([EPS, GN_EPS, 1.0, 0.0], np.float32)[None]
    return c


def build(nc, x_in, p_in, units, small, consts, out):
    ctx = ExitStack()
    with ctx:
        def sb(name, shape, dt=F32):
            return ctx.enter_context(nc.sbuf_tensor(name, shape, dt))

        x = sb("x", [P, KD, SEQ])
        raw = sb("raw", [P, 2, UNIT])
        whi = sb("whi", [P, 2, UNIT], F32R)
        wlo = sb("wlo", [P, 2, UNIT], F32R)
        scr = sb("scr", [P, 4, SEQ])
        sm = sb("sm", [P, NSMALL])
        cst = sb("cst", [P, NCST_F32])
        masks = sb("masks", [P, NCST - NCST_F32], mybir.dt.bfloat16)
        sd = sb("sd", [P, 4 * TB])
        rinv = sb("rinv", [P, 4 * TB])
        wf_hi = sb("wf_hi", [P, KD * NH], F32R)
        wf_lo = sb("wf_lo", [P, KD * NH], F32R)
        tiny = sb("tiny", [P, 176])
        base = nc.sbuf_base
        sb("arena", [P, 60 * SEQ])

        def at(name, tile_offset, shape, dt=F32):
            return nc.alloc_sbuf_tensor_at(name, [P] + shape, dt, offset=base + 4 * tile_offset)
        HALF, TOP = 16 * SEQ, 38 * SEQ + 16
        h_hi, h_lo = at("h_hi", 0, [KD, SEQ], F32R), at("h_lo", 8 * SEQ, [KD, SEQ], F32R)
        y_ffn = at("y_ffn", 0, [KD, SEQ])
        act_hi = at("act_hi_t", HALF, [KF, SEQ], F32R)
        act_lo = at("act_lo_t", HALF + KF * SEQ, [KF, SEQ], F32R)
        y_mix, gate = at("y_mix", HALF, [KD, SEQ]), at("gate", HALF + 8 * SEQ, [KD, SEQ])
        p_raw = at("p_raw", 8 * SEQ, [2, SEQ])
        p_hi, p_lo = at("p_hi", 10 * SEQ, [2, SEQ], F32R), at("p_lo", 12 * SEQ, [2, SEQ], F32R)
        o = HALF
        z = at("z", o, [8, SEQ + 1]); o += 8 * (SEQ + 1)
        lg = at("lg", o, [2, SEQ]); o += 1024
        fq = at("fq", o, [2, SEQ]); o += 1024
        fk = at("fk", o, [2, SEQ]); o += 1024
        fv = at("fv", o, [TB, GW]); o += 1024
        sq = at("sq", o, [2, SEQ]); o += 1024
        sk = at("sk", o, [SEQ]); o += 512
        sv = at("sv", o, [TB, 2 * HD]); o += 512
        lx = at("lx", o, [2, SEQ + 3]); o += 2 * (SEQ + 3)
        assert o <= TOP
        def rt(name, tile, shape=None):
            return at(name, TOP + tile * SEQ, shape or [SEQ])
        kr = rt("kr", 0, [2, SEQ])
        e1, e3, e2, bg, kg, nrm, bon, gg = (rt(n, 2 + i) for i, n in enumerate(
            ("e1", "e3", "e2", "bg", "kg", "nrm", "bon", "gg")))
        tok = rt("tok", 10, [4, TB, P])
        st = rt("st", 0, [NCH, HD])
        m1, av, us, yr, vp = rt("m1", 3), rt("av", 4, [8, HD]), rt("us", 5, [8, HD]), rt("yr", 6), rt("vp", 7, [8, HD])
        gsd, ym = rt("gsd", 4), rt("ym", 7)
        am = at("am", 0, [8, 4, P])
        tm, wm, xl, pm = (at(n, 4096 + 1024 * i, [8, P]) for i, n in enumerate(("tm", "wm", "xl", "pm")))
        xc, gr, gi, la, lth = (rt(n, 14 + i) for i, n in enumerate(("xc", "gr", "gi", "la", "lth")))
        cb, prob, probT = rt("cb", 14, [2, SEQ]), rt("prob", 16, [3, SEQ]), rt("probT", 19, [2, SEQ])
        gsq = rt("gsq", 14, [6, SEQ])

        psum = ctx.enter_context(nc.psum_tensor("psum", [P, 8, SEQ], F32))

        s = make_semaphores(lambda name: ctx.enter_context(nc.semaphore(name)))
        b = Buffers()
        b.s, b.x, b.raw, b.whi, b.wlo, b.scr = s, x, raw, whi, wlo, scr
        b.psum, b.sm, b.cst, b.masks, b.sd = psum, sm, cst, masks, sd
        b.rinv, b.wf_hi, b.wf_lo, b.tiny, b.h_hi, b.h_lo = rinv, wf_hi, wf_lo, tiny, h_hi, h_lo
        b.y_ffn, b.act_hi, b.act_lo, b.y_mix, b.gate, b.p_raw = y_ffn, act_hi, act_lo, y_mix, gate, p_raw
        b.p_hi, b.p_lo, b.z, b.lx, b.lg, b.fq = p_hi, p_lo, z, lx, lg, fq
        b.fk, b.fv, b.sq, b.sk, b.sv, b.kr = fk, fv, sq, sk, sv, kr
        b.e1, b.e3, b.e2, b.bg, b.kg, b.nrm = e1, e3, e2, bg, kg, nrm
        b.bon, b.gg, b.tok, b.st, b.m1, b.av = bon, gg, tok, st, m1, av
        b.us, b.yr, b.vp, b.gsd, b.ym, b.am = us, yr, vp, gsd, ym, am
        b.tm, b.wm, b.xl, b.pm, b.xc, b.gr = tm, wm, xl, pm, xc, gr
        b.gi, b.la, b.lth, b.cb, b.prob, b.probT, b.gsq = gi, la, lth, cb, prob, probT, gsq
        load_input(nc, x_in, consts, b)
        with nc.Fori(0, DEPTH) as layer:
            run_layer(nc, layer, p_in, units, small, b)
            for sem in s.of_layer:
                nc.sync.sem_clear(sem)
            nc.all_engine_barrier()
        store_output(nc, out, b)


def load_input(nc, x_in, consts, b):
    s, scr = b.s, b.scr
    with nc.Block() as block:
        @block.sync
        def _(sp):
            sp.dma_start(scr[:, :, :].rearrange("p a n -> p (a n)")[:, 0:NCST - NCST_F32], consts[:, NCST_F32:NCST]
                         ).then_inc(s.in_masks, 16)
            sp.dma_start(b.cst[:, :], consts[:, 0:NCST_F32]).then_inc(s.in_cst, 16)
            for n in range(KD // 2):
                sp.dma_start(b.x[:, 2 * n:2 * n + 2, :], x_in[:, 2 * n:2 * n + 2, :]).then_inc(s.in_x[n], 16)

        @block.vector
        def _(dve):
            dve.wait_ge(s.in_masks, 16)
            nc.vector.tensor_copy(b.masks[:, :], scr[:, :, :].rearrange("p a n -> p (a n)")[:, 0:NCST - NCST_F32])


def store_output(nc, out, b):
    s = b.s
    with nc.Block() as block:
        @block.sync
        def _(sp):
            for n in range(KD // 2):
                sp.dma_start(out[:, 2 * n:2 * n + 2, :], b.x[:, 2 * n:2 * n + 2, :]).then_inc(s.out_dma, 16)
            sp.wait_ge(s.out_dma, 16 * (KD // 2))


def run_layer(nc, layer, p_in, units, small, b):
    s, x, raw, whi, wlo, scr, psum = b.s, b.x, b.raw, b.whi, b.wlo, b.scr, b.psum
    h_hi, h_lo, y_ffn, y_mix, gate, act_hi, act_lo = b.h_hi, b.h_lo, b.y_ffn, b.y_mix, b.gate, b.act_hi, b.act_lo
    z, lx, lg, fq, fk, fv, sq, sk, sv = b.z, b.lx, b.lg, b.fq, b.fk, b.fv, b.sq, b.sk, b.sv
    sm, cst, sd, rinv, tiny = b.sm, b.cst, b.sd, b.rinv, b.tiny
    V, A, T = nc.vector, nc.scalar, nc.tensor

    def vec(name, j=0, w=1):
        return sm[:, VEC[name] + j:VEC[name] + j + w]

    def mat(name, a, w):
        return sm[:, SM[name] + a:SM[name] + a + w]

    def con(name, a=0, w=P):
        if CST[name] >= NCST_F32:
            return b.masks[:, CST[name] - NCST_F32 + a:CST[name] - NCST_F32 + a + w]
        return cst[:, CST[name] + a:CST[name] + a + w]
    ident, ones, bones = con("ident"), con("ones"), con("bones")
    eps, gn_eps, one = con("cols", 0, 1), con("cols", 1, 1), con("cols", 2, 1)
    YG = [lambda j: lx[:, j, 3:3 + SEQ], lambda j: fq[:, j, :], lambda j: z[:, 4 + j, 1:1 + SEQ], lambda j: fk[:, j, :]]

    SPLIT_ORDER = [0, 1, 2, 3, 6, 7, 4, 5]
    key_sum = [b.cb[:, 0, :], b.cb[:, 1, :], scr[:, 2, :], scr[:, 3, :]]
    la8n, la8p = tiny[:, 0:2], tiny[:, 2:4]
    lam_t = [tiny[:, 4 + 2 * i:6 + 2 * i] for i in range(6)]
    f_y, f_e, f_l, ctok = (tiny[:, 16 + 16 * i:32 + 16 * i] for i in range(4))
    nsink, nmax, esink = tiny[:, 80:84], tiny[:, 84:88], tiny[:, 88:92]
    kam1 = tiny[:, 92:94]
    rsum = tiny[:, 96:128]
    rinv_a = tiny[:, 128:160]
    knorm, gnorm = tiny[:, 160:168], tiny[:, 168:176]

    def ubase(stage):
        return {0: U_FFN1, 1: U_FFN2}[stage]

    def sp_program(sp):
        sp.dma_start(sm[:, :], small[bass.ds(layer, 1)].rearrange("a p n -> (a p) n")).then_inc(s.small_in, 16)
        lu = units[bass.ds(layer, 1)].rearrange("a u p n -> (a u) p n")
        for j in range(2):
            sp.dma_start(raw[:, j, :], lu[j]).then_inc(s.raw0 if j == 0 else s.raw1, 16)
        with sp.Fori(0, NUNITS // 2 - 1) as i:
            for j in range(2):
                src = units[bass.ds(layer, 1), bass.ds(2 * i + (2 + j), 1)].rearrange("a u p n -> (a u p) n")
                sp.wait_ge(s.lo_done, 2 * i + (j + 1))
                sp.dma_start(raw[:, j, :], src).then_inc(s.raw0 if j == 0 else s.raw1, 16)

    def pool_program(pool):
        def lo(j, u):
            pool.wait_ge(s.hi_done, u + 1)
            nc.gpsimd.tensor_tensor(wlo[:, j, :], raw[:, j, :], whi[:, j, :], ALU.subtract).then_inc(s.lo_done, 1)
        with pool.Fori(0, NUNITS // 2) as i:
            for j in range(2):
                lo(j, 2 * i + j)

    def spread(bank, column):
        for t in range(TB):
            last = T.matmul(psum[:, bank, t * P:(t + 1) * P], column(t), ident, start=True, stop=True)
        return last

    def spread_heads(bank, values):
        for hh in range(2):
            for t in range(TB):
                last = T.matmul(psum[hh * HD:(hh + 1) * HD, bank, t * P:(t + 1) * P],
                                values[:, 2 * t + hh:2 * t + hh + 1].broadcast_to([P, HD]), ident, start=True, stop=True)
        return last

    def head_sums(bank, src):
        for t in range(TB):
            last = T.matmul(psum[:, bank, 2 * t:2 * t + 2], src[:, t * P:(t + 1) * P], bones[:, 0:P:HD],
                            start=True, stop=True)
        return last

    def pe_attention(pe):
        pe.wait_ge(s.f_lf, 1)
        for t in range(TB):
            for t2 in range(t + 1):
                last = T.matmul(psum[:, 3, t * NH:(t + 1) * NH], con("tri") if t2 == t else ones,
                                f_l[:, t2 * NH:(t2 + 1) * NH], start=(t2 == 0), stop=(t2 == t))
        last.then_inc(s.c_mm, 1)
        yield
        pe.wait_ge(s.c_rdy, 1)
        for h in range(NH):
            spread(h, lambda t: ctok[:, t * NH + h:t * NH + h + 1].broadcast_to([P, P])).then_inc(s.cb_mm, 1)
        yield

        def scores(n):
            kind, h, i = n // 16, (n // 4) % 4, n % 4
            if n >= 2:
                pe.wait_ge(s.at_sc, n - 1)
            else:
                pe.wait_ge(s.cb_rdy, n + 1)
            q = slice(i * P, (i + 1) * P)
            if kind == 0:
                r = slice(HD * (h % 2), HD * (h % 2) + HD)
                w = (i + 1) * P
                T.matmul(psum[:, n % 2, 0:w], fq[r, h // 2, q], fk[r, h // 2, 0:w], start=True, stop=False)
                last = T.matmul(psum[:, n % 2, w - P:w], ident, con("causal"), start=False, stop=True)
            else:
                r = slice(HD * (h // 2), HD * (h // 2) + HD)
                k0 = max(i - 1, 0) * P
                w = (i + 1) * P - k0
                last = T.matmul(psum[:, n % 2, 0:w], sq[r, h % 2, q], sk[r, k0:k0 + w], start=True, stop=True)
            last.then_inc(s.at_s, 1)

        def key_blocks(n):
            kind, i = n // 16, n % 4
            return list(range(0, i + 1)) if kind == 0 else list(range(max(i - 1, 0), i + 1))

        def turn(n):
            pe.wait_ge(s.at_p, n + 1)
            if n >= 1:
                pe.wait_ge(s.at_pt, n)
            else:
                pe.wait_ge(s.cb_rdy, 3)
            for j, _ in enumerate(key_blocks(n)):
                last = T.transpose(psum[:, 2, j * P:(j + 1) * P], b.prob[:, n % 3, j * P:(j + 1) * P], ident)
            last.then_inc(s.at_tr, 1)

        def weigh(n):
            kind, h, i = n // 16, (n // 4) % 4, n % 4
            pair = n // 8
            pe.wait_ge(s.at_pt, n + 1)
            if n == 0:
                pe.wait_ge(s.cb_rdy, 4)
            elif n % 8 == 0:
                pe.wait_ge(s.at_y, pair)
            rows = slice(HD * (h % 2), HD * (h % 2) + HD)
            blocks = key_blocks(n)
            for j, kb in enumerate(blocks):
                v = fv[:, kb, h * HD:(h + 1) * HD] if kind == 0 else sv[:, kb, (h // 2) * HD:(h // 2) * HD + HD]
                last = T.matmul(psum[rows, 3, i * P:(i + 1) * P], v, b.probT[:, n % 2, j * P:(j + 1) * P],
                                start=(j == 0), stop=(j == len(blocks) - 1))
            last.then_inc(s.at_pv, 1)

        scores(0)
        for n in range(ATT_UNITS + 4):
            if n + 1 < ATT_UNITS:
                scores(n + 1)
            if 2 <= n < ATT_UNITS + 2:
                turn(n - 2)
            if 3 <= n < ATT_UNITS + 3:
                weigh(n - 3)
            yield

    def pe_rwkv(pe):
        for p in range(2):
            if p:
                pe.wait_ge(s.rw_done, 1)
            pe.wait_ge(s.rw_tanh, 2)
            T.matmul(psum[:, 4, :], mat("wa2", p * P, P)[0:64], z[0:64, 0, 1:1 + SEQ], start=True, stop=True
                     ).then_inc(s.rw_lora, 1)
            T.matmul(psum[:, 5, :], mat("wa2", p * P, P)[64:128], z[64:128, 0, 1:1 + SEQ], start=True, stop=True
                     ).then_inc(s.rw_lora, 1)
            T.matmul(psum[:, 6, :], mat("g2", p * P, P), z[:, 1, 1:1 + SEQ], start=True, stop=True
                     ).then_inc(s.rw_lora, 1)
            yield
            pe.wait_ge(s.rw_sqk, p + 1)
            head_sums(7, scr[:, 0, :]).then_inc(s.rw_ss, 1)
            yield
            pe.wait_ge(s.rw_kn, p + 1)
            spread_heads(7, knorm).then_inc(s.rw_knb, 1)
            pe.wait_ge(s.rw_ops, p + 1)
            T.matmul(psum[:, 6, :], bones, scr[:, 1, :], start=True, stop=True).then_inc(s.rw_bonus, 1)
            yield
            if p == 0:
                pe.wait_ge(s.lru_gt, 2)
            for q, src in ((0, b.kr[:, 0, :]), (1, b.bg[:, :]), (3, z[:, 6 + p, 1:1 + SEQ]), (2, b.kg[:, :])):
                if q == 2:
                    pe.wait_ge(s.rw_bon, p + 1)
                for t in range(TB):
                    last = T.transpose(psum[:, 4 + q, t * P:(t + 1) * P], src[:, t * P:(t + 1) * P], ident)
                last.then_inc(s.rw_tr, 1)
            yield
            pe.wait_ge(s.rw_tok, 4 * (p + 1))
            if p == 0:
                pe.wait_ge(s.lru_gt, 4)
                pe.wait_ge(s.f_y, 1)
            for q in range(8):
                hh, t = q % 2, q // 2
                r = slice(HD * hh, HD * hh + HD)
                if q >= 4:
                    pe.wait_ge(s.rw_am, 8 * p + q - 3)
                kk_r = b.kr[r, :, t * P:(t + 1) * P]
                for g, src in enumerate((b.bg, b.kg)):
                    last = T.matmul(psum[:, 4 + q % 4, g * 2 * P:(g + 1) * 2 * P], src[r, t * P:(t + 1) * P], kk_r,
                                    start=True, stop=True)
                last.then_inc(s.rw_A, 1)
            yield
            pe.wait_ge(s.rw_am, 8 * (p + 1))
            pe.wait_ge(s.rw_xl, 6 * p + 1)
            for half in range(2):
                for q in range(4):
                    last = T.transpose(psum[:, 5 + 2 * half, q * P:(q + 1) * P], b.xl[:, 4 * half + q, :], ident)
                last.then_inc(s.rw_TP, 1)
            yield
            for l in range(1, 6):
                pe.wait_ge(s.rw_xl, 6 * p + l + 1)
                for half in range(2):
                    pe.wait_ge(s.rw_updw, 12 * p + 2 * l - 1 + half)
                    pe.wait_ge(s.rw_updt, 10 * p + 2 * l - 1 + half)
                    for q in range(4):
                        last = T.matmul(psum[:, 4 + 2 * half, q * P:(q + 1) * P], b.xl[:, 4 * half + q, :],
                                        b.tm[:, 4 * half + q, :], start=True, stop=True)
                    last.then_inc(s.rw_P, 1)
                for half in range(2):
                    pe.wait_ge(s.rw_Pe, 2 * (5 * p + l - 1) + half + 1)
                    for q in range(4):
                        last = T.matmul(psum[:, 4 + 2 * half, q * P:(q + 1) * P], b.pm[:, 4 * half + q, :],
                                        b.wm[:, 4 * half + q, :], start=True, stop=True)
                    if l < 5:
                        for q in range(4):
                            last = T.matmul(psum[:, 5 + 2 * half, q * P:(q + 1) * P], b.wm[:, 4 * half + q, :],
                                            b.pm[:, 4 * half + q, :], start=True, stop=True)
                    last.then_inc(s.rw_TP, 1)
                yield
            pe.wait_ge(s.rw_updw, 12 * (p + 1))
            for q in range(8):
                hh, t = q % 2, q // 2
                last = T.matmul(psum[:, 4, q * HD:(q + 1) * HD], b.am[:, q, 2, :], b.tok[:, 3, t, hh * HD:(hh + 1) * HD],
                                start=True, stop=True)
            last.then_inc(s.rw_av, 1)
            for q in range(8):
                hh, t = q % 2, q // 2
                last = T.matmul(psum[hh * HD:(hh + 1) * HD, 5, t * P:(t + 1) * P],
                                b.tok[:, 0, t, hh * HD:(hh + 1) * HD], b.wm[:, q, :], start=True, stop=True)
            last.then_inc(s.rw_m1, 1)
            yield
            pe.wait_ge(s.rw_avE, p + 1)
            for q in range(8):
                last = T.matmul(psum[:, 6, q * HD:(q + 1) * HD], b.wm[:, q, :], b.av[:, q, :], start=True, stop=True)
            last.then_inc(s.rw_vp, 1)
            yield
            pe.wait_ge(s.rw_m1E, p + 1)
            pe.wait_ge(s.rw_vpE, p + 1)
            for cc in range(NCH):
                r, t = slice(64 * (cc % 2), 64 * (cc % 2) + 64), cc // 2
                pe.wait_ge(s.rw_s, 8 * p + cc + 1)
                for hh in range(2):
                    hr = slice(hh * HD, (hh + 1) * HD)
                    last = T.matmul(psum[r, 4 + 2 * hh, 0:HD], b.m1[hr, cc * CH:(cc + 1) * CH], b.st[hr, cc, :],
                                    start=True, stop=True)
                last.then_inc(s.rw_u, 1)
                yield
                if cc < NCH - 1:
                    pe.wait_ge(s.rw_usb, 8 * p + cc + 1)
                    for hh in range(2):
                        hr = slice(hh * HD, (hh + 1) * HD)
                        T.matmul(psum[hr, 5, 0:HD], b.tok[r, 1, t, hr], b.us[r, 2 * t + hh, :], start=True, stop=False)
                        last = T.matmul(psum[hr, 5, 0:HD], b.tok[r, 2, t, hr], b.tok[r, 3, t, hr], start=False, stop=True)
                    last.then_inc(s.rw_x, 1)
                    yield
            pe.wait_ge(s.rw_usb, 8 * (p + 1))
            for hh in range(2):
                hr = slice(hh * HD, (hh + 1) * HD)
                for t in range(TB):
                    q = 2 * t + hh
                    for cc in (2 * t, 2 * t + 1):
                        r = slice(cc % 2 * CH, (cc % 2 + 1) * CH)
                        dst = psum[hr, 7, cc * CH:(cc + 1) * CH]
                        T.matmul(dst, b.us[:, q, :], b.am[:, q, 1, r], start=True, stop=False)
                        T.matmul(dst, b.tok[:, 3, t, hr], b.am[:, q, 3, r], start=False, stop=False)
                        last = T.matmul(dst, b.st[hr, cc, :], b.kr[hr, 1, cc * CH:(cc + 1) * CH], start=False, stop=True)
            last.then_inc(s.rw_y, 1)
            yield
            pe.wait_ge(s.rw_yE, p + 1)
            T.matmul(psum[:, 4, :], bones, b.yr[:, :], start=True, stop=True).then_inc(s.rw_mean, 1)
            yield
            pe.wait_ge(s.rw_ysq, p + 1)
            head_sums(5, scr[:, 0, :]).then_inc(s.rw_var, 1)
            pe.wait_ge(s.rw_gs, p + 1)
            spread_heads(4, gnorm).then_inc(s.rw_gsb, 1)
            yield

    def group_sum(pe, bank, col, j, i):
        pe.wait_ge(s.grp_sq, i + 1)
        for t in range(TB):
            last = T.matmul(psum[:, bank, col + t:col + t + 1], b.gsq[:, i % 6, t * P:(t + 1) * P], ones[:, 0:1],
                            start=(i in (0, 6) and t == 0), stop=(i in (5, 7) and t == TB - 1), skip_group_check=True)
        if i in (5, 7):
            last.then_inc(s.grp_mm, 1)

    def last_rstd(pe):
        pe.wait_ge(s.grp_r, 2)
        spread(6, lambda t: rinv[:, 12 + t:13 + t].broadcast_to([P, P])).then_inc(s.grp_rstd, 1)

    def pe_groups(pe):
        pe.wait_ge(s.at_y, 4)
        for i in range(6):
            group_sum(pe, 3, 4 * (i // 2), i % 2, i)
        yield
        pe.wait_ge(s.grp_r, 1)
        for i in range(3):
            spread(i, lambda t: rinv[:, 4 * i + t:4 * i + t + 1].broadcast_to([P, P])).then_inc(s.grp_rstd, 1)
        yield
        yield
        yield

    def pe_program(pe):
        def blk(slot, n):
            return whi[:, slot, n * P:(n + 1) * P], wlo[:, slot, n * P:(n + 1) * P]

        def mm3(dst, w, a_hi, a_lo, start, stop):
            T.matmul(dst, w[0], a_hi, start=start, stop=False)
            T.matmul(dst, w[0], a_lo, start=False, stop=False)
            return T.matmul(dst, w[1], a_hi, start=False, stop=stop)

        def mm3t(dst, a_hi, a_lo, w_hi, w_lo, start, stop):
            T.matmul(dst, a_hi, w_hi, start=start, stop=False)
            T.matmul(dst, a_hi, w_lo, start=False, stop=False)
            return T.matmul(dst, a_lo, w_hi, start=False, stop=stop)

        def stat(n, k, bank):
            i = SQ_BASE[n] + k
            pe.wait_ge(s.sq_ready, i + 1)
            if k == 0 and n:
                pe.wait_ge(s.norm_sd, n)
            for t in range(TB):
                last = T.matmul(psum[:, bank, t:t + 1], scr[:, i % 4, t * P:(t + 1) * P], ones[:, 0:1],
                                start=(k == 0 and t == 0), stop=(k == NORM_TILES[n] - 1 and t == TB - 1),
                                skip_group_check=True)
            last.then_inc(s.stat_mm, 1)

        def rstd(n, bank):
            pe.wait_ge(s.norm_r, n + 1)
            if n:
                pe.wait_ge(s.rstd_used, n)
            spread(bank, lambda t: rinv[:, t:t + 1].broadcast_to([P, P])).then_inc(s.norm_rstd, 1)

        def norm(n, sbank=7, rbank=6):
            for k in range(NORM_TILES[n]):
                stat(n, k, sbank)
            rstd(n, rbank)

        def project(u, bank, done_last=True):
            order = SPLIT_ORDER if U_OUT <= u < U_OUT + 4 else range(KD)
            for n, k in enumerate(order):
                if u in (U_MIX, U_OUT, U_WG):
                    pe.wait_ge(s.h_rdy, h_count(u, n))
                for j in range(2):
                    last = mm3(psum[:, bank + j, :], blk(u % 2, 2 * k + j), h_hi[:, k, :], h_lo[:, k, :],
                               n == 0, n == KD - 1)
            return last

        def h_count(u, k):
            return {U_FFN1: 0, U_MIX: 8, U_OUT: 16, U_FFN2: 24, U_WG: 32}[u] + k + 1

        def ffn(f):
            u0 = ubase(f)
            n_post = (N_FFN1P, N_FFN2P)[f]
            def gate_unit(tiles_wait):
                for k in range(KD):
                    if tiles_wait:
                        pe.wait_ge(s.h_rdy, h_count(u0, k))
                    for j in range(2):
                        last = mm3(psum[:, j, :], blk(u0 % 2, 2 * k + j), h_hi[:, k, :], h_lo[:, k, :],
                                   k == 0, k == KD - 1)
                last.then_inc(s.unit_done, 1)

            def up_unit():
                for k in range(KD):
                    for j in range(2):
                        last = mm3(psum[:, 2 + j, :], blk((u0 + 1) % 2, 2 * k + j), h_hi[:, k, :], h_lo[:, k, :],
                                   k == 0, k == KD - 1)
                last.then_inc(s.unit_done, 1)
            pe.wait_ge(s.lo_done, u0 + 1)
            gate_unit(True)
            pe.wait_ge(s.lo_done, u0 + 2)
            up_unit()
            with pe.Fori(0, UP_STEPS - 1) as i:
                pe.wait_ge(s.lo_done, 2 * i + (u0 + 3))
                pe.wait_ge(s.silu_done, i + (UP_STEPS * f + 2))
                gate_unit(False)
                pe.wait_ge(s.lo_done, 2 * i + (u0 + 4))
                pe.wait_ge(s.act_f, i + (UP_STEPS * f + 2))
                up_unit()
            d0 = u0 + 2 * UP_STEPS
            pe.wait_ge(s.silu_done, UP_STEPS * (f + 1) + 1)
            pe.wait_ge(s.act_f, UP_STEPS * (f + 1) + 1)

            def down(slot, m, start):
                for ff in range(2):
                    for d in range(KD):
                        last = mm3(psum[:, d, :], blk(slot, ff * KD + d), act_tile(act_hi, m, ff), act_tile(act_lo, m, ff),
                                   start and ff == 0, False)
                last.then_inc(s.unit_done, 1)

            def act_tile(t, m, ff):
                if isinstance(m, int):
                    return t[:, 2 * m + ff, :]
                return t[:, bass.ds(2 * m + ff, 1), :].rearrange("p a n -> p (a n)")
            pe.wait_ge(s.lo_done, d0 + 1)
            pe.wait_ge(s.act_rdy, UP_STEPS * f + 2)
            down(d0 % 2, 0, True)
            with pe.Fori(0, 4) as i:
                for j in (1, 2):
                    pe.wait_ge(s.lo_done, 2 * i + (d0 + j + 1))
                    pe.wait_ge(s.act_rdy, 2 * i + (UP_STEPS * f + j + 2))
                    down((d0 + j) % 2, 2 * i + j, False)
            pe.wait_ge(s.lo_done, d0 + 10)
            pe.wait_ge(s.act_rdy, UP_STEPS * f + 11)
            down((d0 + 9) % 2, 9, False)
            pe.wait_ge(s.lo_done, d0 + 11)
            pe.wait_ge(s.act_rdy, UP_STEPS * (f + 1) + 1)
            slot = (d0 + 10) % 2
            for d in range(KD):
                for ff in range(2):
                    last = mm3(psum[:, d, :], blk(slot, ff * KD + d), act_hi[:, 20 + ff, :], act_lo[:, 20 + ff, :],
                               False, ff == 1)
                last.then_inc(s.down_d, 1)
                if d == KD - 1:
                    pe.wait_ge(s.down_d, KD * (f + 1))
                    pe.sem_inc(s.unit_done, 1)
                if d >= 2:
                    if d == 2:
                        pe.wait_ge(s.y_evac, Y_BASE[n_post] + 1)
                    stat(n_post, d - 2, 0)
            stat(n_post, KD - 2, 0)
            stat(n_post, KD - 1, 0)
            pe.wait_ge(s.y_evac, Y_BASE[n_post] + 2)
            rstd(n_post, 1)

        def unit_ready(u):
            pe.wait_ge(s.lo_done, u + 1)

        norm(N_FFN1)
        ffn(0)
        norm(N_MIX)
        rwkv = pe_rwkv(pe)
        for m, name in enumerate(MIX_UNITS):
            u = U_MIX + m
            bank = 2 * (m % 2)
            unit_ready(u)
            if m >= 2:
                pe.wait_ge(s.tile_evac, 2 * (m - 1))
            if name == "fv":
                for t in range(TB):
                    for k in range(KD):
                        c = slice(t * P, (t + 1) * P)
                        last = mm3t(psum[:, bank + t // 2, (t % 2) * GW:(t % 2 + 1) * GW], h_hi[:, k, c], h_lo[:, k, c],
                                    whi[:, u % 2, k * GW:(k + 1) * GW], wlo[:, u % 2, k * GW:(k + 1) * GW],
                                    k == 0, k == KD - 1)
            elif name == "skv":
                for k in range(KD):
                    mm3(psum[:, bank, :], blk(u % 2, 2 * k), h_hi[:, k, :], h_lo[:, k, :], k == 0, k == KD - 1)
                for t in range(TB):
                    for k in range(KD):
                        c = slice(t * P, (t + 1) * P)
                        w = blk(u % 2, 2 * k + 1)
                        last = mm3t(psum[:, bank + 1, t * P:(t + 1) * P], h_hi[:, k, c], h_lo[:, k, c], w[0], w[1],
                                    k == 0, k == KD - 1)
            else:
                last = project(u, bank)
            last.then_inc(s.unit_done, 1)
            if m == 4 or m == 5 or m == 7 or m == 8:
                next(rwkv)
            if m == 6 or m == 9:
                j = 0 if m == 6 else 1
                pe.wait_ge(s.lru_xc, j + 1)
                if j == 0:
                    pe.wait_ge(s.rw_gates, 3)
                else:
                    pe.wait_ge(s.rw_tok, 4)
                for g, w in enumerate(("bda", "bdx")):
                    T.matmul(psum[:, 4 + g, :], mat(w, j * P, P), b.xc[:, :], start=True, stop=True
                             ).then_inc(s.lru_mm, 1)
        pe.wait_ge(s.wf_rdy, 2)
        for k in range(KD):
            last = mm3(psum[0:NH, 7, :], (b.wf_hi[:, k * NH:(k + 1) * NH], b.wf_lo[:, k * NH:(k + 1) * NH]),
                       h_hi[:, k, :], h_lo[:, k, :], k == 0, k == KD - 1)
        last.then_inc(s.f_mm, 1)
        pe.wait_ge(s.f_t, 1)
        for t in range(TB):
            last = T.transpose(psum[:, 7, t * NH:(t + 1) * NH], b.probT[0:NH, 0, t * P:(t + 1) * P], ident[0:NH, 0:NH])
        last.then_inc(s.f_tr, 1)

        pe.wait_ge(s.tile_evac, 2 * len(MIX_UNITS))
        turns = {"R": rwkv, "T": pe_attention(pe), "G": pe_groups(pe)}
        for turn in MERGE:
            next(turns[turn])
        for j in range(2):
            group_sum(pe, 3, 12, j, 6 + j)
        last_rstd(pe)
        for m in range(4):
            u = U_OUT + m
            unit_ready(u)
            if m >= 2:
                pe.wait_ge(s.y_evac, Y_BASE[N_MIXP] + 2 * (m - 1))
            project(u, 2 * (m % 2)).then_inc(s.unit_done, 1)
        norm(N_MIXP)
        norm(N_FFN2)
        ffn(1)
        unit_ready(U_WP)
        pe.wait_ge(s.p_rdy, 1)
        pe.wait_ge(s.y_evac, Y_BASE[N_FFN2P] + KD)
        for d in range(KD + 2):
            if d < KD:
                if d >= 4:
                    pe.wait_ge(s.y_evac, Y_BASE[N_PEP] + d - 3)
                for k in range(2):
                    last = mm3(psum[:, 2 + d % 4, :], blk(U_WP % 2, k * KD + d), b.p_hi[:, k, :], b.p_lo[:, k, :],
                               k == 0, k == 1)
                last.then_inc(s.pt_mm, 1)
            if d == KD:
                pe.wait_ge(s.pt_mm, KD)
                pe.sem_inc(s.unit_done, 1)
            if d >= 2:
                stat(N_PE, d - 2, 7)
        rstd(N_PE, 6)
        pe.wait_ge(s.y_evac, Y_BASE[N_PEP] + KD)
        for m in range(4):
            u = U_WG + m
            unit_ready(u)
            if m >= 2:
                pe.wait_ge(s.gate_rdy, 2 * (m - 1))
            project(u, 2 * (m % 2)).then_inc(s.unit_done, 1)
            if m == 1:
                for k in range(KD):
                    stat(N_PEP, k, 7)
            if m == 2:
                rstd(N_PEP, 6)

    def act_attention(act):
        def exps(n):
            kind, h, i = n // 16, (n // 4) % 4, n % 4
            act.wait_ge(s.at_max, n + 1)
            w = (i + 1) * P if kind == 0 else min(i + 1, 2) * P
            c = n % 4
            if kind == 1:
                A.activation(esink[:, c:c + 1], vec("sink", h), ACT.Exp, bias=nmax[:, c:c + 1]).then_inc(s.at_es, 1)
            A.activation(b.prob[:, n % 3, 0:w], b.prob[:, n % 3, 0:w], ACT.Exp, bias=nmax[:, c:c + 1],
                         accum_out=rsum[:, n:n + 1]).then_inc(s.at_exp, 1)

        def turned(n):
            kind, i = n // 16, n % 4
            w = (i + 1) * P if kind == 0 else min(i + 1, 2) * P
            act.wait_ge(s.at_tr, n + 1)
            if n >= 2:
                act.wait_ge(s.at_pv, n - 1)
            A.activation(b.probT[:, n % 2, 0:w], psum[:, 2, 0:w], ACT.Copy).then_inc(s.at_pt, 1)
        yield
        for h in range(NH):
            act.wait_ge(s.cb_mm, h + 1)
            A.activation(key_sum[h], psum[:, h, :], ACT.Copy, scale=-1.0).then_inc(s.cb_rdy, 1)
        yield
        for n in range(ATT_UNITS + 4):
            if 2 <= n < ATT_UNITS + 2:
                turned(n - 2)
            if n < ATT_UNITS:
                exps(n)
            yield

    def act_rwkv(act):
        for p in range(2):
            act.wait_ge(s.rw_kkr, p + 1)
            A.activation(scr[:, 0, :], b.kr[:, 0, :], ACT.Square).then_inc(s.rw_sqk, 1)
            act.wait_ge(s.rw_lora, 3 * p + 1)
            A.activation(b.e3[:, :], psum[:, 4, :], ACT.Sigmoid, bias=vec("w0", p)).then_inc(s.rw_gates, 1)
            act.wait_ge(s.rw_lora, 3 * p + 2)
            A.activation(b.bg[:, :], psum[:, 5, :], ACT.Sigmoid, bias=vec("a0", p)).then_inc(s.rw_gates, 1)
            act.wait_ge(s.rw_lora, 3 * p + 3)
            A.activation(b.gg[:, :], psum[:, 6, :], ACT.Copy).then_inc(s.rw_gates, 1)
            yield
            act.wait_ge(s.rw_cum, p + 1)
            A.activation(b.e2[:, :], b.e1[:, :], ACT.Exp, scale=DECAY).then_inc(s.rw_E, 1)
            A.activation(b.e3[:, :], b.e3[:, :], ACT.Exp, scale=-DECAY).then_inc(s.rw_E, 1)
            A.activation(b.e1[:, :], b.e1[:, :], ACT.Exp, scale=-DECAY).then_inc(s.rw_E, 1)
            act.wait_ge(s.rw_ss, p + 1)
            A.activation(knorm, psum[:, 7, 0:8], ACT.Sqrt).then_inc(s.rw_nrm, 1)
            yield
            yield
            for n, q in enumerate((0, 1, 3, 2)):
                act.wait_ge(s.rw_tr, 4 * p + n + 1)
                A.activation(b.tok[:, q, :, :].rearrange("p t n -> p (t n)"), psum[:, 4 + q, :], ACT.Copy
                             ).then_inc(s.rw_tok, 1)
            yield
            yield
            yield
            for l in range(1, 6):
                for half in range(2):
                    act.wait_ge(s.rw_P, 2 * (5 * p + l - 1) + half + 1)
                    A.activation(b.pm[:, 4 * half:4 * half + 4, :].rearrange("p q n -> p (q n)"),
                                 psum[:, 4 + 2 * half, :], ACT.Copy).then_inc(s.rw_Pe, 1)
                yield
            act.wait_ge(s.rw_av, p + 1)
            A.activation(b.av[:, :, :].rearrange("p q n -> p (q n)"), psum[:, 4, :], ACT.Copy).then_inc(s.rw_avE, 1)
            act.wait_ge(s.rw_m1, p + 1)
            A.activation(b.m1[:, :], psum[:, 5, :], ACT.Copy).then_inc(s.rw_m1E, 1)
            yield
            act.wait_ge(s.rw_vp, p + 1)
            A.activation(b.vp[:, :, :].rearrange("p q n -> p (q n)"), psum[:, 6, :], ACT.Copy).then_inc(s.rw_vpE, 1)
            yield
            for cc in range(2 * NCH - 1):
                yield
            act.wait_ge(s.rw_y, p + 1)
            A.activation(b.yr[:, :], psum[:, 7, :], ACT.Copy).then_inc(s.rw_yE, 1)
            yield
            act.wait_ge(s.rw_ym, p + 1)
            A.activation(scr[:, 0, :], b.ym[:, :], ACT.Square).then_inc(s.rw_ysq, 1)
            yield
            act.wait_ge(s.rw_var, p + 1)
            A.activation(gnorm, psum[:, 5, 0:8], ACT.Sqrt, bias=gn_eps, scale=1.0 / HD).then_inc(s.rw_sd, 1)
            yield

    def act_groups(act):
        act.wait_ge(s.at_y, 4)
        act.wait_ge(s.lru_y, 2)
        for i, k in enumerate(SPLIT_ORDER[:6]):
            A.activation(b.gsq[:, i, :], YG[k // 2](k % 2), ACT.Square).then_inc(s.grp_sq, 1)
        yield
        act.wait_ge(s.grp_mm, 1)
        A.activation(sd[:, 0:12], psum[:, 3, 0:12], ACT.Sqrt, bias=eps, scale=1.0 / GW).then_inc(s.grp_sd, 1)
        yield
        yield
        act.wait_ge(s.rw_y, 2)
        for i, k in enumerate(SPLIT_ORDER[:6]):
            group_hi(act, i, k)
        yield

    def group_hi(act, i, k):
        act.wait_ge(s.h_f, 16 + i + 1)
        A.activation(h_hi[:, k, :], YG[k // 2](k % 2), ACT.Copy).then_inc(s.h_hi_rdy, 1)

    def act_program(act):
        steps = [0]

        def link(ins):
            steps[0] += 1
            ins.then_inc(s.act_step, 1)
            act.wait_ge(s.act_step, steps[0])

        def hi(slot, raw_count, done):
            act.wait_ge(s.raw0 if slot == 0 else s.raw1, raw_count)
            if done is not None:
                act.wait_ge(s.unit_done, done)
            A.activation(whi[:, slot, :], raw[:, slot, :], ACT.Copy).then_inc(s.hi_done, 1)

        def hi_u(u):
            if u < NUNITS:
                hi(u % 2, 16 * (u // 2 + 1), u - 1 if u >= 2 else None)

        def square(n, k, src):
            i = SQ_BASE[n] + k
            if i >= 4:
                act.wait_ge(s.stat_mm, i - 3)
            A.activation(scr[:, i % 4, :], src, ACT.Square).then_inc(s.sq_ready, 1)

        def root(n, bank, width):
            act.wait_ge(s.stat_mm, SQ_BASE[n] + NORM_TILES[n])
            if n:
                act.wait_ge(s.norm_r, n)
            A.activation(sd[:, 0:TB], psum[:, bank, 0:TB], ACT.Sqrt, bias=eps, scale=1.0 / width).then_inc(s.norm_sd, 1)

        def h_part(n_apply, k):
            act.wait_ge(s.h_f, n_apply + 1)
            A.activation(h_hi[:, k, :], scr[:, n_apply % 4, :], ACT.Copy).then_inc(s.h_hi_rdy, 1)

        def norm_of_x(n, upd, apply0):
            for k in range(KD):
                if upd:
                    act.wait_ge(s.x_upd, KD * (upd - 1) + k + 1)
                elif k % 2 == 0:
                    act.wait_ge(s.in_x[k // 2], 16)
                square(n, k, x[:, k, :])
            root(n, 7, D)
            if n == N_FFN1:
                hi_u(0)
            for k in range(KD):
                h_part(apply0 + k, k)
            if n == N_FFN1:
                hi_u(1)

        def ffn(f):
            u0 = ubase(f)
            n_post = (N_FFN1P, N_FFN2P)[f]
            with act.Fori(0, UP_STEPS) as i:
                act.wait_ge(s.unit_done, 2 * i + (u0 + 1))
                act.wait_ge(s.act_f, i + (UP_STEPS * f + 1))
                A.activation(scr[:, 0:2, :], psum[:, 0:2, :], ACT.Silu).then_inc(s.silu_done, 1)
                hi(u0 % 2, 16 * i + 16 * ((u0 + 2) // 2 + 1), None)
                act.wait_ge(s.act_f, i + (UP_STEPS * f + 2))
                A.activation(act_hi[:, bass.ds(2 * i, 2), :], scr[:, 2:4, :], ACT.Copy).then_inc(s.act_hi_rdy, 1)
                act.wait_ge(s.unit_done, 2 * i + (u0 + 2))
                hi((u0 + 1) % 2, 16 * i + 16 * ((u0 + 3) // 2 + 1), None)
            d0 = u0 + 2 * UP_STEPS
            if f == 1:
                act.dma_start(b.p_raw[:, :, :], p_in[bass.ds(layer, 1)].rearrange("a p t n -> (a p) t n")
                              ).then_inc(s.p_in, 16)
            with act.Fori(0, 5) as i:
                for j in range(2):
                    act.wait_ge(s.unit_done, 2 * i + (d0 + j + 1))
                    hi((d0 + j) % 2, 16 * i + 16 * ((d0 + 2 + j) // 2 + 1), None)
            if f == 1:
                act.wait_ge(s.p_in, 16)
                A.activation(b.p_hi[:, :, :], b.p_raw[:, :, :], ACT.Copy).then_inc(s.p_hi, 1)
            for d in range(KD):
                act.wait_ge(s.down_d, KD * f + d + 1)
                square(n_post, d, psum[:, d, :])
                A.activation(y_ffn[:, d, :], psum[:, d, :], ACT.Copy,
                             scale=vec(("ffn1_post", "ffn2_post")[f], d)).then_inc(s.y_evac, 1)
            hi_u(d0 + DOWN + 1)
            root(n_post, 0, D)

        act.sem_inc(s.silu_done, 1)

        def lru_gates(j):
            for g, (dst, bias) in enumerate(((b.gr, "ba"), (b.gi, "bx"))):
                act.wait_ge(s.lru_mm, 2 * j + g + 1)
                if j:
                    act.wait_ge(s.lru_y, 1)
                A.activation(dst[:, :], psum[:, 4 + g, :], ACT.Sigmoid, bias=vec(bias, j)).then_inc(s.lru_gt, 1)
            act.wait_ge(s.lam_sp, 1)
            act.wait_ge(s.lru_gt, 2 * j + 2)
            A.activation(b.la[:, :], b.gr[:, :], ACT.Exp, scale=la8n[:, j:j + 1]).then_inc(s.lru_a, 1)
            A.activation(b.lth[:, :], b.gr[:, :], ACT.Tanh, scale=la8p[:, j:j + 1]).then_inc(s.lru_a, 1)
            act.wait_ge(s.lru_a, 3 * j + 2)
            A.activation(b.gr[:, :], b.la[:, :], ACT.Square).then_inc(s.lru_a, 1)

        def lru_roots(j):
            act.wait_ge(s.lru_t, j + 1)
            A.activation(b.gr[:, :], b.gr[:, :], ACT.Sqrt).then_inc(s.lru_s, 1)
            act.wait_ge(s.lru_poly, j + 1)
            A.activation(b.lth[:, :], b.lth[:, :], ACT.Tanh, scale=float(np.sqrt(2 / np.pi))).then_inc(s.lru_th, 1)
        norm_of_x(N_FFN1, 0, 0)
        act.wait_ge(s.small_in, 16)
        A.activation(b.wf_hi[:, :], mat("wf", 0, 32), ACT.Copy).then_inc(s.wf_rdy, 1)
        link(A.activation(lam_t[0], vec("lam", 0, 2), ACT.Abs))
        A.activation(lam_t[1], lam_t[0], ACT.Exp, scale=-1.0).then_inc(s.lam_e, 1)
        ffn(0)
        norm_of_x(N_MIX, 1, 8)
        rwkv = act_rwkv(act)
        for m, name in enumerate(MIX_UNITS):
            u = U_MIX + m
            act.wait_ge(s.unit_done, u + 1)
            bank = 2 * (m % 2)
            two = psum[:, bank:bank + 2, :]
            if name in ("wag", "k", "r", "v"):
                A.activation(z[:, 2 * m:2 * m + 2, 1:1 + SEQ], two, ACT.Copy).then_inc(s.tile_evac, 2)
            elif name == "lx":
                A.activation(lx[:, :, 3:3 + SEQ], two, ACT.Copy).then_inc(s.tile_evac, 2)
            elif name == "fq":
                A.activation(fq[:, :, :], two, ACT.Copy, scale=HD ** -0.5).then_inc(s.tile_evac, 2)
            elif name == "sq":
                A.activation(sq[:, :, :], two, ACT.Copy, scale=HD ** -0.5).then_inc(s.tile_evac, 2)
            elif name == "skv":
                A.activation(sk[:, :], psum[:, bank, :], ACT.Copy).then_inc(s.tile_evac, 1)
                A.activation(sv[:, :, :].rearrange("p t n -> p (t n)"), psum[:, bank + 1, :], ACT.Copy
                             ).then_inc(s.tile_evac, 1)
            else:
                dst = {"lg": lg, "fk": fk}.get(name)
                dst = dst[:, :, :] if dst is not None else fv[:, :, :].rearrange("p (a t) n -> p a (t n)", a=2)
                A.activation(dst, two, ACT.Copy).then_inc(s.tile_evac, 2)
            hi_u(u + 2)
            if m == 2:
                act.wait_ge(s.z_mixed, 2)
                A.activation(z[0:64, 0, 1:1 + SEQ], z[0:64, 0, 1:1 + SEQ], ACT.Tanh).then_inc(s.rw_tanh, 1)
                A.activation(z[:, 1, 1:1 + SEQ], z[:, 1, 1:1 + SEQ], ACT.Sigmoid).then_inc(s.rw_tanh, 1)
            if m == 4 or m == 5 or m == 7 or m == 8:
                next(rwkv)
            if m == 6 or m == 9:
                lru_gates(0 if m == 6 else 1)
            if m == 7 or m == 10:
                lru_roots(0 if m == 7 else 1)
        act.wait_ge(s.f_y, 1)
        link(A.activation(f_e, f_y, ACT.Abs))
        link(A.activation(f_e, f_e, ACT.Exp, scale=-1.0))
        A.activation(f_e, f_e, ACT.Ln, bias=one).then_inc(s.f_ln, 1)
        turns = {"R": rwkv, "T": act_attention(act), "G": act_groups(act)}
        for turn in MERGE:
            next(turns[turn])
        act.wait_ge(s.rw_done, 2)
        for j in range(2):
            A.activation(b.gsq[:, j, :], YG[2](j), ACT.Square).then_inc(s.grp_sq, 1)
        act.wait_ge(s.grp_mm, 2)
        A.activation(sd[:, 12:16], psum[:, 3, 12:16], ACT.Sqrt, bias=eps, scale=1.0 / GW).then_inc(s.grp_sd, 1)
        for j in range(2):
            group_hi(act, 6 + j, 4 + j)
        for m in range(4):
            u = U_OUT + m
            act.wait_ge(s.unit_done, u + 1)
            for j in range(2):
                d = 2 * m + j
                bank = 2 * (m % 2) + j
                square(N_MIXP, d, psum[:, bank, :])
                A.activation(y_mix[:, d, :], psum[:, bank, :], ACT.Copy, scale=vec("mix_post", d)).then_inc(s.y_evac, 1)
            hi_u(u + 2)
        root(N_MIXP, 7, D)
        norm_of_x(N_FFN2, 2, 24)
        ffn(1)
        for d in range(KD + 2):
            if d < KD:
                act.wait_ge(s.pt_mm, d + 1)
                A.activation(y_mix[:, d, :], psum[:, 2 + d % 4, :], ACT.Copy).then_inc(s.y_evac, 1)
            if d >= 2:
                act.wait_ge(s.x_upd, 2 * KD + d - 1)
                square(N_PE, d - 2, x[:, d - 2, :])
        root(N_PE, 7, D)
        for k in range(KD):
            h_part(32 + k, k)
        hi_u(U_WP + 2)
        for m in range(4):
            u = U_WG + m
            act.wait_ge(s.unit_done, u + 1)
            if m < 2:
                for k in range(4 * m, 4 * m + 4):
                    act.wait_ge(s.y_evac, Y_BASE[N_PEP] + k + 1)
                    square(N_PEP, k, y_mix[:, k, :])
            for j in range(2):
                A.activation(gate[:, 2 * m + j, :], psum[:, 2 * (m % 2) + j, :], ACT.Sigmoid).then_inc(s.gate_rdy, 1)
            hi_u(u + 2)
            if m == 1:
                root(N_PEP, 7, D)

    def dve_attention(dve, link):
        dve.wait_ge(s.c_mm, 1)
        V.tensor_copy(ctok, psum[:, 3, 0:16]).then_inc(s.c_rdy, 1)
        dve.wait_ge(s.c_rdy, 1)
        yield
        yield

        def top(n):
            kind, h, i = n // 16, (n // 4) % 4, n % 4
            w = (i + 1) * P if kind == 0 else min(i + 1, 2) * P
            dst = b.prob[:, n % 3, 0:w]
            dve.wait_ge(s.at_s, n + 1)
            if n >= 3:
                dve.wait_ge(s.at_tr, n - 2)
            elif n == 0:
                dve.wait_ge(s.cb_rdy, 4)
            if kind == 0:
                V.scalar_tensor_tensor(dst, psum[:, n % 2, 0:w], ctok[:, i * NH + h:i * NH + h + 1], key_sum[h][:, 0:w],
                                       ALU.add, ALU.add).then_inc(s.at_sc, 1)
            else:
                V.tensor_tensor(dst, psum[:, n % 2, 0:w], con("band", 2 * P - w, w), ALU.add).then_inc(s.at_sc, 1)
            dve.wait_ge(s.at_sc, n + 1)
            i = V.tensor_reduce(nmax[:, n % 4:n % 4 + 1], dst, AX.X, ALU.max, negate=True)
            if kind == 1:
                link(i)
                i = V.tensor_tensor(nmax[:, n % 4:n % 4 + 1], nmax[:, n % 4:n % 4 + 1], nsink[:, h:h + 1], ALU.min)
            i.then_inc(s.at_max, 1)

        def share(n):
            kind, h, i = n // 16, (n // 4) % 4, n % 4
            w = (i + 1) * P if kind == 0 else min(i + 1, 2) * P
            dve.wait_ge(s.at_exp, n + 1)
            if kind == 1:
                link(V.tensor_tensor(rsum[:, n:n + 1], rsum[:, n:n + 1], esink[:, n % 4:n % 4 + 1], ALU.add))
            link(V.reciprocal(rinv_a[:, n:n + 1], rsum[:, n:n + 1]))
            V.tensor_scalar(b.prob[:, n % 3, 0:w], b.prob[:, n % 3, 0:w], rinv_a[:, n:n + 1], None, ALU.mult
                            ).then_inc(s.at_p, 1)

        for n in range(ATT_UNITS + 4):
            if n % 8 == 3 and n > 3:
                pair = n // 8 - 1
                dve.wait_ge(s.at_pv, 8 * (pair + 1))
                V.tensor_copy((fq if pair < 2 else fk)[:, pair % 2, :], psum[:, 3, :]).then_inc(s.at_y, 1)
            if 2 <= n < ATT_UNITS + 2:
                share(n - 2)
            if n < ATT_UNITS:
                top(n)
            yield

    def dve_rwkv(dve, link):
        for p in range(2):
            k_, r_, v_ = (z[:, 2 * m + p, 1:1 + SEQ] for m in (1, 2, 3))
            V.tensor_scalar(b.kr[:, 0, :], k_, vec("kk", p), None, ALU.mult).then_inc(s.rw_kkr, 1)
            if p == 0:
                yield
            dve.wait_ge(s.rw_gates, 3 * p + 1)
            link(V.tensor_tensor_scan(b.e1[:, :], con("reset", 0, SEQ), b.e3[:, :], 0.0, ALU.mult, ALU.add))
            V.tensor_tensor(b.e3[:, :], b.e1[:, :], b.e3[:, :], ALU.subtract).then_inc(s.rw_cum, 1)
            dve.wait_ge(s.rw_gates, 3 * p + 2)
            link(V.tensor_scalar(b.kg[:, :], b.bg[:, :], vec("ka", p), kam1[:, p:p + 1], ALU.mult, ALU.add))
            link(V.tensor_tensor(b.kg[:, :], b.kg[:, :], k_, ALU.mult))
            link(V.scalar_tensor_tensor(scr[:, 1, :], r_, vec("rk", p), b.kg[:, :], ALU.mult, ALU.mult))
            yield
            dve.wait_ge(s.rw_nrm, p + 1)
            link(V.tensor_scalar(knorm, knorm, 1e-12, None, ALU.max))
            V.reciprocal(knorm, knorm).then_inc(s.rw_kn, 1)
            yield
            dve.wait_ge(s.rw_knb, p + 1)
            link(V.tensor_tensor(b.kr[:, 0, :], b.kr[:, 0, :], psum[:, 7, :], ALU.mult))
            link(V.tensor_tensor(b.bg[:, :], b.kr[:, 0, :], b.bg[:, :], ALU.mult))
            dve.wait_ge(s.rw_E, 3 * (p + 1))
            link(V.tensor_tensor(b.bg[:, :], b.bg[:, :], b.e2[:, :], ALU.mult))
            link(V.tensor_tensor(b.kg[:, :], b.kg[:, :], b.e2[:, :], ALU.mult))
            link(V.scalar_tensor_tensor(b.kr[:, 0, :], b.kr[:, 0, :], -1.0, b.e3[:, :], ALU.mult, ALU.mult))
            V.tensor_tensor(b.kr[:, 1, :], r_, b.e1[:, :], ALU.mult).then_inc(s.rw_ops, 1)
            dve.wait_ge(s.rw_bonus, p + 1)
            V.tensor_tensor(b.bon[:, :], psum[:, 6, :], v_, ALU.mult).then_inc(s.rw_bon, 1)
            yield
            yield
            if p == 0:
                dve.wait_ge(s.f_mm, 1)
            for q in range(8):
                dve.wait_ge(s.rw_A, 8 * p + q + 1)
                V.tensor_tensor(b.am[:, q, :, :].rearrange("p g n -> p (g n)"), psum[:, 4 + q % 4, :],
                                con("mask4", 0, 4 * P), ALU.mult).then_inc(s.rw_am, 1)
            dve.wait_ge(s.rw_am, 8 * (p + 1))

            def level(l):
                V.tensor_tensor(b.xl[:, :, :], b.am[:, :, 0, :],
                                con("level", l * P)[:, None, :].broadcast_to([P, 8, P]), ALU.mult).then_inc(s.rw_xl, 1)
            level(0)
            yield
            dve.wait_ge(s.rw_xl, 6 * p + 1)
            halves = [slice(4 * half, 4 * half + 4) for half in range(2)]
            ones4 = ident[:, None, :].broadcast_to([P, 4, P])
            for h4 in halves:
                V.tensor_tensor(b.wm[:, h4, :], b.xl[:, h4, :], ones4, ALU.add).then_inc(s.rw_updw, 1)
            dve.wait_ge(s.rw_TP, 12 * p + 2)
            dve.wait_ge(s.rw_updw, 12 * p + 2)
            level(1)
            for half, h4 in enumerate(halves):
                V.tensor_tensor(b.tm[:, h4, :], psum[:, 5 + 2 * half, :].rearrange("p (q n) -> p q n", q=4), ones4,
                                ALU.add).then_inc(s.rw_updt, 1)
            dve.wait_ge(s.rw_updt, 10 * p + 2)
            yield
            for l in range(1, 6):
                if l < 5:
                    dve.wait_ge(s.rw_P, 2 * (5 * p + l))
                    level(l + 1)
                for half in range(2):
                    dve.wait_ge(s.rw_TP, 2 * (6 * p + l) + half + 1)
                    w_, t_ = (m[:, 4 * half:4 * half + 4, :].rearrange("p q n -> p (q n)") for m in (b.wm, b.tm))
                    V.tensor_tensor(w_, w_, psum[:, 4 + 2 * half, :], ALU.add).then_inc(s.rw_updw, 1)
                    if l < 5:
                        V.tensor_tensor(t_, t_, psum[:, 5 + 2 * half, :], ALU.add).then_inc(s.rw_updt, 1)
                dve.wait_ge(s.rw_updw, 12 * p + 2 * (l + 1))
                dve.wait_ge(s.rw_updt, 10 * p + 2 * min(l + 1, 5))
                yield
            yield
            V.memset(b.st[:, 0, :], 0.0).then_inc(s.rw_s, 1)
            yield
            dve.wait_ge(s.rw_vpE, p + 1)
            for cc in range(NCH):
                r, t = slice(64 * (cc % 2), 64 * (cc % 2) + 64), cc // 2
                dve.wait_ge(s.rw_u, 8 * p + cc + 1)
                V.tensor_tensor(b.us[r, 2 * t:2 * t + 2, :], psum[r, 4:8:2, 0:HD], b.vp[r, 2 * t:2 * t + 2, :], ALU.add
                                ).then_inc(s.rw_usb, 1)
                yield
                if cc < NCH - 1:
                    dve.wait_ge(s.rw_x, 7 * p + cc + 1)
                    dve.wait_ge(s.rw_s, 8 * p + cc + 1)
                    link(V.tensor_tensor(b.st[:, cc + 1, :], psum[:, 5, 0:HD], b.st[:, cc, :], ALU.add))
                    last = (cc + 1) * CH - 1
                    V.tensor_scalar(b.st[:, cc + 1, :], b.st[:, cc + 1, :], b.e1[:, last:last + 1], None, ALU.mult
                                    ).then_inc(s.rw_s, 1)
                    yield
            yield
            dve.wait_ge(s.rw_mean, p + 1)
            V.scalar_tensor_tensor(b.ym[:, :], psum[:, 4, :], -1.0 / HD, b.yr[:, :], ALU.mult, ALU.add
                                   ).then_inc(s.rw_ym, 1)
            yield
            dve.wait_ge(s.rw_sd, p + 1)
            V.reciprocal(gnorm, gnorm).then_inc(s.rw_gs, 1)
            dve.wait_ge(s.rw_ym, p + 1)
            dve.wait_ge(s.rw_gsb, p + 1)
            link(V.tensor_tensor(b.ym[:, :], b.ym[:, :], psum[:, 4, :], ALU.mult))
            link(V.tensor_scalar(b.ym[:, :], b.ym[:, :], vec("ln_g", p), vec("ln_b", p), ALU.mult, ALU.add))
            dve.wait_ge(s.rw_bon, p + 1)
            link(V.tensor_tensor(b.ym[:, :], b.ym[:, :], b.bon[:, :], ALU.add))
            V.tensor_tensor(r_, b.ym[:, :], b.gg[:, :], ALU.mult).then_inc(s.rw_done, 1)
            dve.wait_ge(s.rw_done, p + 1)
            yield

    def group_lo(dve, i, k):
        dve.wait_ge(s.h_hi_rdy, 16 + i + 1)
        V.tensor_tensor(h_lo[:, k, :], YG[k // 2](k % 2), h_hi[:, k, :], ALU.subtract).then_inc(s.h_rdy, 1)

    def dve_groups(dve):
        yield
        dve.wait_ge(s.grp_sd, 1)
        V.reciprocal(rinv[:, 0:12], sd[:, 0:12]).then_inc(s.grp_r, 1)
        yield
        for i, k in enumerate(SPLIT_ORDER[:6]):
            dve.wait_ge(s.grp_rstd, i // 2 + 1)
            V.scalar_tensor_tensor(YG[k // 2](k % 2), YG[k // 2](k % 2), vec("grp_gain", k), psum[:, i // 2, :],
                                   ALU.mult, ALU.mult).then_inc(s.h_f, 1)
        yield
        for i, k in enumerate(SPLIT_ORDER[:6]):
            group_lo(dve, i, k)
        yield

    def dve_program(dve):
        steps = [0]

        def link(ins):
            steps[0] += 1
            ins.then_inc(s.dve_step, 1)
            dve.wait_ge(s.dve_step, steps[0])

        def invert(n):
            dve.wait_ge(s.norm_sd, n + 1)
            if n:
                dve.wait_ge(s.norm_rstd, n)
            V.reciprocal(rinv[:, 0:TB], sd[:, 0:TB]).then_inc(s.norm_r, 1)

        def apply(n, tiles, bank, apply0, gain):
            dve.wait_ge(s.norm_rstd, n + 1)
            cnt = len(tiles)
            for k in range(cnt + 1):
                if k < cnt:
                    src, g, _ = tiles[k]
                    i = V.scalar_tensor_tensor(scr[:, (apply0 + k) % 4, :], src, g, psum[:, bank, :], ALU.mult, ALU.mult)
                    i.then_inc(s.h_f, 1)
                    if k == cnt - 1:
                        dve.wait_ge(s.h_f, apply0 + cnt)
                        dve.sem_inc(s.rstd_used, 1)
                if k >= 1:
                    dst = tiles[k - 1][2]
                    dve.wait_ge(s.h_hi_rdy, apply0 + k)
                    V.tensor_tensor(h_lo[:, dst, :], scr[:, (apply0 + k - 1) % 4, :], h_hi[:, dst, :], ALU.subtract
                                    ).then_inc(s.h_rdy, 1)

        def apply_x(n, apply0, gain):
            apply(n, [(x[:, k, :], vec(gain, k), k) for k in range(KD)], 6, apply0, gain)

        def residual(n, y, bank, half, upd):
            dve.wait_ge(s.y_evac, Y_BASE[n] + KD)
            dve.wait_ge(s.norm_rstd, n + 1)
            for k in range(KD + 1):
                if k < KD:
                    V.scalar_tensor_tensor(y[:, k, :], y[:, k, :], 0.5 if half else 1.0, psum[:, bank, :],
                                           ALU.mult, ALU.mult).then_inc(s.dve_step, 1)
                if k >= 1:
                    dve.wait_ge(s.dve_step, steps[0] + k)
                    if k == KD:
                        dve.sem_inc(s.rstd_used, 1)
                    V.tensor_tensor(x[:, k - 1, :], x[:, k - 1, :], y[:, k - 1, :], ALU.add).then_inc(s.x_upd, 1)
            steps[0] += KD
            dve.wait_ge(s.x_upd, upd * KD)

        def ffn(f):
            with dve.Fori(0, UP_STEPS) as i:
                dve.wait_ge(s.silu_done, i + (UP_STEPS * f + 2))
                dve.wait_ge(s.unit_done, 2 * i + (ubase(f) + 2))
                dve.wait_ge(s.act_rdy, i + (UP_STEPS * f + 1))
                V.tensor_tensor(scr[:, 2:4, :], scr[:, 0:2, :], psum[:, 2:4, :], ALU.mult).then_inc(s.act_f, 1)
                dve.wait_ge(s.act_hi_rdy, i + (UP_STEPS * f + 1))
                V.tensor_tensor(act_lo[:, bass.ds(2 * i, 2), :], scr[:, 2:4, :], act_hi[:, bass.ds(2 * i, 2), :],
                                ALU.subtract).then_inc(s.act_rdy, 1)

        dve.sem_inc(s.act_f, 1)
        dve.sem_inc(s.act_rdy, 1)
        def convolve(j):
            dve.wait_ge(s.tile_evac, 10)
            link(V.tensor_scalar(b.xc[:, :], lx[:, j, 0:SEQ], vec("conv_w", j), vec("conv_b", j), ALU.mult, ALU.add))
            for t in range(1, 4):
                i = V.scalar_tensor_tensor(b.xc[:, :], lx[:, j, t:t + SEQ], vec("conv_w", 2 * t + j), b.xc[:, :],
                                           ALU.mult, ALU.add)
                if t < 3:
                    link(i)
                else:
                    i.then_inc(s.lru_xc, 1)

        def lru_product(j):
            dve.wait_ge(s.lru_a, 3 * j + 3)
            V.scalar_tensor_tensor(b.gr[:, :], b.gr[:, :], 1.0, b.lth[:, :], ALU.add, ALU.mult).then_inc(s.lru_t, 1)
            dve.wait_ge(s.lru_xc, j + 1)
            link(V.tensor_tensor(b.gi[:, :], b.gi[:, :], b.xc[:, :], ALU.mult))
            dve.wait_ge(s.lru_t, j + 1)
            link(V.tensor_tensor(b.lth[:, :], lg[:, j, :], lg[:, j, :], ALU.mult))
            link(V.tensor_scalar(b.lth[:, :], b.lth[:, :], 0.044715, 1.0, ALU.mult, ALU.add))
            V.tensor_tensor(b.lth[:, :], b.lth[:, :], lg[:, j, :], ALU.mult).then_inc(s.lru_poly, 1)

        def lru_output(j):
            dve.wait_ge(s.lru_s, j + 1)
            link(V.tensor_tensor(b.gi[:, :], b.gi[:, :], b.gr[:, :], ALU.mult))
            link(V.tensor_tensor_scan(b.xc[:, :], b.la[:, :], b.gi[:, :], 0.0, ALU.mult, ALU.add))
            dve.wait_ge(s.lru_th, j + 1)
            link(V.scalar_tensor_tensor(b.lth[:, :], b.lth[:, :], 1.0, lg[:, j, :], ALU.add, ALU.mult))
            V.scalar_tensor_tensor(lx[:, j, 3:3 + SEQ], b.xc[:, :], 0.5, b.lth[:, :], ALU.mult, ALU.mult
                                   ).then_inc(s.lru_y, 1)
            dve.wait_ge(s.lru_y, j + 1)

        invert(N_FFN1)
        dve.wait_ge(s.small_in, 16)
        apply_x(N_FFN1, 0, "ffn1_pre")
        dve.wait_ge(s.wf_rdy, 1)
        V.tensor_tensor(b.wf_lo[:, :], mat("wf", 0, 32), b.wf_hi[:, :], ALU.subtract).then_inc(s.wf_rdy, 1)
        dve.wait_ge(s.lam_e, 1)
        e, w, w2, acc = lam_t[1], lam_t[2], lam_t[3], lam_t[4]
        link(V.tensor_scalar(w, e, 2.0, None, ALU.add))
        link(V.reciprocal(w2, w))
        link(V.tensor_tensor(w, w2, e, ALU.mult))
        link(V.tensor_tensor(w2, w, w, ALU.mult))
        link(V.memset(acc, 1.0 / 19))
        for n in range(17, 0, -2):
            link(V.tensor_tensor(acc, acc, w2, ALU.mult))
            link(V.tensor_scalar(acc, acc, 1.0 / n, None, ALU.add))
        link(V.tensor_tensor(acc, acc, w, ALU.mult))
        link(V.tensor_scalar(w, vec("lam", 0, 2), -1.0, 0.0, ALU.mult, ALU.max))
        link(V.scalar_tensor_tensor(acc, acc, 2.0, w, ALU.mult, ALU.add))
        link(V.tensor_scalar(la8n, acc, -8.0, None, ALU.mult))
        V.tensor_scalar(la8p, acc, 8.0, None, ALU.mult).then_inc(s.lam_sp, 1)
        link(V.tensor_scalar(nsink, vec("sink", 0, 4), -1.0, None, ALU.mult))
        link(V.tensor_scalar(kam1, vec("ka", 0, 2), -1.0, 1.0, ALU.mult, ALU.add))
        ffn(0)
        invert(N_FFN1P)
        residual(N_FFN1P, y_ffn, 1, True, 1)
        invert(N_MIX)
        apply_x(N_MIX, 8, "mix_pre")
        dve.wait_ge(s.down_d, KD)
        link(V.memset(z[:, :, 0:1], 0.0))
        link(V.memset(lx[:, :, 0:3], 0.0))
        for m in range(4):
            dve.wait_ge(s.tile_evac, 2 * (m + 1))
            link(V.tensor_tensor(scr[:, 2:4, :], z[:, 2 * m:2 * m + 2, 0:SEQ], z[:, 2 * m:2 * m + 2, 1:1 + SEQ],
                                 ALU.subtract))
            for j in range(2):
                V.scalar_tensor_tensor(z[:, 2 * m + j, 1:1 + SEQ], scr[:, 2 + j, :], vec("mu", 2 * m + j),
                                       z[:, 2 * m + j, 1:1 + SEQ], ALU.mult, ALU.add).then_inc(s.z_mixed, 1)
            dve.wait_ge(s.z_mixed, 2 * (m + 1))
        rwkv = dve_rwkv(dve, link)
        next(rwkv)
        convolve(0)
        next(rwkv)
        next(rwkv)
        lru_product(0)
        next(rwkv)
        lru_output(0)
        next(rwkv)
        convolve(1)
        lru_product(1)
        lru_output(1)
        dve.wait_ge(s.f_mm, 1)
        V.tensor_copy(b.probT[0:NH, 0, :], psum[0:NH, 7, :]).then_inc(s.f_t, 1)
        dve.wait_ge(s.f_tr, 1)
        V.tensor_tensor(f_y, psum[:, 7, 0:16], vec("fb", 0, 16), ALU.add).then_inc(s.f_y, 1)
        dve.wait_ge(s.f_ln, 1)
        V.scalar_tensor_tensor(f_l, f_y, 0.0, f_e, ALU.min, ALU.subtract).then_inc(s.f_lf, 1)
        turns = {"R": rwkv, "T": dve_attention(dve, link), "G": dve_groups(dve)}
        for turn in MERGE:
            next(turns[turn])
        dve.wait_ge(s.grp_sd, 2)
        V.reciprocal(rinv[:, 12:16], sd[:, 12:16]).then_inc(s.grp_r, 1)
        dve.wait_ge(s.grp_rstd, 4)
        for j in range(2):
            V.scalar_tensor_tensor(YG[2](j), YG[2](j), vec("grp_gain", 4 + j), psum[:, 6, :], ALU.mult, ALU.mult
                                   ).then_inc(s.h_f, 1)
        for j in range(2):
            group_lo(dve, 6 + j, 4 + j)
        invert(N_MIXP)
        residual(N_MIXP, y_mix, 6, False, 2)
        invert(N_FFN2)
        apply_x(N_FFN2, 24, "ffn2_pre")
        ffn(1)
        dve.wait_ge(s.p_hi, 1)
        V.tensor_tensor(b.p_lo[:, :, :], b.p_raw[:, :, :], b.p_hi[:, :, :], ALU.subtract).then_inc(s.p_rdy, 1)
        invert(N_FFN2P)
        residual(N_FFN2P, y_ffn, 1, True, 3)
        invert(N_PE)
        apply_x(N_PE, 32, "pe_pre")
        invert(N_PEP)
        dve.wait_ge(s.norm_rstd, N_PEP + 1)
        for k in range(KD):
            V.scalar_tensor_tensor(y_mix[:, k, :], y_mix[:, k, :], vec("pe_post", k), psum[:, 6, :], ALU.mult, ALU.mult
                                   ).then_inc(s.dve_step, 1)
        steps[0] += KD
        dve.wait_ge(s.dve_step, steps[0])
        for k in range(KD + 1):
            if k < KD:
                dve.wait_ge(s.gate_rdy, k + 1)
                V.tensor_tensor(y_mix[:, k, :], y_mix[:, k, :], gate[:, k, :], ALU.mult).then_inc(s.dve_step, 1)
            if k >= 1:
                dve.wait_ge(s.dve_step, steps[0] + k)
                V.tensor_tensor(x[:, k - 1, :], x[:, k - 1, :], y_mix[:, k - 1, :], ALU.add).then_inc(s.x_upd, 1)

    with nc.Block() as block:
        @block.sync
        def _(sp):
            sp_program(sp)

        @block.gpsimd
        def _(pool):
            pool_program(pool)

        @block.tensor
        def _(pe):
            pe_program(pe)

        @block.scalar
        def _(act):
            act_program(act)

        @block.vector
        def _(dve):
            dve_program(dve)


def kernel(**inputs):
    import numpy as _np
    import concourse.bacc as _bacc
    from concourse import mybir as _mybir
    from concourse.bass_utils import run_bass_kernel_spmd as _run
    a = {k: _np.asarray(v) for k, v in inputs.items()}

    def cols(w, lo, n=GW):
        return w[:, lo:lo + n].reshape(KD, P, n).transpose(1, 0, 2).reshape(P, KD * n)

    def ffn_units(wg, wu, wd):
        for i in range(UP_STEPS):
            yield cols(wg, i * GW)
            yield cols(wu, i * GW)
        for m in range(DOWN):
            yield wd[2 * m * P:2 * (m + 1) * P].reshape(2, P, D).transpose(1, 0, 2).reshape(P, UNIT)

    off = {"lx": 0, "lg": 256, "fq": 512, "fk": 768, "fv": 1024, "r": 1284, "k": 1540, "v": 1796,
           "wag": 2052, "sq": 2308, "skv": 2564}
    units = _np.empty((DEPTH, NUNITS, P, UNIT), _np.float32)
    small = _np.zeros((DEPTH, P, NSMALL), _np.float32)
    for l in range(DEPTH):
        w_in = a["w_in"][l]
        todo = list(ffn_units(a["ffn1_wg"][l], a["ffn1_wu"][l], a["ffn1_wd"][l]))
        for name in MIX_UNITS:
            if name == "sq":
                w = w_in[:, 2308:2564].reshape(D, NH, HD)[:, [0, 2, 1, 3]].reshape(D, GW)
                todo.append(cols(w, 0))
            else:
                todo.append(cols(w_in, off[name]))
        todo += [cols(a["w_out"][l], m * GW) for m in range(4)]
        todo += list(ffn_units(a["ffn2_wg"][l], a["ffn2_wu"][l], a["ffn2_wd"][l]))
        todo.append(a["pe_wp"][l].reshape(2, P, D).transpose(1, 0, 2).reshape(P, UNIT))
        todo += [cols(a["pe_wg"][l], m * GW) for m in range(4)]
        for u, t in enumerate(todo):
            units[l, u] = t

        def put(name, v):
            v = _np.asarray(v).reshape(-1, P).T
            small[l, :, VEC[name]:VEC[name] + v.shape[1]] = v
        for name in ("ffn1_pre", "ffn1_post", "mix_pre", "mix_post", "grp_gain", "ffn2_pre", "ffn2_post",
                     "pe_pre", "pe_post"):
            put(name, a[name][l])
        put("conv_w", a["lru_conv_w"][l])
        put("conv_b", a["lru_conv_b"][l])
        put("ba", a["lru_ba"][l])
        put("bx", a["lru_bx"][l])
        put("lam", a["lru_lambda"][l])
        mu = a["rw_mu"][l]
        put("mu", _np.concatenate([mu[768:1024], mu[256:512], mu[0:256], mu[512:768]]))
        for name in ("w0", "a0", "kk", "ka", "rk", "ln_g", "ln_b"):
            put(name, a["rw_" + name][l])
        small[l, :, VEC["fb"]:VEC["fb"] + 16] = _np.tile(a["fox_fb"][l], 4)[None]
        small[l, :, VEC["sink"]:VEC["sink"] + 4] = a["sw_sinks"][l][None]
        for h in range(NH):
            r, c = HD * (h % 2), P * (h // 2) + HD * (h % 2)
            small[l, r:r + HD, SM["bda"] + c:SM["bda"] + c + HD] = a["lru_wa"][l, h]
            small[l, r:r + HD, SM["bdx"] + c:SM["bdx"] + c + HD] = a["lru_wx"][l, h]
        small[l, 0:64, SM["wa2"]:SM["wa2"] + GW] = a["rw_w2"][l]
        small[l, 64:128, SM["wa2"]:SM["wa2"] + GW] = a["rw_a2"][l]
        small[l, :, SM["g2"]:SM["g2"] + GW] = a["rw_g2"][l]
        small[l, :, SM["wf"]:SM["wf"] + 32] = cols(w_in, 1280, NH)

    nc = _bacc.Bacc("TRN2", target_bir_lowering=False, num_devices=1)
    def feature_major(v, tiles):
        v = v.reshape(-1, SEQ, tiles, P).transpose(0, 3, 2, 1)
        return _np.ascontiguousarray(v)

    arrays = {"x_in": feature_major(a["x"], KD)[0], "p_in": feature_major(a["p"], DPLE // P),
              "units_in": units, "small_in_t": small, "consts_in": host_constants()}
    args = [nc.dram_tensor(n, v.shape, _mybir.dt.from_np(v.dtype), kind="ExternalInput").ap()
            for n, v in arrays.items()]
    args.append(nc.dram_tensor("out_0", (P, KD, SEQ), F32, kind="ExternalOutput").ap())
    build(nc, *args)
    r = _run(nc, [arrays], core_ids=[0])
    out = r.results[0]["out_0"].reshape(P, KD, SEQ)
    return _np.ascontiguousarray(out.transpose(2, 1, 0)).reshape(1, SEQ, D)
```

```python
from contextlib import ExitStack

import numpy as np
import concourse.bass as bass
from concourse import mybir

F32 = mybir.dt.float32
F32R = mybir.dt.float32r
ALU = mybir.AluOpType
ACT = mybir.ActivationFunctionType
AX = mybir.AxisListType

P = 128
SEQ = 512
TB = SEQ // P
D = 1024
KD = D // P
DFF = 2816
KF = DFF // P
DEPTH = 2
GW = 256
NH = 4
HD = 64
DPLE = 256
UNIT = 2048
UP_STEPS = KF // 2
DOWN = KF // 2
FFN_UNITS = 2 * UP_STEPS + DOWN
MIX_UNITS = ["wag", "k", "r", "v", "lx", "lg", "fq", "fk", "fv", "sq", "skv"]
U_FFN1 = 0
U_MIX = FFN_UNITS
U_OUT = U_MIX + len(MIX_UNITS)
U_FFN2 = U_OUT + 4
U_WP = U_FFN2 + FFN_UNITS
U_WG = U_WP + 1
NUNITS = U_WG + 4
EPS = 1e-6
GN_EPS = 64e-5
DECAY = float(np.exp(-0.5))
NEG = -1.0e30
CH = 64
NCH = SEQ // CH

VEC = {}
_at = 0
for _n, _w in (("ffn1_pre", 8), ("ffn1_post", 8), ("mix_pre", 8), ("mix_post", 8), ("grp_gain", 8),
               ("ffn2_pre", 8), ("ffn2_post", 8), ("pe_pre", 8), ("pe_post", 8), ("conv_w", 8),
               ("conv_b", 2), ("ba", 2), ("bx", 2), ("lam", 2), ("mu", 8), ("w0", 2), ("a0", 2),
               ("kk", 2), ("ka", 2), ("rk", 2), ("ln_g", 2), ("ln_b", 2), ("fb", 16), ("sink", 4)):
    VEC[_n] = _at
    _at += _w
NVEC = _at
SM = {}
for _n, _w in (("bda", 256), ("bdx", 256), ("wa2", 256), ("g2", 256), ("wf", 32)):
    SM[_n] = _at
    _at += _w
NSMALL = _at
CST = {}
_at = 0
for _n, _w in (("ident", 128), ("ones", 128), ("bones", 128), ("causal", 128), ("band", 256), ("tri", 128),
               ("cols", 4), ("mask4", 512), ("level", 6 * 128), ("reset", 512)):
    CST[_n] = _at
    _at += _w
NCST = _at
NCST_F32 = CST["mask4"]
N_FFN1, N_FFN1P, N_MIX, N_MIXP, N_FFN2, N_FFN2P, N_PE, N_PEP = range(8)
PRE = {N_FFN1: 0, N_MIX: 1, N_FFN2: 2, N_PE: 3}
POST = {N_FFN1P: 0, N_MIXP: 1, N_FFN2P: 2, N_PEP: 3}
POOL_TILES = (1, 3, 5)
Y_BASE = {N_FFN1P: 0, N_MIXP: 8, N_FFN2P: 16, N_PEP: 24}

LAYER_SEMS = ["small_in", "raw0", "raw1", "hi_done", "lo_done", "unit_done", "out_tile", "sq_ready", "stat_mm", "ysq_rdy", "ysq_sum", "stat_post", "norm_sd",
        "norm_r", "norm_rstd", "rstd_used", "h_f", "h_hi_rdy", "h_rdy", "x_upd", "x_pool", "y_scaled", "sq_pool", "sq_dve", "silu_done",
        "act_f", "act_hi_rdy", "act_rdy", "down_d", "y_evac", "dve_step", "act_step", "tile_evac",
        "wf_rdy", "f_mm", "f_t", "f_tr", "f_y", "f_ln", "f_lf", "c_mm", "c_rdy", "cb_mm", "cb_rdy",
        "lam_e", "lam_sp", "lru_xc", "lru_mm", "lru_gt", "lru_a", "lru_t", "lru_s", "lru_poly", "lru_th",
        "lru_y", "at_s", "at_sc", "at_max", "at_exp", "at_p", "at_tr", "at_pt", "at_pv",
        "at_y", "z_mixed", "rw_tanh", "rw_lora", "rw_gates", "rw_cum", "rw_E", "rw_kkr", "rw_sqk", "rw_ss",
        "rw_nrm", "rw_ops", "rw_bonus", "rw_tr", "rw_tok", "rw_bon", "rw_A", "rw_am", "rw_xl", "rw_P",
        "rw_Pe", "rw_TP", "rw_WP", "rw_updw", "rw_updt", "rw_av", "rw_avE", "rw_m1", "rw_m1E", "rw_vp", "rw_vpE", "rw_u",
        "rw_usb", "rw_x", "rw_s", "rw_y", "rw_yE", "rw_mean", "rw_ym", "rw_ysq", "rw_var", "rw_sd", "rw_kn", "rw_knb", "rw_gs", "rw_gsb",
        "rw_done", "p_in", "p_hi", "p_rdy", "pt_mm", "gate_rdy", "grp_sq", "grp_sum", "grp_mm", "grp_sd", "grp_r",
        "grp_rstd"]


ATT_UNITS = 2 * NH * TB
ATT_TICKS = 3 + ATT_UNITS + 4
R_PREP = 4
DENSE = ["R"] * 7
CHAIN = ["R", "T"] * (2 + 2 * NCH - 1)
TAIL = ["R", "T", "R", "T", "R"]
PREP = ["R", "R", "T", "T", "T", "R", "T", "T", "T", "R", "T", "T"]
MERGE = ["T", "R", "T", "R", "T"] + DENSE[2:] + CHAIN + TAIL + PREP + DENSE
_left = ATT_TICKS - MERGE.count("T")
MERGE += ["R", "T"] * _left + ["R", "G"] * 6
MERGE += ["R"] * (2 * (R_PREP + 7 + 2 + 2 * NCH - 1 + 3) - R_PREP - MERGE.count("R") - 2) + ["G", "R", "R"]


class Buffers:
    pass


class Semaphores:
    pass


def make_semaphores(make):
    s = Semaphores()
    s.in_cst, s.in_masks, s.out_dma = make("in_cst"), make("in_masks"), make("out_dma")
    s.in_x = [make(f"in_x{n}") for n in range(KD // 2)]
    s.of_layer = [make(name) for name in LAYER_SEMS]
    (s.small_in, s.raw0, s.raw1, s.hi_done, s.lo_done, s.unit_done, s.out_tile, s.sq_ready,
     s.stat_mm, s.ysq_rdy, s.ysq_sum, s.stat_post, s.norm_sd, s.norm_r, s.norm_rstd, s.rstd_used, s.h_f,
     s.h_hi_rdy, s.h_rdy, s.x_upd, s.x_pool, s.y_scaled, s.sq_pool, s.sq_dve, s.silu_done, s.act_f, s.act_hi_rdy, s.act_rdy,
     s.down_d, s.y_evac, s.dve_step, s.act_step, s.tile_evac, s.wf_rdy, s.f_mm, s.f_t, s.f_tr,
     s.f_y, s.f_ln, s.f_lf, s.c_mm, s.c_rdy, s.cb_mm,
     s.cb_rdy, s.lam_e, s.lam_sp, s.lru_xc, s.lru_mm, s.lru_gt, s.lru_a,
     s.lru_t, s.lru_s, s.lru_poly, s.lru_th, s.lru_y, s.at_s,
     s.at_sc, s.at_max, s.at_exp, s.at_p, s.at_tr, s.at_pt, s.at_pv,
     s.at_y, s.z_mixed, s.rw_tanh, s.rw_lora, s.rw_gates, s.rw_cum, s.rw_E,
     s.rw_kkr, s.rw_sqk, s.rw_ss, s.rw_nrm, s.rw_ops, s.rw_bonus, s.rw_tr,
     s.rw_tok, s.rw_bon, s.rw_A, s.rw_am, s.rw_xl, s.rw_P, s.rw_Pe, s.rw_TP, s.rw_WP,
     s.rw_updw, s.rw_updt, s.rw_av, s.rw_avE, s.rw_m1, s.rw_m1E, s.rw_vp,
     s.rw_vpE, s.rw_u, s.rw_usb, s.rw_x, s.rw_s, s.rw_y, s.rw_yE, s.rw_mean,
     s.rw_ym, s.rw_ysq, s.rw_var, s.rw_sd, s.rw_kn, s.rw_knb, s.rw_gs, s.rw_gsb,
     s.rw_done, s.p_in,
     s.p_hi, s.p_rdy, s.pt_mm, s.gate_rdy, s.grp_sq, s.grp_sum, s.grp_mm, s.grp_sd, s.grp_r,
     s.grp_rstd) = s.of_layer
    return s


def host_constants():
    c = np.zeros((P, NCST), np.float32)
    i = np.arange(P)
    c[:, CST["ident"]:CST["ident"] + P] = np.eye(P)
    c[:, CST["ones"]:CST["ones"] + P] = 1
    same = (i[:, None] // CH) == (i[None, :] // CH)
    c[:, CST["bones"]:CST["bones"] + P] = same
    strict = same & (i[:, None] < i[None, :])
    incl = same & (i[:, None] <= i[None, :])
    for n, m in enumerate((strict, incl, strict, incl)):
        c[:, CST["mask4"] + n * P:CST["mask4"] + (n + 1) * P] = m
    for l in range(6):
        b = (i >> l) & 1
        m = ((i[:, None] >> (l + 1)) == (i[None, :] >> (l + 1))) & (b[:, None] == 0) & (b[None, :] == 1)
        c[:, CST["level"] + l * P:CST["level"] + (l + 1) * P] = m
    c[:, CST["causal"]:CST["causal"] + P] = np.where(i[None, :] <= i[:, None], 0, NEG)
    w = np.arange(2 * P)
    first = (i[:, None] // CH) * CH + CH
    c[:, CST["band"]:CST["band"] + 2 * P] = np.where((w[None] >= first) & (w[None] < first + P), 0, NEG)
    c[:, CST["tri"]:CST["tri"] + P] = i[:, None] <= i[None, :]
    c[:, CST["reset"]:CST["reset"] + SEQ] = (np.arange(SEQ) % CH != 0)[None]
    c[:, CST["cols"]:CST["cols"] + 4] = np.array([EPS, GN_EPS, 1.0, 0.0], np.float32)[None]
    return c


def build(nc, x_in, p_in, units, small, consts, out):
    ctx = ExitStack()
    with ctx:
        def sb(name, shape, dt=F32):
            return ctx.enter_context(nc.sbuf_tensor(name, shape, dt))

        x = sb("x", [P, KD, SEQ])
        raw = sb("raw", [P, 2, UNIT])
        whi = sb("whi", [P, 2, UNIT], F32R)
        wlo = sb("wlo", [P, 2, UNIT], F32R)
        scr = sb("scr", [P, 4, SEQ])
        sm = sb("sm", [P, NSMALL])
        cst = sb("cst", [P, NCST_F32])
        masks = sb("masks", [P, NCST - NCST_F32], mybir.dt.bfloat16)
        sd = sb("sd", [P, 4 * TB])
        rinv = sb("rinv", [P, 4 * TB])
        wf_hi = sb("wf_hi", [P, KD * NH], F32R)
        wf_lo = sb("wf_lo", [P, KD * NH], F32R)
        tiny = sb("tiny", [P, 208])
        base = nc.sbuf_base
        sb("arena", [P, 60 * SEQ])

        def at(name, tile_offset, shape, dt=F32):
            return nc.alloc_sbuf_tensor_at(name, [P] + shape, dt, offset=base + 4 * tile_offset)
        HALF, TOP = 16 * SEQ, 38 * SEQ + 16
        h_hi, h_lo = at("h_hi", 0, [KD, SEQ], F32R), at("h_lo", 8 * SEQ, [KD, SEQ], F32R)
        y_ffn = at("y_ffn", 0, [KD, SEQ])
        act_hi = at("act_hi_t", HALF, [KF, SEQ], F32R)
        act_lo = at("act_lo_t", HALF + KF * SEQ, [KF, SEQ], F32R)
        y_mix, gate = at("y_mix", HALF, [KD, SEQ]), at("gate", HALF + 8 * SEQ, [KD, SEQ])
        ysq = [at("ysq_ffn", HALF, [KD, SEQ]), at("ysq", HALF + 16 * SEQ, [KD, SEQ])]
        p_raw = at("p_raw", 8 * SEQ, [2, SEQ])
        p_hi, p_lo = at("p_hi", 10 * SEQ, [2, SEQ], F32R), at("p_lo", 12 * SEQ, [2, SEQ], F32R)
        o = HALF
        z = at("z", o, [8, SEQ + 1]); o += 8 * (SEQ + 1)
        lg = at("lg", o, [2, SEQ]); o += 1024
        fq = at("fq", o, [2, SEQ]); o += 1024
        fk = at("fk", o, [2, SEQ]); o += 1024
        fv = at("fv", o, [TB, GW]); o += 1024
        sq = at("sq", o, [2, SEQ]); o += 1024
        sk = at("sk", o, [SEQ]); o += 512
        sv = at("sv", o, [TB, 2 * HD]); o += 512
        lx = at("lx", o, [2, SEQ + 3]); o += 2 * (SEQ + 3)
        assert o <= TOP
        def rt(name, tile, shape=None):
            return at(name, TOP + tile * SEQ, shape or [SEQ])
        kr = rt("kr", 0, [2, SEQ])
        e1, e3, e2, bg, kg = (rt(n, 2 + i) for i, n in enumerate(("e1", "e3", "e2", "bg", "kg")))
        bon, gg = rt("bon", 8), rt("gg", 9)
        tok = rt("tok", 10, [4, TB, P])
        st = rt("st", 0, [NCH, HD])
        m1, av, us, yr, vp = rt("m1", 3), rt("av", 4, [8, HD]), rt("us", 5, [8, HD]), rt("yr", 6), rt("vp", 7, [8, HD])
        ym = rt("ym", 7)
        am = at("am", 0, [8, 4, P])
        tm, wm, xl, pm = (at(n, 4096 + 1024 * i, [8, P]) for i, n in enumerate(("tm", "wm", "xl", "pm")))
        xc, gr, gi, la, lth = (rt(n, 14 + i) for i, n in enumerate(("xc", "gr", "gi", "la", "lth")))
        cb, prob, probT = rt("cb", 14, [2, SEQ]), rt("prob", 16, [3, SEQ]), rt("probT", 19, [2, SEQ])
        gsq = rt("gsq", 14, [7, SEQ])

        psum = ctx.enter_context(nc.psum_tensor("psum", [P, 8, SEQ], F32))

        s = make_semaphores(lambda name: ctx.enter_context(nc.semaphore(name)))
        b = Buffers()
        b.s, b.x, b.raw, b.whi, b.wlo, b.scr = s, x, raw, whi, wlo, scr
        b.psum, b.sm, b.cst, b.masks, b.sd = psum, sm, cst, masks, sd
        b.rinv, b.wf_hi, b.wf_lo, b.tiny, b.h_hi, b.h_lo = rinv, wf_hi, wf_lo, tiny, h_hi, h_lo
        b.y_ffn, b.act_hi, b.act_lo, b.y_mix, b.gate, b.p_raw = y_ffn, act_hi, act_lo, y_mix, gate, p_raw
        b.p_hi, b.p_lo, b.z, b.lx, b.lg, b.fq = p_hi, p_lo, z, lx, lg, fq
        b.fk, b.fv, b.sq, b.sk, b.sv, b.kr = fk, fv, sq, sk, sv, kr
        b.e1, b.e3, b.e2, b.bg, b.kg = e1, e3, e2, bg, kg
        b.bon, b.gg, b.tok, b.st, b.m1, b.av = bon, gg, tok, st, m1, av
        b.us, b.yr, b.vp, b.ym, b.am = us, yr, vp, ym, am
        b.tm, b.wm, b.xl, b.pm, b.xc, b.gr = tm, wm, xl, pm, xc, gr
        b.gi, b.la, b.lth, b.cb, b.prob, b.probT, b.gsq, b.ysq = gi, la, lth, cb, prob, probT, gsq, ysq
        load_input(nc, x_in, consts, b)
        layer_range = range(s.of_layer[0].num, s.of_layer[-1].num + 1)
        assert [sem.num for sem in s.of_layer] == list(layer_range)
        with nc.Fori(0, DEPTH) as layer:
            run_layer(nc, layer, p_in, units, small, b)
            nc.sync.sem_clear(layer_range)
            nc.all_engine_barrier()
        store_output(nc, out, b)


def load_input(nc, x_in, consts, b):
    s, scr = b.s, b.scr
    with nc.Block() as block:
        @block.sync
        def _(sp):
            for n in range(KD // 2):
                sp.dma_start(b.x[:, 2 * n:2 * n + 2, :], x_in[:, 2 * n:2 * n + 2, :]).then_inc(s.in_x[n], 16)
                if n == 0:
                    sp.dma_start(scr[:, :, :].rearrange("p a n -> p (a n)")[:, 0:NCST - NCST_F32],
                                 consts[:, NCST_F32:NCST]).then_inc(s.in_masks, 16)
                    sp.dma_start(b.cst[:, :], consts[:, 0:NCST_F32]).then_inc(s.in_cst, 16)

        @block.vector
        def _(dve):
            dve.wait_ge(s.in_masks, 16)
            nc.vector.tensor_copy(b.masks[:, :], scr[:, :, :].rearrange("p a n -> p (a n)")[:, 0:NCST - NCST_F32])


def store_output(nc, out, b):
    s = b.s
    with nc.Block() as block:
        @block.sync
        def _(sp):
            for n in range(KD // 2):
                sp.dma_start(out[:, 2 * n:2 * n + 2, :], b.x[:, 2 * n:2 * n + 2, :]).then_inc(s.out_dma, 16)
            sp.wait_ge(s.out_dma, 16 * (KD // 2))


def run_layer(nc, layer, p_in, units, small, b):
    s, x, raw, whi, wlo, scr, psum = b.s, b.x, b.raw, b.whi, b.wlo, b.scr, b.psum
    h_hi, h_lo, y_ffn, y_mix, gate, act_hi, act_lo = b.h_hi, b.h_lo, b.y_ffn, b.y_mix, b.gate, b.act_hi, b.act_lo
    z, lx, lg, fq, fk, fv, sq, sk, sv = b.z, b.lx, b.lg, b.fq, b.fk, b.fv, b.sq, b.sk, b.sv
    sm, cst, sd, rinv, tiny = b.sm, b.cst, b.sd, b.rinv, b.tiny
    V, A, T = nc.vector, nc.scalar, nc.tensor

    def vec(name, j=0, w=1):
        return sm[:, VEC[name] + j:VEC[name] + j + w]

    def mat(name, a, w):
        return sm[:, SM[name] + a:SM[name] + a + w]

    def con(name, a=0, w=P):
        if CST[name] >= NCST_F32:
            return b.masks[:, CST[name] - NCST_F32 + a:CST[name] - NCST_F32 + a + w]
        return cst[:, CST[name] + a:CST[name] + a + w]
    ident, ones, bones = con("ident"), con("ones"), con("bones")
    eps, gn_eps, one = con("cols", 0, 1), con("cols", 1, 1), con("cols", 2, 1)
    sqx = b.ysq[1]
    YG = [lambda j: lx[:, j, 3:3 + SEQ], lambda j: fq[:, j, :], lambda j: z[:, 4 + j, 1:1 + SEQ], lambda j: fk[:, j, :]]

    SPLIT_ORDER = [0, 1, 2, 3, 6, 7, 4, 5]
    key_sum = [b.cb[:, 0, :], b.cb[:, 1, :], scr[:, 2, :], scr[:, 3, :]]
    la8n, la8p = tiny[:, 0:2], tiny[:, 2:4]
    lam_t = [tiny[:, 4 + 2 * i:6 + 2 * i] for i in range(6)]
    f_y, f_e, ctok = (tiny[:, 16 + 16 * i:32 + 16 * i] for i in range(3))
    f_pad = tiny[:, 176:204]
    f_l = f_pad[:, 12:28]
    nsink, nmax, esink = tiny[:, 80:84], tiny[:, 84:88], tiny[:, 88:92]
    kam1 = tiny[:, 92:94]
    rsum = tiny[:, 96:128]
    rinv_a = tiny[:, 128:160]
    knorm, gnorm = tiny[:, 160:168], tiny[:, 168:176]

    def ubase(stage):
        return {0: U_FFN1, 1: U_FFN2}[stage]

    def sp_program(sp):
        lu = units[bass.ds(layer, 1)].rearrange("a u p n -> (a u) p n")
        for j in range(2):
            sp.dma_start(raw[:, j, :], lu[j]).then_inc(s.raw0 if j == 0 else s.raw1, 16)
            if j == 0:
                sp.dma_start(sm[:, :], small[bass.ds(layer, 1)].rearrange("a p n -> (a p) n")).then_inc(s.small_in, 16)
        with sp.Fori(0, NUNITS // 2 - 1) as i:
            for j in range(2):
                src = units[bass.ds(layer, 1), bass.ds(2 * i + (2 + j), 1)].rearrange("a u p n -> (a u p) n")
                sp.wait_ge(s.lo_done, 2 * i + (j + 1))
                sp.dma_start(raw[:, j, :], src).then_inc(s.raw0 if j == 0 else s.raw1, 16)

    def pool_program(pool):
        def lo(j, u):
            pool.wait_ge(s.hi_done, u + 1)
            nc.gpsimd.tensor_tensor(wlo[:, j, :], raw[:, j, :], whi[:, j, :], ALU.subtract).then_inc(s.lo_done, 1)
        def lo_units(first, end):
            if first % 2:
                lo(1, first)
                first += 1
            with pool.Fori(0, (end - first) // 2) as i:
                for j in range(2):
                    lo((first + j) % 2, 2 * i + (first + j))
            if (end - first) % 2:
                lo((end - 1) % 2, end - 1)

        def help_norm(n, y):
            q = PRE[n]

            def add(a, c):
                nc.gpsimd.tensor_tensor(sqx[:, a, :], sqx[:, a, :], sqx[:, c, :], ALU.add).then_inc(s.sq_pool, 1)
            for i, k in enumerate(POOL_TILES):
                if y is not None:
                    pool.wait_ge(s.y_scaled, KD * (q - 1) + k + 1)
                    nc.gpsimd.tensor_tensor(x[:, k, :], x[:, k, :], y[:, k, :], ALU.add).then_inc(s.x_pool, 1)
                if i:
                    pool.wait_ge(s.sq_ready, KD * q + 2 * i)
                    add(2 * i - 2, 2 * i - 1)
        help_norm(N_FFN1, None)
        lo_units(0, U_MIX + 1)
        help_norm(N_MIX, y_ffn)
        lo_units(U_MIX + 1, U_FFN2)
        help_norm(N_FFN2, y_mix)
        lo_units(U_FFN2, U_WP + 1)
        help_norm(N_PE, y_ffn)
        lo_units(U_WP + 1, NUNITS)

    def spread(bank, column):
        for t in range(TB):
            last = T.matmul(psum[:, bank, t * P:(t + 1) * P], column(t), ident, start=True, stop=True)
        return last

    def spread_heads(bank, values):
        for hh in range(2):
            for t in range(TB):
                last = T.matmul(psum[hh * HD:(hh + 1) * HD, bank, t * P:(t + 1) * P],
                                values[:, 2 * t + hh:2 * t + hh + 1].broadcast_to([P, HD]), ident, start=True, stop=True)
        return last

    def head_sums(bank, src):
        for t in range(TB):
            last = T.matmul(psum[:, bank, 2 * t:2 * t + 2], src[:, t * P:(t + 1) * P], bones[:, 0:P:HD],
                            start=True, stop=True)
        return last

    def pe_attention(pe):
        pe.wait_ge(s.f_t, 1)
        for t in range(TB):
            last = T.transpose(psum[:, 2, t * NH:(t + 1) * NH], b.probT[0:NH, 0, t * P:(t + 1) * P], ident[0:NH, 0:NH])
        last.then_inc(s.f_tr, 1)
        yield
        pe.wait_ge(s.f_lf, 1)
        for t in range(TB):
            last = T.matmul(psum[:, 3, 0:TB * NH], con("tri") if t == 0 else ones,
                            f_pad[:, (TB - 1 - t) * NH:(2 * TB - 1 - t) * NH], start=(t == 0), stop=(t == TB - 1))
        last.then_inc(s.c_mm, 1)
        yield
        pe.wait_ge(s.c_rdy, 1)
        for h in range(NH):
            spread(h, lambda t: ctok[:, t * NH + h:t * NH + h + 1].broadcast_to([P, P])).then_inc(s.cb_mm, 1)
        yield

        def scores(n):
            kind, h, i = n // 16, (n // 4) % 4, n % 4
            if n >= 2:
                pe.wait_ge(s.at_sc, n - 1)
            else:
                pe.wait_ge(s.cb_rdy, n + 1)
            q = slice(i * P, (i + 1) * P)
            if kind == 0:
                r = slice(HD * (h % 2), HD * (h % 2) + HD)
                w = (i + 1) * P
                T.matmul(psum[:, n % 2, 0:w], fq[r, h // 2, q], fk[r, h // 2, 0:w], start=True, stop=False)
                last = T.matmul(psum[:, n % 2, w - P:w], ident, con("causal"), start=False, stop=True)
            else:
                r = slice(HD * (h // 2), HD * (h // 2) + HD)
                k0 = max(i - 1, 0) * P
                w = (i + 1) * P - k0
                last = T.matmul(psum[:, n % 2, 0:w], sq[r, h % 2, q], sk[r, k0:k0 + w], start=True, stop=True)
            last.then_inc(s.at_s, 1)

        def key_blocks(n):
            kind, i = n // 16, n % 4
            return list(range(0, i + 1)) if kind == 0 else list(range(max(i - 1, 0), i + 1))

        def turn(n):
            pe.wait_ge(s.at_p, n + 1)
            if n >= 1:
                pe.wait_ge(s.at_pt, n)
            else:
                pe.wait_ge(s.cb_rdy, 3)
            for j, _ in enumerate(key_blocks(n)):
                last = T.transpose(psum[:, 2, j * P:(j + 1) * P], b.prob[:, n % 3, j * P:(j + 1) * P], ident)
            last.then_inc(s.at_tr, 1)

        def weigh(n):
            kind, h, i = n // 16, (n // 4) % 4, n % 4
            pair = n // 8
            pe.wait_ge(s.at_pt, n + 1)
            if n == 0:
                pe.wait_ge(s.cb_rdy, 4)
            elif n % 8 == 0:
                pe.wait_ge(s.at_y, pair)
            rows = slice(HD * (h % 2), HD * (h % 2) + HD)
            blocks = key_blocks(n)
            for j, kb in enumerate(blocks):
                v = fv[:, kb, h * HD:(h + 1) * HD] if kind == 0 else sv[:, kb, (h // 2) * HD:(h // 2) * HD + HD]
                last = T.matmul(psum[rows, 3, i * P:(i + 1) * P], v, b.probT[:, n % 2, j * P:(j + 1) * P],
                                start=(j == 0), stop=(j == len(blocks) - 1))
            last.then_inc(s.at_pv, 1)

        scores(0)
        for n in range(ATT_UNITS + 4):
            if n + 1 < ATT_UNITS:
                scores(n + 1)
            if 2 <= n < ATT_UNITS + 2:
                turn(n - 2)
            if 3 <= n < ATT_UNITS + 3:
                weigh(n - 3)
            yield

    def pe_rwkv(pe):
        for p in range(2):
            if p:
                pe.wait_ge(s.rw_sd, 1)
            pe.wait_ge(s.rw_tanh, 2)
            T.matmul(psum[:, 4, :], mat("wa2", p * P, P)[0:64], z[0:64, 0, 1:1 + SEQ], start=True, stop=True
                     ).then_inc(s.rw_lora, 1)
            T.matmul(psum[:, 5, :], mat("wa2", p * P, P)[64:128], z[64:128, 0, 1:1 + SEQ], start=True, stop=True
                     ).then_inc(s.rw_lora, 1)
            T.matmul(psum[:, 6, :], mat("g2", p * P, P), z[:, 1, 1:1 + SEQ], start=True, stop=True
                     ).then_inc(s.rw_lora, 1)
            yield
            pe.wait_ge(s.rw_sqk, p + 1)
            head_sums(7, scr[:, 0, :]).then_inc(s.rw_ss, 1)
            yield
            pe.wait_ge(s.rw_kn, p + 1)
            spread_heads(7, knorm).then_inc(s.rw_knb, 1)
            pe.wait_ge(s.rw_ops, p + 1)
            T.matmul(psum[:, 6, :], bones, scr[:, 1, :], start=True, stop=True).then_inc(s.rw_bonus, 1)
            yield
            if p == 0:
                pe.wait_ge(s.lru_gt, 2)
            for q, src in ((0, b.kr[:, 0, :]), (1, b.bg[:, :]), (3, z[:, 6 + p, 1:1 + SEQ]), (2, b.kg[:, :])):
                if q == 2:
                    pe.wait_ge(s.rw_bon, p + 1)
                for t in range(TB):
                    last = T.transpose(psum[:, 4 + q, t * P:(t + 1) * P], src[:, t * P:(t + 1) * P], ident)
                last.then_inc(s.rw_tr, 1)
            yield
            pe.wait_ge(s.rw_tok, 4 * (p + 1))
            if p == 0:
                pe.wait_ge(s.lru_gt, 4)
                pe.wait_ge(s.f_t, 1)
            for q in range(8):
                hh, t = q % 2, q // 2
                r = slice(HD * hh, HD * hh + HD)
                if q >= 4:
                    pe.wait_ge(s.rw_am, 8 * p + q - 3)
                kk_r = b.kr[r, :, t * P:(t + 1) * P]
                for g, src in enumerate((b.bg, b.kg)):
                    last = T.matmul(psum[:, 4 + q % 4, g * 2 * P:(g + 1) * 2 * P], src[r, t * P:(t + 1) * P], kk_r,
                                    start=True, stop=True)
                last.then_inc(s.rw_A, 1)
            yield
            pe.wait_ge(s.rw_am, 8 * (p + 1))
            pe.wait_ge(s.rw_xl, 6 * p + 1)
            for half in range(2):
                for q in range(4):
                    last = T.transpose(psum[:, 5 + 2 * half, q * P:(q + 1) * P], b.xl[:, 4 * half + q, :], ident)
                last.then_inc(s.rw_TP, 1)
            yield
            for l in range(1, 6):
                pe.wait_ge(s.rw_xl, 6 * p + l + 1)
                for half in range(2):
                    pe.wait_ge(s.rw_updt, 10 * p + 2 * l - 1 + half)
                    for q in range(4):
                        last = T.matmul(psum[:, 5 + 2 * half, q * P:(q + 1) * P], b.xl[:, 4 * half + q, :],
                                        b.tm[:, 4 * half + q, :], start=True, stop=True)
                    last.then_inc(s.rw_P, 1)
                for half in range(2):
                    pe.wait_ge(s.rw_Pe, 2 * (5 * p + l - 1) + half + 1)
                    pe.wait_ge(s.rw_updw, 12 * p + 2 * l - 1 + half)
                    if l < 5:
                        for q in range(4):
                            last = T.matmul(psum[:, 5 + 2 * half, q * P:(q + 1) * P], b.wm[:, 4 * half + q, :],
                                            b.pm[:, 4 * half + q, :], start=True, stop=True)
                        last.then_inc(s.rw_TP, 1)
                    for q in range(4):
                        last = T.matmul(psum[:, 4 + 2 * half, q * P:(q + 1) * P], b.pm[:, 4 * half + q, :],
                                        b.wm[:, 4 * half + q, :], start=True, stop=True)
                    last.then_inc(s.rw_WP, 1)
                yield
            pe.wait_ge(s.rw_updw, 12 * (p + 1))
            for q in range(8):
                hh, t = q % 2, q // 2
                last = T.matmul(psum[:, 4, q * HD:(q + 1) * HD], b.am[:, q, 2, :], b.tok[:, 3, t, hh * HD:(hh + 1) * HD],
                                start=True, stop=True)
            last.then_inc(s.rw_av, 1)
            for q in range(8):
                hh, t = q % 2, q // 2
                last = T.matmul(psum[hh * HD:(hh + 1) * HD, 5, t * P:(t + 1) * P],
                                b.tok[:, 0, t, hh * HD:(hh + 1) * HD], b.wm[:, q, :], start=True, stop=True)
            last.then_inc(s.rw_m1, 1)
            yield
            pe.wait_ge(s.rw_avE, p + 1)
            for q in range(8):
                last = T.matmul(psum[:, 6, q * HD:(q + 1) * HD], b.wm[:, q, :], b.av[:, q, :], start=True, stop=True)
            last.then_inc(s.rw_vp, 1)
            yield
            pe.wait_ge(s.rw_m1E, p + 1)
            pe.wait_ge(s.rw_vpE, p + 1)

            def outputs(t):
                for hh in range(2):
                    hr = slice(hh * HD, (hh + 1) * HD)
                    q = 2 * t + hh
                    for cc in (2 * t, 2 * t + 1):
                        r = slice(cc % 2 * CH, (cc % 2 + 1) * CH)
                        dst = psum[hr, 7, cc * CH:(cc + 1) * CH]
                        T.matmul(dst, b.us[:, q, :], b.am[:, q, 1, r], start=True, stop=False)
                        T.matmul(dst, b.tok[:, 3, t, hr], b.am[:, q, 3, r], start=False, stop=False)
                        last = T.matmul(dst, b.st[hr, cc, :], b.kr[hr, 1, cc * CH:(cc + 1) * CH], start=False, stop=True)
                return last
            for cc in range(NCH):
                r, t = slice(64 * (cc % 2), 64 * (cc % 2) + 64), cc // 2
                pe.wait_ge(s.rw_s, 8 * p + cc + 1)
                for hh in range(2):
                    hr = slice(hh * HD, (hh + 1) * HD)
                    last = T.matmul(psum[r, 4 + 2 * hh, 0:HD], b.m1[hr, cc * CH:(cc + 1) * CH], b.st[hr, cc, :],
                                    start=True, stop=True)
                last.then_inc(s.rw_u, 1)
                yield
                if cc < NCH - 1:
                    pe.wait_ge(s.rw_usb, 8 * p + cc + 1)
                    for hh in range(2):
                        hr = slice(hh * HD, (hh + 1) * HD)
                        T.matmul(psum[hr, 5, 0:HD], b.tok[r, 1, t, hr], b.us[r, 2 * t + hh, :], start=True, stop=False)
                        last = T.matmul(psum[hr, 5, 0:HD], b.tok[r, 2, t, hr], b.tok[r, 3, t, hr], start=False, stop=True)
                    last.then_inc(s.rw_x, 1)
                    if cc % 2:
                        outputs(cc // 2)
                    yield
            pe.wait_ge(s.rw_usb, 8 * (p + 1))
            outputs(TB - 1).then_inc(s.rw_y, 1)
            yield
            pe.wait_ge(s.rw_yE, p + 1)
            T.matmul(psum[:, 4, :], bones, b.yr[:, :], start=True, stop=True).then_inc(s.rw_mean, 1)
            yield
            pe.wait_ge(s.rw_ysq, p + 1)
            head_sums(5, scr[:, 0, :]).then_inc(s.rw_var, 1)
            pe.wait_ge(s.rw_gs, p + 1)
            spread_heads(7, gnorm).then_inc(s.rw_gsb, 1)
            yield

    def group_sum(bank, col, i):
        for t in range(TB):
            last = T.matmul(psum[:, bank, col + t:col + t + 1], b.gsq[:, i % 7, t * P:(t + 1) * P], ones[:, 0:1],
                            start=(i in (0, 6) and t == 0), stop=(i in (4, 7) and t == TB - 1), skip_group_check=True)
        if i in (4, 7):
            last.then_inc(s.grp_mm, 1)

    def last_rstd(pe):
        pe.wait_ge(s.grp_r, 2)
        spread(6, lambda t: rinv[:, 12 + t:13 + t].broadcast_to([P, P])).then_inc(s.grp_rstd, 1)

    def pe_groups(pe):
        pe.wait_ge(s.at_y, 4)
        yield
        pe.wait_ge(s.grp_sum, 1)
        for i in (0, 2, 4):
            group_sum(3, 2 * i, i)
        yield
        yield
        pe.wait_ge(s.grp_r, 1)
        for i in range(3):
            spread(i, lambda t: rinv[:, 4 * i + t:4 * i + t + 1].broadcast_to([P, P])).then_inc(s.grp_rstd, 1)
        yield
        yield
        yield
        yield

    def pe_program(pe):
        def blk(slot, n):
            return whi[:, slot, n * P:(n + 1) * P], wlo[:, slot, n * P:(n + 1) * P]

        def mm3(dst, w, a_hi, a_lo, start, stop):
            T.matmul(dst, w[0], a_hi, start=start, stop=False)
            T.matmul(dst, w[0], a_lo, start=False, stop=False)
            return T.matmul(dst, w[1], a_hi, start=False, stop=stop)

        def mm3t(dst, a_hi, a_lo, w_hi, w_lo, start, stop):
            T.matmul(dst, a_hi, w_hi, start=start, stop=False)
            T.matmul(dst, a_hi, w_lo, start=False, stop=False)
            return T.matmul(dst, a_lo, w_hi, start=False, stop=stop)

        def stat(n, bank):
            q = PRE[n]
            if n:
                pe.wait_ge(s.norm_sd, n)
            for k in (0, 2, 4):
                if k < 4:
                    pe.wait_ge(s.sq_pool, 2 * q + k // 2 + 1)
                else:
                    pe.wait_ge(s.sq_dve, 3 * (q + 1))
                for t in range(TB):
                    last = T.matmul(psum[:, bank, t:t + 1], sqx[:, k, t * P:(t + 1) * P], ones[:, 0:1],
                                    start=(k == 0 and t == 0), stop=(k == 4 and t == TB - 1), skip_group_check=True)
            last.then_inc(s.stat_mm, 1)

        def stat_post(n, bank):
            q = POST[n]
            sqs = b.ysq[0 if n in (N_FFN1P, N_FFN2P) else 1]
            pe.wait_ge(s.norm_sd, n)
            for i, k in enumerate((0, KD - 1)):
                if k == 0:
                    pe.wait_ge(s.ysq_sum, 4 * (q + 1))
                else:
                    pe.wait_ge(s.ysq_rdy, KD * q + k + 1)
                for t in range(TB):
                    last = T.matmul(psum[:, bank, t:t + 1], sqs[:, k, t * P:(t + 1) * P], ones[:, 0:1],
                                    start=(i == 0 and t == 0), stop=(i == 1 and t == TB - 1), skip_group_check=True)
            last.then_inc(s.stat_post, 1)

        def rstd(n, bank):
            pe.wait_ge(s.norm_r, n + 1)
            if n:
                pe.wait_ge(s.rstd_used, n)
            spread(bank, lambda t: rinv[:, t:t + 1].broadcast_to([P, P])).then_inc(s.norm_rstd, 1)

        def norm(n, sbank=7, rbank=6):
            stat(n, sbank)
            rstd(n, rbank)

        def project_by_tile(u, bank):
            for j in range(2):
                for k in range(KD):
                    last = mm3(psum[:, bank + j, :], blk(u % 2, 2 * k + j), h_hi[:, k, :], h_lo[:, k, :],
                               k == 0, k == KD - 1)
                if j == 0:
                    last.then_inc(s.out_tile, 1)
            return last

        def project(u, bank, between=None):
            order = SPLIT_ORDER if U_OUT <= u < U_OUT + 4 else range(KD)
            for n, k in enumerate(order):
                if n == KD // 2 and between:
                    between()
                if u in (U_MIX, U_OUT, U_WG):
                    pe.wait_ge(s.h_rdy, h_count(u, n))
                for j in range(2):
                    last = mm3(psum[:, bank + j, :], blk(u % 2, 2 * k + j), h_hi[:, k, :], h_lo[:, k, :],
                               n == 0, n == KD - 1)
            return last

        def h_count(u, k):
            return {U_FFN1: 0, U_MIX: 8, U_OUT: 16, U_FFN2: 24, U_WG: 32}[u] + k + 1

        def ffn(f):
            u0 = ubase(f)
            n_post = (N_FFN1P, N_FFN2P)[f]
            def gate_unit(tiles_wait):
                for k in range(KD):
                    if tiles_wait:
                        pe.wait_ge(s.h_rdy, h_count(u0, k))
                    for j in range(2):
                        last = mm3(psum[:, j, :], blk(u0 % 2, 2 * k + j), h_hi[:, k, :], h_lo[:, k, :],
                                   k == 0, k == KD - 1)
                last.then_inc(s.unit_done, 1)

            def up_unit():
                for k in range(KD):
                    for j in range(2):
                        last = mm3(psum[:, 2 + j, :], blk((u0 + 1) % 2, 2 * k + j), h_hi[:, k, :], h_lo[:, k, :],
                                   k == 0, k == KD - 1)
                last.then_inc(s.unit_done, 1)
            pe.wait_ge(s.lo_done, u0 + 1)
            gate_unit(True)
            pe.wait_ge(s.lo_done, u0 + 2)
            up_unit()
            with pe.Fori(0, UP_STEPS - 1) as i:
                pe.wait_ge(s.lo_done, 2 * i + (u0 + 3))
                pe.wait_ge(s.silu_done, i + (UP_STEPS * f + 2))
                gate_unit(False)
                pe.wait_ge(s.lo_done, 2 * i + (u0 + 4))
                pe.wait_ge(s.act_f, i + (UP_STEPS * f + 2))
                up_unit()
            d0 = u0 + 2 * UP_STEPS

            def down(slot, m, start):
                for ff in range(2):
                    for d in (4, 5, 6, 7, 0, 1, 2, 3):
                        if start and ff == 0 and d == 0:
                            pe.wait_ge(s.silu_done, UP_STEPS * (f + 1) + 1)
                            pe.wait_ge(s.act_f, UP_STEPS * (f + 1) + 1)
                        last = mm3(psum[:, d, :], blk(slot, ff * KD + d), act_tile(act_hi, m, ff), act_tile(act_lo, m, ff),
                                   start and ff == 0, False)
                last.then_inc(s.unit_done, 1)

            def act_tile(t, m, ff):
                if isinstance(m, int):
                    return t[:, 2 * m + ff, :]
                return t[:, bass.ds(2 * m + ff, 1), :].rearrange("p a n -> p (a n)")
            pe.wait_ge(s.lo_done, d0 + 1)
            pe.wait_ge(s.act_rdy, UP_STEPS * f + 2)
            down(d0 % 2, 0, True)
            with pe.Fori(0, 4) as i:
                for j in (1, 2):
                    pe.wait_ge(s.lo_done, 2 * i + (d0 + j + 1))
                    pe.wait_ge(s.act_rdy, 2 * i + (UP_STEPS * f + j + 2))
                    down((d0 + j) % 2, 2 * i + j, False)
            pe.wait_ge(s.lo_done, d0 + 10)
            pe.wait_ge(s.act_rdy, UP_STEPS * f + 11)
            down((d0 + 9) % 2, 9, False)
            pe.wait_ge(s.lo_done, d0 + 11)
            pe.wait_ge(s.act_rdy, UP_STEPS * (f + 1) + 1)
            slot = (d0 + 10) % 2
            for d in range(KD):
                for ff in range(2):
                    last = mm3(psum[:, d, :], blk(slot, ff * KD + d), act_hi[:, 20 + ff, :], act_lo[:, 20 + ff, :],
                               False, ff == 1)
                last.then_inc(s.down_d, 1)
                if d == KD - 1:
                    pe.wait_ge(s.down_d, KD * (f + 1))
                    pe.sem_inc(s.unit_done, 1)
            pe.wait_ge(s.y_evac, Y_BASE[n_post] + 1)
            stat_post(n_post, 0)
            pe.wait_ge(s.y_evac, Y_BASE[n_post] + 2)
            rstd(n_post, 1)

        def unit_ready(u):
            pe.wait_ge(s.lo_done, u + 1)

        pe.wait_ge(s.in_cst, 16)
        norm(N_FFN1)
        ffn(0)
        norm(N_MIX)
        rwkv = pe_rwkv(pe)
        for m, name in enumerate(MIX_UNITS):
            u = U_MIX + m
            bank = 2 * (m % 2)
            unit_ready(u)
            if m >= 2:
                pe.wait_ge(s.tile_evac, 2 * (m - 1))
            if name == "fv":
                for t in range(TB):
                    for k in range(KD):
                        c = slice(t * P, (t + 1) * P)
                        last = mm3t(psum[:, bank + t // 2, (t % 2) * GW:(t % 2 + 1) * GW], h_hi[:, k, c], h_lo[:, k, c],
                                    whi[:, u % 2, k * GW:(k + 1) * GW], wlo[:, u % 2, k * GW:(k + 1) * GW],
                                    k == 0, k == KD - 1)
            elif name == "skv":
                for k in range(KD):
                    mm3(psum[:, bank, :], blk(u % 2, 2 * k), h_hi[:, k, :], h_lo[:, k, :], k == 0, k == KD - 1)
                for t in range(TB):
                    for k in range(KD):
                        c = slice(t * P, (t + 1) * P)
                        w = blk(u % 2, 2 * k + 1)
                        last = mm3t(psum[:, bank + 1, t * P:(t + 1) * P], h_hi[:, k, c], h_lo[:, k, c], w[0], w[1],
                                    k == 0, k == KD - 1)
            else:
                last = project(u, bank)
            last.then_inc(s.unit_done, 1)
            if m == 4 or m == 5 or m == 7 or m == 8:
                next(rwkv)
            if m == 6 or m == 9:
                j = 0 if m == 6 else 1
                pe.wait_ge(s.lru_xc, j + 1)
                if j == 0:
                    pe.wait_ge(s.rw_gates, 3)
                else:
                    pe.wait_ge(s.rw_tok, 4)
                for g, w in enumerate(("bda", "bdx")):
                    T.matmul(psum[:, 4 + g, :], mat(w, j * P, P), b.xc[:, :], start=True, stop=True
                             ).then_inc(s.lru_mm, 1)
        pe.wait_ge(s.wf_rdy, 2)
        for k in range(KD):
            last = mm3(psum[0:NH, 7, :], (b.wf_hi[:, k * NH:(k + 1) * NH], b.wf_lo[:, k * NH:(k + 1) * NH]),
                       h_hi[:, k, :], h_lo[:, k, :], k == 0, k == KD - 1)
        last.then_inc(s.f_mm, 1)
        pe.wait_ge(s.tile_evac, 2 * len(MIX_UNITS))
        turns = {"R": rwkv, "T": pe_attention(pe), "G": pe_groups(pe)}
        for turn in MERGE:
            next(turns[turn])
        for j in range(2):
            pe.wait_ge(s.grp_sq, 7 + j)
            group_sum(3, 12, 6 + j)
        last_rstd(pe)
        for m in range(4):
            u = U_OUT + m
            unit_ready(u)
            if m >= 2:
                pe.wait_ge(s.y_evac, Y_BASE[N_MIXP] + 2 * (m - 1))
            (project_by_tile if m == 3 else project)(u, 2 * (m % 2)).then_inc(s.unit_done, 1)
        stat_post(N_MIXP, 7)
        rstd(N_MIXP, 6)
        norm(N_FFN2)
        ffn(1)
        unit_ready(U_WP)
        pe.wait_ge(s.p_rdy, 1)
        pe.wait_ge(s.y_evac, Y_BASE[N_FFN2P] + KD)
        for d in range(KD):
            if d >= 4:
                pe.wait_ge(s.y_evac, Y_BASE[N_PEP] + d - 3)
            for k in range(2):
                last = mm3(psum[:, 2 + d % 4, :], blk(U_WP % 2, k * KD + d), b.p_hi[:, k, :], b.p_lo[:, k, :],
                           k == 0, k == 1)
            last.then_inc(s.pt_mm, 1)
        pe.wait_ge(s.pt_mm, KD)
        pe.sem_inc(s.unit_done, 1)
        norm(N_PE)
        pe.wait_ge(s.y_evac, Y_BASE[N_PEP] + KD)
        for m in range(4):
            u = U_WG + m
            unit_ready(u)
            if m >= 2:
                pe.wait_ge(s.gate_rdy, 2 * (m - 1))
            if m == 3:
                last = project_by_tile(u, 2 * (m % 2))
            else:
                last = project(u, 2 * (m % 2), between=(lambda: rstd(N_PEP, 6)) if m == 2 else None)
            last.then_inc(s.unit_done, 1)
            if m == 1:
                stat_post(N_PEP, 7)

    def act_attention(act, link):
        def exps(n):
            kind, h, i = n // 16, (n // 4) % 4, n % 4
            act.wait_ge(s.at_max, n + 1)
            w = (i + 1) * P if kind == 0 else min(i + 1, 2) * P
            c = n % 4
            if kind == 1:
                A.activation(esink[:, c:c + 1], vec("sink", h), ACT.Exp, bias=nmax[:, c:c + 1])
            A.activation(b.prob[:, n % 3, 0:w], b.prob[:, n % 3, 0:w], ACT.Exp, bias=nmax[:, c:c + 1],
                         accum_out=rsum[:, n:n + 1]).then_inc(s.at_exp, 1)

        def turned(n):
            kind, i = n // 16, n % 4
            w = (i + 1) * P if kind == 0 else min(i + 1, 2) * P
            act.wait_ge(s.at_tr, n + 1)
            if n >= 2:
                act.wait_ge(s.at_pv, n - 1)
            A.activation(b.probT[:, n % 2, 0:w], psum[:, 2, 0:w], ACT.Copy).then_inc(s.at_pt, 1)
        act.wait_ge(s.f_y, 1)
        link(A.activation(f_e, f_y, ACT.Abs))
        link(A.activation(f_e, f_e, ACT.Exp, scale=-1.0))
        A.activation(f_e, f_e, ACT.Ln, bias=one).then_inc(s.f_ln, 1)
        yield
        yield
        for h in range(NH):
            act.wait_ge(s.cb_mm, h + 1)
            A.activation(key_sum[h], psum[:, h, :], ACT.Copy, scale=-1.0).then_inc(s.cb_rdy, 1)
        yield
        for n in range(ATT_UNITS + 4):
            if 2 <= n < ATT_UNITS + 2:
                turned(n - 2)
            if n < ATT_UNITS:
                exps(n)
            yield

    def act_rwkv(act):
        for p in range(2):
            act.wait_ge(s.rw_lora, 3 * p + 1)
            A.activation(b.e3[:, :], psum[:, 4, :], ACT.Sigmoid, bias=vec("w0", p)).then_inc(s.rw_gates, 1)
            act.wait_ge(s.rw_lora, 3 * p + 2)
            A.activation(b.bg[:, :], psum[:, 5, :], ACT.Sigmoid, bias=vec("a0", p)).then_inc(s.rw_gates, 1)
            act.wait_ge(s.rw_lora, 3 * p + 3)
            if p:
                act.wait_ge(s.rw_done, 1)
            A.activation(b.gg[:, :], psum[:, 6, :], ACT.Copy).then_inc(s.rw_gates, 1)
            act.wait_ge(s.rw_kkr, p + 1)
            A.activation(scr[:, 0, :], b.kr[:, 0, :], ACT.Square).then_inc(s.rw_sqk, 1)
            yield
            act.wait_ge(s.rw_ss, p + 1)
            A.activation(knorm, psum[:, 7, 0:8], ACT.Sqrt).then_inc(s.rw_nrm, 1)
            act.wait_ge(s.rw_cum, p + 1)
            A.activation(b.e2[:, :], b.e1[:, :], ACT.Exp, scale=DECAY).then_inc(s.rw_E, 1)
            A.activation(b.e3[:, :], b.e3[:, :], ACT.Exp, scale=-DECAY).then_inc(s.rw_E, 1)
            A.activation(b.e1[:, :], b.e1[:, :], ACT.Exp, scale=-DECAY).then_inc(s.rw_E, 1)
            yield
            yield
            for n, q in enumerate((0, 1, 3, 2)):
                act.wait_ge(s.rw_tr, 4 * p + n + 1)
                A.activation(b.tok[:, q, :, :].rearrange("p t n -> p (t n)"), psum[:, 4 + q, :], ACT.Copy
                             ).then_inc(s.rw_tok, 1)
            yield
            yield
            yield
            for l in range(1, 6):
                for half in range(2):
                    act.wait_ge(s.rw_P, 2 * (5 * p + l - 1) + half + 1)
                    A.activation(b.pm[:, 4 * half:4 * half + 4, :].rearrange("p q n -> p (q n)"),
                                 psum[:, 5 + 2 * half, :], ACT.Copy).then_inc(s.rw_Pe, 1)
                yield
            act.wait_ge(s.rw_av, p + 1)
            A.activation(b.av[:, :, :].rearrange("p q n -> p (q n)"), psum[:, 4, :], ACT.Copy).then_inc(s.rw_avE, 1)
            act.wait_ge(s.rw_m1, p + 1)
            A.activation(b.m1[:, :], psum[:, 5, :], ACT.Copy).then_inc(s.rw_m1E, 1)
            yield
            act.wait_ge(s.rw_vp, p + 1)
            A.activation(b.vp[:, :, :].rearrange("p q n -> p (q n)"), psum[:, 6, :], ACT.Copy).then_inc(s.rw_vpE, 1)
            yield
            for cc in range(2 * NCH - 1):
                yield
            act.wait_ge(s.rw_y, p + 1)
            A.activation(b.yr[:, :], psum[:, 7, :], ACT.Copy).then_inc(s.rw_yE, 1)
            yield
            act.wait_ge(s.rw_ym, p + 1)
            A.activation(scr[:, 0, :], b.ym[:, :], ACT.Square).then_inc(s.rw_ysq, 1)
            yield
            act.wait_ge(s.rw_var, p + 1)
            A.activation(gnorm, psum[:, 5, 0:8], ACT.Sqrt, bias=gn_eps, scale=1.0 / HD).then_inc(s.rw_sd, 1)
            yield

    def act_groups(act):
        act.wait_ge(s.at_y, 4)
        act.wait_ge(s.lru_y, 2)
        act.wait_ge(s.rw_done, 1)
        for i, k in enumerate(SPLIT_ORDER[:7]):
            A.activation(b.gsq[:, i, :], YG[k // 2](k % 2), ACT.Square).then_inc(s.grp_sq, 1)
        yield
        yield
        act.wait_ge(s.grp_mm, 1)
        A.activation(sd[:, 0:12], psum[:, 3, 0:12], ACT.Sqrt, bias=eps, scale=1.0 / GW).then_inc(s.grp_sd, 1)
        yield
        yield
        yield
        yield
        act.wait_ge(s.rw_y, 2)
        for i, k in enumerate(SPLIT_ORDER[:6]):
            group_hi(act, i, k)
        yield

    def group_hi(act, i, k):
        act.wait_ge(s.h_f, 16 + i + 1)
        A.activation(h_hi[:, k, :], YG[k // 2](k % 2), ACT.Copy).then_inc(s.h_hi_rdy, 1)

    def act_program(act):
        steps = [0]

        def link(ins):
            steps[0] += 1
            ins.then_inc(s.act_step, 1)
            act.wait_ge(s.act_step, steps[0])

        def hi(slot, raw_count, done):
            act.wait_ge(s.raw0 if slot == 0 else s.raw1, raw_count)
            if done is not None:
                act.wait_ge(s.unit_done, done)
            A.activation(whi[:, slot, :], raw[:, slot, :], ACT.Copy).then_inc(s.hi_done, 1)

        def hi_u(u):
            if u < NUNITS:
                hi(u % 2, 16 * (u // 2 + 1), u - 1 if u >= 2 else None)

        def square(n, k, src):
            A.activation(sqx[:, k, :], src, ACT.Square).then_inc(s.sq_ready, 1)

        def square_post(n, k, src):
            A.activation(b.ysq[0 if n in (N_FFN1P, N_FFN2P) else 1][:, k, :], src, ACT.Square).then_inc(s.ysq_rdy, 1)

        def root(n, bank, width):
            if n in POST:
                act.wait_ge(s.stat_post, POST[n] + 1)
            else:
                act.wait_ge(s.stat_mm, PRE[n] + 1)
            if n:
                act.wait_ge(s.norm_r, n)
            A.activation(sd[:, 0:TB], psum[:, bank, 0:TB], ACT.Sqrt, bias=eps, scale=1.0 / width).then_inc(s.norm_sd, 1)

        def h_part(n_apply, k):
            act.wait_ge(s.h_f, n_apply + 1)
            A.activation(h_hi[:, k, :], scr[:, n_apply % 4, :], ACT.Copy).then_inc(s.h_hi_rdy, 1)

        def wait_x(upd, k):
            if k in POOL_TILES:
                act.wait_ge(s.x_pool, len(POOL_TILES) * (upd - 1) + POOL_TILES.index(k) + 1)
            else:
                act.wait_ge(s.x_upd, (KD - len(POOL_TILES)) * (upd - 1) + 1 + len([i for i in range(k) if i not in POOL_TILES]))

        def norm_of_x(n, upd, apply0):
            for k in range(KD):
                if upd:
                    wait_x(upd, k)
                elif k % 2 == 0:
                    act.wait_ge(s.in_x[k // 2], 16)
                square(n, k, x[:, k, :])
            if n == N_FFN1:
                hi_u(0)
            root(n, 7, D)
            for k in range(KD):
                h_part(apply0 + k, k)
            if n == N_FFN1:
                hi_u(1)

        def ffn(f):
            u0 = ubase(f)
            n_post = (N_FFN1P, N_FFN2P)[f]
            with act.Fori(0, UP_STEPS) as i:
                act.wait_ge(s.unit_done, 2 * i + (u0 + 1))
                act.wait_ge(s.act_f, i + (UP_STEPS * f + 1))
                A.activation(scr[:, 0:2, :], psum[:, 0:2, :], ACT.Silu).then_inc(s.silu_done, 1)
                hi(u0 % 2, 16 * i + 16 * ((u0 + 2) // 2 + 1), None)
                act.wait_ge(s.act_f, i + (UP_STEPS * f + 2))
                A.activation(act_hi[:, bass.ds(2 * i, 2), :], scr[:, 2:4, :], ACT.Copy).then_inc(s.act_hi_rdy, 1)
                act.wait_ge(s.unit_done, 2 * i + (u0 + 2))
                hi((u0 + 1) % 2, 16 * i + 16 * ((u0 + 3) // 2 + 1), None)
            d0 = u0 + 2 * UP_STEPS
            if f == 1:
                act.dma_start(b.p_raw[:, :, :], p_in[bass.ds(layer, 1)].rearrange("a p t n -> (a p) t n")
                              ).then_inc(s.p_in, 16)
            with act.Fori(0, 5) as i:
                for j in range(2):
                    act.wait_ge(s.unit_done, 2 * i + (d0 + j + 1))
                    hi((d0 + j) % 2, 16 * i + 16 * ((d0 + 2 + j) // 2 + 1), None)
            if f == 1:
                act.wait_ge(s.p_in, 16)
                A.activation(b.p_hi[:, :, :], b.p_raw[:, :, :], ACT.Copy).then_inc(s.p_hi, 1)
            for d in range(KD):
                act.wait_ge(s.down_d, KD * f + d + 1)
                square_post(n_post, d, psum[:, d, :])
                A.activation(y_ffn[:, d, :], psum[:, d, :], ACT.Copy,
                             scale=vec(("ffn1_post", "ffn2_post")[f], d)).then_inc(s.y_evac, 1)
            hi_u(d0 + DOWN + 1)
            root(n_post, 0, D)

        act.sem_inc(s.silu_done, 1)

        def lru_gates(j):
            for g, (dst, bias) in enumerate(((b.gr, "ba"), (b.gi, "bx"))):
                act.wait_ge(s.lru_mm, 2 * j + g + 1)
                if j:
                    act.wait_ge(s.lru_y, 1)
                A.activation(dst[:, :], psum[:, 4 + g, :], ACT.Sigmoid, bias=vec(bias, j)).then_inc(s.lru_gt, 1)
            act.wait_ge(s.lam_sp, 1)
            act.wait_ge(s.lru_gt, 2 * j + 2)
            A.activation(b.la[:, :], b.gr[:, :], ACT.Exp, scale=la8n[:, j:j + 1]).then_inc(s.lru_a, 1)
            A.activation(b.lth[:, :], b.gr[:, :], ACT.Tanh, scale=la8p[:, j:j + 1]).then_inc(s.lru_a, 1)
            act.wait_ge(s.lru_a, 3 * j + 2)
            A.activation(b.gr[:, :], b.la[:, :], ACT.Square).then_inc(s.lru_a, 1)

        def lru_roots(j):
            act.wait_ge(s.lru_t, j + 1)
            A.activation(b.gr[:, :], b.gr[:, :], ACT.Sqrt).then_inc(s.lru_s, 1)
            act.wait_ge(s.lru_poly, j + 1)
            A.activation(b.lth[:, :], b.lth[:, :], ACT.Tanh, scale=float(np.sqrt(2 / np.pi))).then_inc(s.lru_th, 1)
        norm_of_x(N_FFN1, 0, 0)
        act.wait_ge(s.small_in, 16)
        A.activation(b.wf_hi[:, :], mat("wf", 0, 32), ACT.Copy).then_inc(s.wf_rdy, 1)
        link(A.activation(lam_t[0], vec("lam", 0, 2), ACT.Abs))
        A.activation(lam_t[1], lam_t[0], ACT.Exp, scale=-1.0).then_inc(s.lam_e, 1)
        ffn(0)
        norm_of_x(N_MIX, 1, 8)
        rwkv = act_rwkv(act)
        for m, name in enumerate(MIX_UNITS):
            u = U_MIX + m
            if m == 7 or m == 10:
                lru_roots(0 if m == 7 else 1)
            hi_u(u + 2)
            act.wait_ge(s.unit_done, u + 1)
            bank = 2 * (m % 2)
            two = psum[:, bank:bank + 2, :]
            if name in ("wag", "k", "r", "v"):
                A.activation(z[:, 2 * m:2 * m + 2, 1:1 + SEQ], two, ACT.Copy).then_inc(s.tile_evac, 2)
            elif name == "lx":
                A.activation(lx[:, :, 3:3 + SEQ], two, ACT.Copy).then_inc(s.tile_evac, 2)
            elif name == "fq":
                A.activation(fq[:, :, :], two, ACT.Copy, scale=HD ** -0.5).then_inc(s.tile_evac, 2)
            elif name == "sq":
                A.activation(sq[:, :, :], two, ACT.Copy, scale=HD ** -0.5).then_inc(s.tile_evac, 2)
            elif name == "skv":
                A.activation(sk[:, :], psum[:, bank, :], ACT.Copy).then_inc(s.tile_evac, 1)
                A.activation(sv[:, :, :].rearrange("p t n -> p (t n)"), psum[:, bank + 1, :], ACT.Copy
                             ).then_inc(s.tile_evac, 1)
            else:
                dst = {"lg": lg, "fk": fk}.get(name)
                dst = dst[:, :, :] if dst is not None else fv[:, :, :].rearrange("p (a t) n -> p a (t n)", a=2)
                A.activation(dst, two, ACT.Copy).then_inc(s.tile_evac, 2)
            if m == 2:
                act.wait_ge(s.z_mixed, 2)
                A.activation(z[0:64, 0, 1:1 + SEQ], z[0:64, 0, 1:1 + SEQ], ACT.Tanh).then_inc(s.rw_tanh, 1)
                A.activation(z[:, 1, 1:1 + SEQ], z[:, 1, 1:1 + SEQ], ACT.Sigmoid).then_inc(s.rw_tanh, 1)
            if m == 4 or m == 5 or m == 7 or m == 8:
                next(rwkv)
            if m == 6 or m == 9:
                lru_gates(0 if m == 6 else 1)
        turns = {"R": rwkv, "T": act_attention(act, link), "G": act_groups(act)}
        for turn in MERGE:
            next(turns[turn])
        act.wait_ge(s.rw_done, 2)
        A.activation(b.gsq[:, 0, :], YG[2](1), ACT.Square).then_inc(s.grp_sq, 1)
        act.wait_ge(s.grp_mm, 2)
        A.activation(sd[:, 12:16], psum[:, 3, 12:16], ACT.Sqrt, bias=eps, scale=1.0 / GW).then_inc(s.grp_sd, 1)
        for j in range(2):
            group_hi(act, 6 + j, 4 + j)
        for m in range(4):
            u = U_OUT + m
            if m < 3:
                hi_u(u + 2)
                act.wait_ge(s.unit_done, u + 1)
            else:
                act.wait_ge(s.out_tile, 1)
            for j in range(2):
                if m == 3 and j == 1:
                    act.wait_ge(s.unit_done, u + 1)
                d = 2 * m + j
                bank = 2 * (m % 2) + j
                square_post(N_MIXP, d, psum[:, bank, :])
                A.activation(y_mix[:, d, :], psum[:, bank, :], ACT.Copy, scale=vec("mix_post", d)).then_inc(s.y_evac, 1)
        hi_u(U_OUT + 5)
        root(N_MIXP, 7, D)
        norm_of_x(N_FFN2, 2, 24)
        ffn(1)
        for d in range(KD):
            act.wait_ge(s.pt_mm, d + 1)
            A.activation(y_mix[:, d, :], psum[:, 2 + d % 4, :], ACT.Copy).then_inc(s.y_evac, 1)
            wait_x(3, d)
            square(N_PE, d, x[:, d, :])
        root(N_PE, 7, D)
        for k in range(KD):
            h_part(32 + k, k)
        hi_u(U_WP + 2)
        act.wait_ge(s.y_evac, Y_BASE[N_PEP] + KD)
        for k in range(KD):
            square_post(N_PEP, k, y_mix[:, k, :])
        for m in range(4):
            u = U_WG + m
            if m < 3:
                hi_u(u + 2)
                act.wait_ge(s.unit_done, u + 1)
            else:
                act.wait_ge(s.out_tile, 2)
            for j in range(2):
                if m == 3 and j == 1:
                    act.wait_ge(s.unit_done, u + 1)
                A.activation(gate[:, 2 * m + j, :], psum[:, 2 * (m % 2) + j, :], ACT.Sigmoid).then_inc(s.gate_rdy, 1)
            if m == 1:
                root(N_PEP, 7, D)

    def dve_attention(dve, link):
        dve.wait_ge(s.f_tr, 1)
        V.tensor_tensor(f_y, psum[:, 2, 0:16], vec("fb", 0, 16), ALU.add).then_inc(s.f_y, 1)
        dve.wait_ge(s.f_ln, 1)
        V.scalar_tensor_tensor(f_l, f_y, 0.0, f_e, ALU.min, ALU.subtract).then_inc(s.f_lf, 1)
        yield
        dve.wait_ge(s.c_mm, 1)
        V.tensor_copy(ctok, psum[:, 3, 0:16]).then_inc(s.c_rdy, 1)
        dve.wait_ge(s.c_rdy, 1)
        yield
        yield

        def top(n):
            kind, h, i = n // 16, (n // 4) % 4, n % 4
            w = (i + 1) * P if kind == 0 else min(i + 1, 2) * P
            dst = b.prob[:, n % 3, 0:w]
            dve.wait_ge(s.at_s, n + 1)
            if n >= 3:
                dve.wait_ge(s.at_tr, n - 2)
            elif n == 0:
                dve.wait_ge(s.cb_rdy, 4)
            if kind == 0:
                V.scalar_tensor_tensor(dst, psum[:, n % 2, 0:w], ctok[:, i * NH + h:i * NH + h + 1], key_sum[h][:, 0:w],
                                       ALU.add, ALU.add).then_inc(s.at_sc, 1)
            else:
                V.tensor_tensor(dst, psum[:, n % 2, 0:w], con("band", 2 * P - w, w), ALU.add).then_inc(s.at_sc, 1)
            dve.wait_ge(s.at_sc, n + 1)
            i = V.tensor_reduce(nmax[:, n % 4:n % 4 + 1], dst, AX.X, ALU.max, negate=True)
            if kind == 1:
                link(i)
                i = V.tensor_tensor(nmax[:, n % 4:n % 4 + 1], nmax[:, n % 4:n % 4 + 1], nsink[:, h:h + 1], ALU.min)
            i.then_inc(s.at_max, 1)

        def share(n):
            kind, h, i = n // 16, (n // 4) % 4, n % 4
            w = (i + 1) * P if kind == 0 else min(i + 1, 2) * P
            dve.wait_ge(s.at_exp, n + 1)
            if kind == 1:
                link(V.tensor_tensor(rsum[:, n:n + 1], rsum[:, n:n + 1], esink[:, n % 4:n % 4 + 1], ALU.add))
            link(V.reciprocal(rinv_a[:, n:n + 1], rsum[:, n:n + 1]))
            V.tensor_scalar(b.prob[:, n % 3, 0:w], b.prob[:, n % 3, 0:w], rinv_a[:, n:n + 1], None, ALU.mult
                            ).then_inc(s.at_p, 1)

        for n in range(ATT_UNITS + 4):
            if n % 8 == 3 and n > 3:
                pair = n // 8 - 1
                dve.wait_ge(s.at_pv, 8 * (pair + 1))
                V.tensor_copy((fq if pair < 2 else fk)[:, pair % 2, :], psum[:, 3, :]).then_inc(s.at_y, 1)
            if 2 <= n < ATT_UNITS + 2:
                share(n - 2)
            if n < ATT_UNITS:
                top(n)
            yield

    def dve_rwkv(dve, link):
        for p in range(2):
            k_, r_, v_ = (z[:, 2 * m + p, 1:1 + SEQ] for m in (1, 2, 3))
            V.tensor_scalar(b.kr[:, 0, :], k_, vec("kk", p), None, ALU.mult).then_inc(s.rw_kkr, 1)
            if p == 0:
                yield
            dve.wait_ge(s.rw_gates, 3 * p + 1)
            link(V.tensor_tensor_scan(b.e1[:, :], con("reset", 0, SEQ), b.e3[:, :], 0.0, ALU.mult, ALU.add))
            V.tensor_tensor(b.e3[:, :], b.e1[:, :], b.e3[:, :], ALU.subtract).then_inc(s.rw_cum, 1)
            dve.wait_ge(s.rw_gates, 3 * p + 2)
            link(V.tensor_scalar(b.kg[:, :], b.bg[:, :], vec("ka", p), kam1[:, p:p + 1], ALU.mult, ALU.add))
            link(V.tensor_tensor(b.kg[:, :], b.kg[:, :], k_, ALU.mult))
            link(V.scalar_tensor_tensor(scr[:, 1, :], r_, vec("rk", p), b.kg[:, :], ALU.mult, ALU.mult))
            yield
            dve.wait_ge(s.rw_nrm, p + 1)
            link(V.tensor_scalar(knorm, knorm, 1e-12, None, ALU.max))
            V.reciprocal(knorm, knorm).then_inc(s.rw_kn, 1)
            yield
            dve.wait_ge(s.rw_knb, p + 1)
            link(V.tensor_tensor(b.kr[:, 0, :], b.kr[:, 0, :], psum[:, 7, :], ALU.mult))
            link(V.tensor_tensor(b.bg[:, :], b.kr[:, 0, :], b.bg[:, :], ALU.mult))
            dve.wait_ge(s.rw_E, 3 * (p + 1))
            link(V.tensor_tensor(b.bg[:, :], b.bg[:, :], b.e2[:, :], ALU.mult))
            link(V.tensor_tensor(b.kg[:, :], b.kg[:, :], b.e2[:, :], ALU.mult))
            link(V.scalar_tensor_tensor(b.kr[:, 0, :], b.kr[:, 0, :], -1.0, b.e3[:, :], ALU.mult, ALU.mult))
            V.tensor_tensor(b.kr[:, 1, :], r_, b.e1[:, :], ALU.mult).then_inc(s.rw_ops, 1)
            dve.wait_ge(s.rw_bonus, p + 1)
            V.tensor_tensor(b.bon[:, :], psum[:, 6, :], v_, ALU.mult).then_inc(s.rw_bon, 1)
            yield
            yield
            if p == 0:
                dve.wait_ge(s.f_mm, 1)
            for q in range(8):
                dve.wait_ge(s.rw_A, 8 * p + q + 1)
                V.tensor_tensor(b.am[:, q, :, :].rearrange("p g n -> p (g n)"), psum[:, 4 + q % 4, :],
                                con("mask4", 0, 4 * P), ALU.mult).then_inc(s.rw_am, 1)
            dve.wait_ge(s.rw_am, 8 * (p + 1))

            def level(l):
                V.tensor_tensor(b.xl[:, :, :], b.am[:, :, 0, :],
                                con("level", l * P)[:, None, :].broadcast_to([P, 8, P]), ALU.mult).then_inc(s.rw_xl, 1)
            level(0)
            yield
            dve.wait_ge(s.rw_xl, 6 * p + 1)
            halves = [slice(4 * half, 4 * half + 4) for half in range(2)]
            ones4 = ident[:, None, :].broadcast_to([P, 4, P])
            for h4 in halves:
                V.tensor_tensor(b.wm[:, h4, :], b.xl[:, h4, :], ones4, ALU.add).then_inc(s.rw_updw, 1)
            dve.wait_ge(s.rw_TP, 10 * p + 2)
            dve.wait_ge(s.rw_updw, 12 * p + 2)
            level(1)
            for half, h4 in enumerate(halves):
                V.tensor_tensor(b.tm[:, h4, :], psum[:, 5 + 2 * half, :].rearrange("p (q n) -> p q n", q=4), ones4,
                                ALU.add).then_inc(s.rw_updt, 1)
            dve.wait_ge(s.rw_updt, 10 * p + 2)
            yield
            for l in range(1, 6):
                if l < 5:
                    dve.wait_ge(s.rw_P, 2 * (5 * p + l))
                    level(l + 1)
                for half in range(2):
                    w_, t_ = (m[:, 4 * half:4 * half + 4, :].rearrange("p q n -> p (q n)") for m in (b.wm, b.tm))
                    if l < 5:
                        dve.wait_ge(s.rw_TP, 10 * p + 2 * l + half + 1)
                        V.tensor_tensor(t_, t_, psum[:, 5 + 2 * half, :], ALU.add).then_inc(s.rw_updt, 1)
                    dve.wait_ge(s.rw_WP, 2 * (5 * p + l - 1) + half + 1)
                    V.tensor_tensor(w_, w_, psum[:, 4 + 2 * half, :], ALU.add).then_inc(s.rw_updw, 1)
                dve.wait_ge(s.rw_updw, 12 * p + 2 * (l + 1))
                dve.wait_ge(s.rw_updt, 10 * p + 2 * min(l + 1, 5))
                yield
            yield
            V.memset(b.st[:, 0, :], 0.0).then_inc(s.rw_s, 1)
            yield
            dve.wait_ge(s.rw_vpE, p + 1)
            for cc in range(NCH):
                r, t = slice(64 * (cc % 2), 64 * (cc % 2) + 64), cc // 2
                dve.wait_ge(s.rw_u, 8 * p + cc + 1)
                V.tensor_tensor(b.us[r, 2 * t:2 * t + 2, :], psum[r, 4:8:2, 0:HD], b.vp[r, 2 * t:2 * t + 2, :], ALU.add
                                ).then_inc(s.rw_usb, 1)
                yield
                if cc < NCH - 1:
                    dve.wait_ge(s.rw_x, 7 * p + cc + 1)
                    dve.wait_ge(s.rw_s, 8 * p + cc + 1)
                    link(V.tensor_tensor(b.st[:, cc + 1, :], psum[:, 5, 0:HD], b.st[:, cc, :], ALU.add))
                    last = (cc + 1) * CH - 1
                    V.tensor_scalar(b.st[:, cc + 1, :], b.st[:, cc + 1, :], b.e1[:, last:last + 1], None, ALU.mult
                                    ).then_inc(s.rw_s, 1)
                    yield
            yield
            dve.wait_ge(s.rw_mean, p + 1)
            V.scalar_tensor_tensor(b.ym[:, :], psum[:, 4, :], -1.0 / HD, b.yr[:, :], ALU.mult, ALU.add
                                   ).then_inc(s.rw_ym, 1)
            yield
            dve.wait_ge(s.rw_sd, p + 1)
            V.reciprocal(gnorm, gnorm).then_inc(s.rw_gs, 1)
            dve.wait_ge(s.rw_ym, p + 1)
            dve.wait_ge(s.rw_gsb, p + 1)
            link(V.tensor_tensor(b.ym[:, :], b.ym[:, :], psum[:, 7, :], ALU.mult))
            link(V.tensor_scalar(b.ym[:, :], b.ym[:, :], vec("ln_g", p), vec("ln_b", p), ALU.mult, ALU.add))
            dve.wait_ge(s.rw_bon, p + 1)
            link(V.tensor_tensor(b.ym[:, :], b.ym[:, :], b.bon[:, :], ALU.add))
            V.tensor_tensor(r_, b.ym[:, :], b.gg[:, :], ALU.mult).then_inc(s.rw_done, 1)
            dve.wait_ge(s.rw_done, p + 1)
            yield

    def group_lo(dve, i, k):
        dve.wait_ge(s.h_hi_rdy, 16 + i + 1)
        V.tensor_tensor(h_lo[:, k, :], YG[k // 2](k % 2), h_hi[:, k, :], ALU.subtract).then_inc(s.h_rdy, 1)

    def dve_groups(dve):
        dve.wait_ge(s.grp_sq, 6)
        V.tensor_tensor(b.gsq[:, 0:6:2, :], b.gsq[:, 0:6:2, :], b.gsq[:, 1:6:2, :], ALU.add).then_inc(s.grp_sum, 1)
        yield
        yield
        dve.wait_ge(s.grp_sd, 1)
        V.reciprocal(rinv[:, 0:12], sd[:, 0:12]).then_inc(s.grp_r, 1)
        yield
        yield
        for i, k in enumerate(SPLIT_ORDER[:6]):
            dve.wait_ge(s.grp_rstd, i // 2 + 1)
            V.scalar_tensor_tensor(YG[k // 2](k % 2), YG[k // 2](k % 2), vec("grp_gain", k), psum[:, i // 2, :],
                                   ALU.mult, ALU.mult).then_inc(s.h_f, 1)
            if i == 2:
                yield
        yield
        for i, k in enumerate(SPLIT_ORDER[:6]):
            group_lo(dve, i, k)
        yield

    def dve_program(dve):
        steps = [0]

        def link(ins):
            steps[0] += 1
            ins.then_inc(s.dve_step, 1)
            dve.wait_ge(s.dve_step, steps[0])

        def invert(n):
            dve.wait_ge(s.norm_sd, n + 1)
            if n:
                dve.wait_ge(s.norm_rstd, n)
            V.reciprocal(rinv[:, 0:TB], sd[:, 0:TB]).then_inc(s.norm_r, 1)

        def add_squares(n):
            q, sqs = POST[n], b.ysq[0 if n in (N_FFN1P, N_FFN2P) else 1]
            for i in (1, 2):
                dve.wait_ge(s.ysq_rdy, KD * q + 2 * i + 2)
                if i == 2:
                    dve.wait_ge(s.ysq_sum, 4 * q + 1)
                V.tensor_tensor(sqs[:, 0:2, :], sqs[:, 0:2, :], sqs[:, 2 * i:2 * i + 2, :], ALU.add).then_inc(s.ysq_sum, 1)
            dve.wait_ge(s.ysq_sum, 4 * q + 2)
            V.tensor_tensor(sqs[:, 0, :], sqs[:, 0, :], sqs[:, 1, :], ALU.add).then_inc(s.ysq_sum, 1)
            dve.wait_ge(s.ysq_rdy, KD * q + KD - 1)
            dve.wait_ge(s.ysq_sum, 4 * q + 3)
            V.tensor_tensor(sqs[:, 0, :], sqs[:, 0, :], sqs[:, KD - 2, :], ALU.add).then_inc(s.ysq_sum, 1)

        def apply(n, tiles, bank, apply0, gain):
            dve.wait_ge(s.norm_rstd, n + 1)
            cnt = len(tiles)
            for k in range(cnt + 1):
                if k < cnt:
                    src, g, _ = tiles[k]
                    i = V.scalar_tensor_tensor(scr[:, (apply0 + k) % 4, :], src, g, psum[:, bank, :], ALU.mult, ALU.mult)
                    i.then_inc(s.h_f, 1)
                    if k == cnt - 1:
                        dve.wait_ge(s.h_f, apply0 + cnt)
                        dve.sem_inc(s.rstd_used, 1)
                if k >= 1:
                    dst = tiles[k - 1][2]
                    dve.wait_ge(s.h_hi_rdy, apply0 + k)
                    V.tensor_tensor(h_lo[:, dst, :], scr[:, (apply0 + k - 1) % 4, :], h_hi[:, dst, :], ALU.subtract
                                    ).then_inc(s.h_rdy, 1)

        def add_x_squares(n):
            q = PRE[n]
            for i in range(3):
                dve.wait_ge(s.sq_ready, KD * q + 6 + i)
                if i:
                    dve.wait_ge(s.sq_dve, 3 * q + i)
                V.tensor_tensor(sqx[:, 4, :], sqx[:, 4, :], sqx[:, 5 + i, :], ALU.add).then_inc(s.sq_dve, 1)

        def apply_x(n, apply0, gain):
            apply(n, [(x[:, k, :], vec(gain, k), k) for k in range(KD)], 6, apply0, gain)

        def residual(n, y, bank, half, upd):
            dve.wait_ge(s.y_evac, Y_BASE[n] + KD)
            dve.wait_ge(s.norm_rstd, n + 1)
            for k in range(KD + 1):
                if k < KD:
                    V.scalar_tensor_tensor(y[:, k, :], y[:, k, :], 0.5 if half else 1.0, psum[:, bank, :],
                                           ALU.mult, ALU.mult).then_inc(s.y_scaled, 1)
                if k == KD:
                    dve.wait_ge(s.y_scaled, upd * KD)
                    dve.sem_inc(s.rstd_used, 1)
                if k >= 1 and k - 1 not in POOL_TILES:
                    dve.wait_ge(s.y_scaled, KD * (upd - 1) + k)
                    V.tensor_tensor(x[:, k - 1, :], x[:, k - 1, :], y[:, k - 1, :], ALU.add).then_inc(s.x_upd, 1)
            dve.wait_ge(s.x_upd, upd * (KD - len(POOL_TILES)))

        def ffn(f):
            with dve.Fori(0, UP_STEPS) as i:
                dve.wait_ge(s.silu_done, i + (UP_STEPS * f + 2))
                dve.wait_ge(s.unit_done, 2 * i + (ubase(f) + 2))
                dve.wait_ge(s.act_rdy, i + (UP_STEPS * f + 1))
                V.tensor_tensor(scr[:, 2:4, :], scr[:, 0:2, :], psum[:, 2:4, :], ALU.mult).then_inc(s.act_f, 1)
                dve.wait_ge(s.act_hi_rdy, i + (UP_STEPS * f + 1))
                V.tensor_tensor(act_lo[:, bass.ds(2 * i, 2), :], scr[:, 2:4, :], act_hi[:, bass.ds(2 * i, 2), :],
                                ALU.subtract).then_inc(s.act_rdy, 1)

        dve.sem_inc(s.act_f, 1)
        dve.sem_inc(s.act_rdy, 1)
        def convolve(j):
            dve.wait_ge(s.tile_evac, 10)
            link(V.tensor_scalar(b.xc[:, :], lx[:, j, 0:SEQ], vec("conv_w", j), vec("conv_b", j), ALU.mult, ALU.add))
            for t in range(1, 4):
                i = V.scalar_tensor_tensor(b.xc[:, :], lx[:, j, t:t + SEQ], vec("conv_w", 2 * t + j), b.xc[:, :],
                                           ALU.mult, ALU.add)
                if t < 3:
                    link(i)
                else:
                    i.then_inc(s.lru_xc, 1)

        def lru_product(j):
            dve.wait_ge(s.lru_a, 3 * j + 3)
            V.scalar_tensor_tensor(b.gr[:, :], b.gr[:, :], 1.0, b.lth[:, :], ALU.add, ALU.mult).then_inc(s.lru_t, 1)
            dve.wait_ge(s.lru_xc, j + 1)
            link(V.tensor_tensor(b.gi[:, :], b.gi[:, :], b.xc[:, :], ALU.mult))
            dve.wait_ge(s.lru_t, j + 1)
            link(V.tensor_tensor(b.lth[:, :], lg[:, j, :], lg[:, j, :], ALU.mult))
            link(V.tensor_scalar(b.lth[:, :], b.lth[:, :], 0.044715, 1.0, ALU.mult, ALU.add))
            V.tensor_tensor(b.lth[:, :], b.lth[:, :], lg[:, j, :], ALU.mult).then_inc(s.lru_poly, 1)

        def lru_output(j):
            dve.wait_ge(s.lru_s, j + 1)
            link(V.tensor_tensor(b.gi[:, :], b.gi[:, :], b.gr[:, :], ALU.mult))
            link(V.tensor_tensor_scan(b.xc[:, :], b.la[:, :], b.gi[:, :], 0.0, ALU.mult, ALU.add))
            dve.wait_ge(s.lru_th, j + 1)
            link(V.scalar_tensor_tensor(b.lth[:, :], b.lth[:, :], 1.0, lg[:, j, :], ALU.add, ALU.mult))
            V.scalar_tensor_tensor(lx[:, j, 3:3 + SEQ], b.xc[:, :], 0.5, b.lth[:, :], ALU.mult, ALU.mult
                                   ).then_inc(s.lru_y, 1)
            dve.wait_ge(s.lru_y, j + 1)

        add_x_squares(N_FFN1)
        invert(N_FFN1)
        dve.wait_ge(s.small_in, 16)
        apply_x(N_FFN1, 0, "ffn1_pre")
        dve.wait_ge(s.wf_rdy, 1)
        V.tensor_tensor(b.wf_lo[:, :], mat("wf", 0, 32), b.wf_hi[:, :], ALU.subtract).then_inc(s.wf_rdy, 1)
        dve.wait_ge(s.lam_e, 1)
        e, w, w2, acc = lam_t[1], lam_t[2], lam_t[3], lam_t[4]
        link(V.tensor_scalar(w, e, 2.0, None, ALU.add))
        link(V.reciprocal(w2, w))
        link(V.tensor_tensor(w, w2, e, ALU.mult))
        link(V.tensor_tensor(w2, w, w, ALU.mult))
        link(V.memset(acc, 1.0 / 19))
        for n in range(17, 0, -2):
            link(V.tensor_tensor(acc, acc, w2, ALU.mult))
            link(V.tensor_scalar(acc, acc, 1.0 / n, None, ALU.add))
        link(V.tensor_tensor(acc, acc, w, ALU.mult))
        link(V.tensor_scalar(w, vec("lam", 0, 2), -1.0, 0.0, ALU.mult, ALU.max))
        link(V.scalar_tensor_tensor(acc, acc, 2.0, w, ALU.mult, ALU.add))
        link(V.tensor_scalar(la8n, acc, -8.0, None, ALU.mult))
        V.tensor_scalar(la8p, acc, 8.0, None, ALU.mult).then_inc(s.lam_sp, 1)
        link(V.memset(f_pad[:, 0:12], 0.0))
        link(V.tensor_scalar(nsink, vec("sink", 0, 4), -1.0, None, ALU.mult))
        link(V.tensor_scalar(kam1, vec("ka", 0, 2), -1.0, 1.0, ALU.mult, ALU.add))
        ffn(0)
        add_squares(N_FFN1P)
        invert(N_FFN1P)
        residual(N_FFN1P, y_ffn, 1, True, 1)
        add_x_squares(N_MIX)
        invert(N_MIX)
        apply_x(N_MIX, 8, "mix_pre")
        dve.wait_ge(s.down_d, KD)
        link(V.memset(z[:, :, 0:1], 0.0))
        link(V.memset(lx[:, :, 0:3], 0.0))
        for m in range(4):
            dve.wait_ge(s.tile_evac, 2 * (m + 1))
            link(V.tensor_tensor(scr[:, 2:4, :], z[:, 2 * m:2 * m + 2, 0:SEQ], z[:, 2 * m:2 * m + 2, 1:1 + SEQ],
                                 ALU.subtract))
            for j in range(2):
                V.scalar_tensor_tensor(z[:, 2 * m + j, 1:1 + SEQ], scr[:, 2 + j, :], vec("mu", 2 * m + j),
                                       z[:, 2 * m + j, 1:1 + SEQ], ALU.mult, ALU.add).then_inc(s.z_mixed, 1)
            dve.wait_ge(s.z_mixed, 2 * (m + 1))
        rwkv = dve_rwkv(dve, link)
        next(rwkv)
        convolve(0)
        next(rwkv)
        next(rwkv)
        lru_product(0)
        next(rwkv)
        lru_output(0)
        next(rwkv)
        convolve(1)
        lru_product(1)
        lru_output(1)
        dve.wait_ge(s.f_mm, 1)
        V.tensor_copy(b.probT[0:NH, 0, :], psum[0:NH, 7, :]).then_inc(s.f_t, 1)
        turns = {"R": rwkv, "T": dve_attention(dve, link), "G": dve_groups(dve)}
        for turn in MERGE:
            next(turns[turn])
        dve.wait_ge(s.grp_sd, 2)
        V.reciprocal(rinv[:, 12:16], sd[:, 12:16]).then_inc(s.grp_r, 1)
        dve.wait_ge(s.grp_rstd, 4)
        for j in range(2):
            V.scalar_tensor_tensor(YG[2](j), YG[2](j), vec("grp_gain", 4 + j), psum[:, 6, :], ALU.mult, ALU.mult
                                   ).then_inc(s.h_f, 1)
        for j in range(2):
            group_lo(dve, 6 + j, 4 + j)
        add_squares(N_MIXP)
        invert(N_MIXP)
        residual(N_MIXP, y_mix, 6, False, 2)
        add_x_squares(N_FFN2)
        invert(N_FFN2)
        apply_x(N_FFN2, 24, "ffn2_pre")
        ffn(1)
        dve.wait_ge(s.p_hi, 1)
        V.tensor_tensor(b.p_lo[:, :, :], b.p_raw[:, :, :], b.p_hi[:, :, :], ALU.subtract).then_inc(s.p_rdy, 1)
        add_squares(N_FFN2P)
        invert(N_FFN2P)
        residual(N_FFN2P, y_ffn, 1, True, 3)
        add_x_squares(N_PE)
        invert(N_PE)
        apply_x(N_PE, 32, "pe_pre")
        add_squares(N_PEP)
        invert(N_PEP)
        dve.wait_ge(s.norm_rstd, N_PEP + 1)
        for k in range(KD):
            V.scalar_tensor_tensor(y_mix[:, k, :], y_mix[:, k, :], vec("pe_post", k), psum[:, 6, :], ALU.mult, ALU.mult
                                   ).then_inc(s.dve_step, 1)
        steps[0] += KD
        dve.wait_ge(s.dve_step, steps[0])
        for k in range(KD + 1):
            if k < KD:
                dve.wait_ge(s.gate_rdy, k + 1)
                V.tensor_tensor(y_mix[:, k, :], y_mix[:, k, :], gate[:, k, :], ALU.mult).then_inc(s.dve_step, 1)
            if k >= 1:
                dve.wait_ge(s.dve_step, steps[0] + k)
                V.tensor_tensor(x[:, k - 1, :], x[:, k - 1, :], y_mix[:, k - 1, :], ALU.add)

    with nc.Block() as block:
        @block.sync
        def _(sp):
            sp_program(sp)

        @block.gpsimd
        def _(pool):
            pool_program(pool)

        @block.tensor
        def _(pe):
            pe_program(pe)

        @block.scalar
        def _(act):
            act_program(act)

        @block.vector
        def _(dve):
            dve_program(dve)


def kernel(**inputs):
    import numpy as _np
    import concourse.bacc as _bacc
    from concourse import mybir as _mybir
    from concourse.bass_utils import run_bass_kernel_spmd as _run
    a = {k: _np.asarray(v) for k, v in inputs.items()}

    def cols(w, lo, n=GW):
        return w[:, lo:lo + n].reshape(KD, P, n).transpose(1, 0, 2).reshape(P, KD * n)

    def ffn_units(wg, wu, wd):
        for i in range(UP_STEPS):
            yield cols(wg, i * GW)
            yield cols(wu, i * GW)
        for m in range(DOWN):
            yield wd[2 * m * P:2 * (m + 1) * P].reshape(2, P, D).transpose(1, 0, 2).reshape(P, UNIT)

    off = {"lx": 0, "lg": 256, "fq": 512, "fk": 768, "fv": 1024, "r": 1284, "k": 1540, "v": 1796,
           "wag": 2052, "sq": 2308, "skv": 2564}
    units = _np.empty((DEPTH, NUNITS, P, UNIT), _np.float32)
    small = _np.zeros((DEPTH, P, NSMALL), _np.float32)
    for l in range(DEPTH):
        w_in = a["w_in"][l]
        todo = list(ffn_units(a["ffn1_wg"][l], a["ffn1_wu"][l], a["ffn1_wd"][l]))
        for name in MIX_UNITS:
            if name == "sq":
                w = w_in[:, 2308:2564].reshape(D, NH, HD)[:, [0, 2, 1, 3]].reshape(D, GW)
                todo.append(cols(w, 0))
            else:
                todo.append(cols(w_in, off[name]))
        todo += [cols(a["w_out"][l], m * GW) for m in range(4)]
        todo += list(ffn_units(a["ffn2_wg"][l], a["ffn2_wu"][l], a["ffn2_wd"][l]))
        todo.append(a["pe_wp"][l].reshape(2, P, D).transpose(1, 0, 2).reshape(P, UNIT))
        todo += [cols(a["pe_wg"][l], m * GW) for m in range(4)]
        for u, t in enumerate(todo):
            units[l, u] = t

        def put(name, v):
            v = _np.asarray(v).reshape(-1, P).T
            small[l, :, VEC[name]:VEC[name] + v.shape[1]] = v
        for name in ("ffn1_pre", "ffn1_post", "mix_pre", "mix_post", "grp_gain", "ffn2_pre", "ffn2_post",
                     "pe_pre", "pe_post"):
            put(name, a[name][l])
        put("conv_w", a["lru_conv_w"][l])
        put("conv_b", a["lru_conv_b"][l])
        put("ba", a["lru_ba"][l])
        put("bx", a["lru_bx"][l])
        put("lam", a["lru_lambda"][l])
        mu = a["rw_mu"][l]
        put("mu", _np.concatenate([mu[768:1024], mu[256:512], mu[0:256], mu[512:768]]))
        for name in ("w0", "a0", "kk", "ka", "rk", "ln_g", "ln_b"):
            put(name, a["rw_" + name][l])
        small[l, :, VEC["fb"]:VEC["fb"] + 16] = _np.tile(a["fox_fb"][l], 4)[None]
        small[l, :, VEC["sink"]:VEC["sink"] + 4] = a["sw_sinks"][l][None]
        for h in range(NH):
            r, c = HD * (h % 2), P * (h // 2) + HD * (h % 2)
            small[l, r:r + HD, SM["bda"] + c:SM["bda"] + c + HD] = a["lru_wa"][l, h]
            small[l, r:r + HD, SM["bdx"] + c:SM["bdx"] + c + HD] = a["lru_wx"][l, h]
        small[l, 0:64, SM["wa2"]:SM["wa2"] + GW] = a["rw_w2"][l]
        small[l, 64:128, SM["wa2"]:SM["wa2"] + GW] = a["rw_a2"][l]
        small[l, :, SM["g2"]:SM["g2"] + GW] = a["rw_g2"][l]
        small[l, :, SM["wf"]:SM["wf"] + 32] = cols(w_in, 1280, NH)

    nc = _bacc.Bacc("TRN2", target_bir_lowering=False, num_devices=1)
    def feature_major(v, tiles):
        v = v.reshape(-1, SEQ, tiles, P).transpose(0, 3, 2, 1)
        return _np.ascontiguousarray(v)

    arrays = {"x_in": feature_major(a["x"], KD)[0], "p_in": feature_major(a["p"], DPLE // P),
              "units_in": units, "small_in_t": small, "consts_in": host_constants()}
    args = [nc.dram_tensor(n, v.shape, _mybir.dt.from_np(v.dtype), kind="ExternalInput").ap()
            for n, v in arrays.items()]
    args.append(nc.dram_tensor("out_0", (P, KD, SEQ), F32, kind="ExternalOutput").ap())
    build(nc, *args)
    r = _run(nc, [arrays], core_ids=[0])
    out = r.results[0]["out_0"].reshape(P, KD, SEQ)
    return _np.ascontiguousarray(out.transpose(2, 1, 0)).reshape(1, SEQ, D)
```
